# Optimizing a Trainium2 kernel written in Bass

```python
import jax, jax.numpy as jnp
from jax import lax
import numpy as np
import jax
import jax.numpy as jnp

D_MODEL = 1024
BATCH = 1
SEQ = 512
DEPTH = 1

PLE_DIM = 256
D_MIX = D_MODEL
W_GRP = D_MIX // 4
N_HEADS_GRP = 4
HEAD_DIM = W_GRP // N_HEADS_GRP
GMLP_CHUNK = 128
RGLRU_CONV = 4
RGLRU_C = 8.0
HGRN_CHUNK = 64
POOL_WINDOWS = (2, 4, 8, 16)
D_FF = 2816
FFN_CONV = 3
EPS = 1e-6
COLS_A = 2 * W_GRP
COLS_B = 2 * W_GRP
COLS_C = 4 * W_GRP
COLS_D = W_GRP
OFF_B = COLS_A
OFF_C = OFF_B + COLS_B
OFF_D = OFF_C + COLS_C
D_PROJ = OFF_D + COLS_D


def rms_norm(x, g):
    xf = x.astype(jnp.float32)
    y = xf * lax.rsqrt(jnp.mean(xf * xf, axis=-1, keepdims=True) + EPS)
    return (y * g.astype(jnp.float32)).astype(x.dtype)

def causal_dwconv(x, w, b):
    k_width = w.shape[0]
    s = x.shape[1]
    xp = jnp.pad(x, ((0, 0), (k_width - 1, 0), (0, 0)))
    y = b
    for k in range(k_width):
        y = y + xp[:, k:k + s] * w[k]
    return y

def gmlp_mixer(ab, ln_g, ln_b, ws, bs):
    bsz, s, _ = ab.shape
    ab = jax.nn.gelu(ab)
    u, v = jnp.split(ab, 2, axis=-1)
    vf = v.astype(jnp.float32)
    mu = jnp.mean(vf, axis=-1, keepdims=True)
    var = jnp.mean(jnp.square(vf - mu), axis=-1, keepdims=True)
    vn = ((vf - mu) * lax.rsqrt(var + EPS) * ln_g.astype(jnp.float32) + ln_b.astype(jnp.float32)).astype(v.dtype)
    vn = vn.reshape(bsz, s // GMLP_CHUNK, GMLP_CHUNK, N_HEADS_GRP, HEAD_DIM)
    mask = jnp.tril(jnp.ones((GMLP_CHUNK, GMLP_CHUNK), dtype=bool))
    wm = jnp.where(mask, ws, jnp.zeros_like(ws))
    sv = jnp.einsum('hts,bnshd->bnthd', wm, vn) + bs.T[:, :, None]
    return u * sv.reshape(bsz, s, W_GRP)

def rglru_mixer(xb, gb, conv_w, conv_b, wa, ba, wx, bx, lam):
    bsz, s, _ = xb.shape
    xc = causal_dwconv(xb, conv_w, conv_b)
    xh = xc.reshape(bsz, s, N_HEADS_GRP, HEAD_DIM)
    r = jax.nn.sigmoid(jnp.einsum('bshd,hde->bshe', xh, wa).reshape(bsz, s, W_GRP) + ba)
    i = jax.nn.sigmoid(jnp.einsum('bshd,hde->bshe', xh, wx).reshape(bsz, s, W_GRP) + bx)
    log_a = -RGLRU_C * r.astype(jnp.float32) * jax.nn.softplus(-lam.astype(jnp.float32))
    a = jnp.exp(log_a)
    mult = jnp.sqrt(-jnp.expm1(2.0 * log_a))
    bterm = mult * (i * xc).astype(jnp.float32)

    def combine(c1, c2):
        a1, b1 = c1
        a2, b2 = c2
        return a1 * a2, a2 * b1 + b2

    _, h = lax.associative_scan(combine, (a, bterm), axis=1)
    return h.astype(xb.dtype) * jax.nn.gelu(gb)

def hgrn2_mixer(q, f, i, g, lb, norm_g):
    bsz, s, _ = q.shape
    n_chunks = s // HGRN_CHUNK
    qf = jax.nn.silu(q.astype(jnp.float32))
    fgate = lb + (1.0 - lb) * jax.nn.sigmoid(f.astype(jnp.float32))
    log_f = jnp.log(fgate)
    kf = 1.0 - fgate
    vf = i.astype(jnp.float32)

    def to_chunks(t):
        return t.reshape(bsz, n_chunks, HGRN_CHUNK, N_HEADS_GRP, HEAD_DIM).transpose(1, 0, 3, 2, 4)

    qc, kc, vc = to_chunks(qf), to_chunks(kf), to_chunks(vf)
    bc = jnp.cumsum(to_chunks(log_f), axis=3)
    mask = jnp.tril(jnp.ones((HGRN_CHUNK, HGRN_CHUNK), dtype=bool))[:, :, None]

    def step(state, xs):
        qq, kk, vv, bb = xs
        diff = bb[:, :, :, None, :] - bb[:, :, None, :, :]
        decay = jnp.exp(jnp.where(mask, diff, -jnp.inf))
        att = jnp.einsum('bhtd,bhsd,bhtsd->bhts', qq, kk, decay)
        o = jnp.einsum('bhts,bhsv->bhtv', att, vv) + jnp.einsum('bhtd,bhdv->bhtv', qq * jnp.exp(bb), state)
        bl = bb[:, :, -1:, :]
        new_state = jnp.exp(bl[:, :, 0, :])[..., None] * state + jnp.einsum('bhsd,bhsv->bhdv', kk * jnp.exp(bl - bb), vv)
        return new_state, o

    s0 = jnp.zeros((bsz, N_HEADS_GRP, HEAD_DIM, HEAD_DIM), jnp.float32)
    _, o = lax.scan(step, s0, (qc, kc, vc, bc))
    o = o.transpose(1, 0, 3, 2, 4).reshape(bsz, s, N_HEADS_GRP, HEAD_DIM)
    o = o * lax.rsqrt(jnp.mean(o * o, axis=-1, keepdims=True) + EPS) * norm_g.astype(jnp.float32)
    o = o.reshape(bsz, s, W_GRP) * jax.nn.silu(g.astype(jnp.float32))
    return o.astype(q.dtype)

def pool_mixer(xd, wd, scale):
    bsz, s, _ = xd.shape
    xf = xd.astype(jnp.float32)
    cs = jnp.cumsum(xf, axis=1)
    pos = jnp.arange(1, s + 1, dtype=jnp.float32)[None, :, None]
    outs = []
    for j, w in enumerate(POOL_WINDOWS):
        c = cs[..., j * HEAD_DIM:(j + 1) * HEAD_DIM]
        shifted = jnp.pad(c, ((0, 0), (w, 0), (0, 0)))[:, :s]
        mean = (c - shifted) / jnp.minimum(pos, float(w))
        outs.append(mean - xf[..., j * HEAD_DIM:(j + 1) * HEAD_DIM])
    pooled = jnp.stack(outs, axis=2)
    y = jnp.einsum('bsgd,gde->bsge', pooled, wd.astype(jnp.float32)).reshape(bsz, s, W_GRP)
    return (y * scale.astype(jnp.float32)).astype(xd.dtype)

def first_inputs(seed: int = 0) -> dict:
    key = jax.random.key(seed)
    ks = jax.random.split(key, 32)

    def nrm(k, shape, scale):
        return jax.random.normal(k, shape, jnp.float32) * scale

    u = jax.random.uniform(ks[14], (DEPTH, W_GRP), jnp.float32, 0.9, 0.999)
    a_base = u ** (1.0 / RGLRU_C)
    b_lam = jnp.log(a_base) - jnp.log1p(-a_base)
    return {
        "x": nrm(ks[0], (BATCH, SEQ, D_MODEL), 1.0),
        "p": nrm(ks[1], (DEPTH, BATCH, SEQ, PLE_DIM), 1.0),
        "norm1_g": 1.0 + nrm(ks[2], (DEPTH, D_MODEL), 0.02),
        "w_in": nrm(ks[3], (DEPTH, D_MODEL, D_PROJ), D_MODEL ** -0.5),
        "a_ln_g": 1.0 + nrm(ks[4], (DEPTH, W_GRP), 0.02),
        "a_ln_b": nrm(ks[5], (DEPTH, W_GRP), 0.02),
        "a_ws": nrm(ks[6], (DEPTH, N_HEADS_GRP, GMLP_CHUNK, GMLP_CHUNK), GMLP_CHUNK ** -0.5),
        "a_bs": 1.0 + nrm(ks[7], (DEPTH, N_HEADS_GRP, GMLP_CHUNK), 0.1),
        "b_conv_w": nrm(ks[8], (DEPTH, RGLRU_CONV, W_GRP), RGLRU_CONV ** -0.5),
        "b_conv_b": nrm(ks[9], (DEPTH, W_GRP), 0.02),
        "b_wa": nrm(ks[10], (DEPTH, N_HEADS_GRP, HEAD_DIM, HEAD_DIM), HEAD_DIM ** -0.5),
        "b_ba": nrm(ks[11], (DEPTH, W_GRP), 0.02),
        "b_wx": nrm(ks[12], (DEPTH, N_HEADS_GRP, HEAD_DIM, HEAD_DIM), HEAD_DIM ** -0.5),
        "b_bx": nrm(ks[13], (DEPTH, W_GRP), 0.02),
        "b_lam": b_lam,
        "c_lb": nrm(ks[15], (DEPTH, W_GRP), 0.5),
        "c_norm_g": 1.0 + nrm(ks[16], (DEPTH, HEAD_DIM), 0.02),
        "d_w": nrm(ks[17], (DEPTH, N_HEADS_GRP, HEAD_DIM, HEAD_DIM), HEAD_DIM ** -0.5),
        "d_scale": 1.0 + nrm(ks[18], (DEPTH, W_GRP), 0.1),
        "w_out": nrm(ks[19], (DEPTH, D_MIX, D_MODEL), D_MIX ** -0.5),
        "norm2_g": 1.0 + nrm(ks[20], (DEPTH, D_MODEL), 0.02),
        "w_up": nrm(ks[21], (DEPTH, D_MODEL, 2 * D_FF), D_MODEL ** -0.5),
        "ffn_conv_w": nrm(ks[22], (DEPTH, FFN_CONV, 2 * D_FF), FFN_CONV ** -0.5),
        "ffn_conv_b": nrm(ks[23], (DEPTH, 2 * D_FF), 0.02),
        "w_down": nrm(ks[24], (DEPTH, D_FF, D_MODEL), D_FF ** -0.5),
        "norm3_g": 1.0 + nrm(ks[25], (DEPTH, D_MODEL), 0.02),
        "w_pe": nrm(ks[26], (DEPTH, PLE_DIM, D_MODEL), PLE_DIM ** -0.5),
        "w_pg": nrm(ks[27], (DEPTH, D_MODEL, D_MODEL), D_MODEL ** -0.5),
        "final_g": 1.0 + nrm(ks[28], (D_MODEL,), 0.02),
    }

def first_block(x, p, norm1_g, w_in, a_ln_g, a_ln_b, a_ws, a_bs, b_conv_w, b_conv_b, b_wa, b_ba, b_wx, b_bx, b_lam, c_lb, c_norm_g, d_w, d_scale, w_out, norm2_g, w_up, ffn_conv_w, ffn_conv_b, w_down, norm3_g, w_pe, w_pg, final_g):
    lbs = jnp.cumsum(jax.nn.softmax(c_lb.astype(jnp.float32), axis=0), axis=0)
    lbs = lbs - lbs[0:1]
    for l in range(DEPTH):
        h = rms_norm(x, norm1_g[l])
        z = h @ w_in[l]
        y_a = gmlp_mixer(z[..., :OFF_B], a_ln_g[l], a_ln_b[l], a_ws[l], a_bs[l])
        y_b = rglru_mixer(z[..., OFF_B:OFF_B + W_GRP], z[..., OFF_B + W_GRP:OFF_C],
                          b_conv_w[l], b_conv_b[l], b_wa[l], b_ba[l], b_wx[l], b_bx[l], b_lam[l])
        zc = z[..., OFF_C:OFF_D]
        y_c = hgrn2_mixer(zc[..., :W_GRP], zc[..., W_GRP:2 * W_GRP], zc[..., 2 * W_GRP:3 * W_GRP],
                          zc[..., 3 * W_GRP:], lbs[l], c_norm_g[l])
        y_d = pool_mixer(z[..., OFF_D:], d_w[l], d_scale[l])
        mix = jnp.concatenate([y_a, y_b, y_c, y_d], axis=-1)
        x = x + mix @ w_out[l]
        hf = rms_norm(x, norm2_g[l]) @ w_up[l]
        hf = causal_dwconv(hf, ffn_conv_w[l], ffn_conv_b[l])
        gt, val = jnp.split(hf, 2, axis=-1)
        x = x + (jax.nn.gelu(gt) * val) @ w_down[l]
        gate = jax.nn.sigmoid(rms_norm(x, norm3_g[l]) @ w_pg[l])
        x = x + (p[l] @ w_pe[l]) * gate
    return rms_norm(x, final_g)


DEPTH_2 = 2

HEAD_DIM_2 = 64
BLOCK = 128
A_HEADS = 8
A_KV_HEADS = 2
WINDOW = 128
B_HEADS = 8
FOX_BIAS_INIT = 3.0
C_HEADS = 8
IDX_HEADS = 4
IDX_DIM = 64
DSA_TOPK_MAX = 256
D_HEADS = 8
MLA_Q_RANK = 256
MLA_KV_RANK = 128
MLA_NOPE = 64
MLA_ROPE = 32
MLA_V = 64
ROPE_THETA = 10000.0
N_EXPERTS = 16
N_GROUPS = 4
EXPERTS_PER_GROUP = N_EXPERTS // N_GROUPS
TOPK_GROUPS = 1
TOPK_EXPERTS = 2
D_FF_EXPERT = 512
LN_EPS = 1e-5
RMS_EPS = 1e-6
ALPHA = (2 * DEPTH_2) ** 0.25
BETA = (8 * DEPTH_2) ** -0.25
N_EVEN = (DEPTH_2 + 1) // 2
N_ODD = DEPTH_2 // 2
MIX_WIDTH = A_HEADS * HEAD_DIM_2 + B_HEADS * HEAD_DIM_2
EVEN_SIZES = (A_HEADS * HEAD_DIM_2, A_KV_HEADS * HEAD_DIM_2, A_KV_HEADS * HEAD_DIM_2,
              B_HEADS * HEAD_DIM_2, B_HEADS * HEAD_DIM_2, B_HEADS * HEAD_DIM_2, B_HEADS)
EVEN_VALUE_SLOTS = (2, 5)
ODD_SIZES = (C_HEADS * HEAD_DIM_2, HEAD_DIM_2, HEAD_DIM_2, IDX_HEADS * IDX_DIM, IDX_DIM, IDX_HEADS,
             MLA_Q_RANK, MLA_KV_RANK, MLA_ROPE)
ODD_VALUE_SLOTS = (2,)


def split_cols(h, sizes):
    out, start = [], 0
    for n in sizes:
        out.append(h[..., start:start + n])
        start += n
    return out

def layer_norm(x, g, b):
    xf = x.astype(jnp.float32)
    mu = jnp.mean(xf, -1, keepdims=True)
    var = jnp.mean(jnp.square(xf - mu), -1, keepdims=True)
    return ((xf - mu) * lax.rsqrt(var + LN_EPS)).astype(x.dtype) * g + b

def rms_norm_2(x, g):
    xf = x.astype(jnp.float32)
    return (xf * lax.rsqrt(jnp.mean(jnp.square(xf), -1, keepdims=True) + RMS_EPS)).astype(x.dtype) * g

def alibi_slopes(n):
    return 2.0 ** (-8.0 * jnp.arange(1, n + 1, dtype=jnp.float32) / n)

def rope(x, pos):
    half = x.shape[-1] // 2
    inv = ROPE_THETA ** (-jnp.arange(half, dtype=jnp.float32) / half)
    ang = pos.astype(jnp.float32)[:, None] * inv[None, :]
    shape = (1, x.shape[1]) + (1,) * (x.ndim - 3) + (half,)
    cos = jnp.cos(ang).reshape(shape).astype(x.dtype)
    sin = jnp.sin(ang).reshape(shape).astype(x.dtype)
    x1, x2 = x[..., :half], x[..., half:]
    return jnp.concatenate([x1 * cos - x2 * sin, x1 * sin + x2 * cos], axis=-1)

def sliding_window_sink_attention(q, k, v, sinks):
    B, S, Hq, d = q.shape
    Hkv = k.shape[2]
    G = Hq // Hkv
    nb = S // BLOCK
    qb = q.reshape(B, nb, BLOCK, Hkv, G, d)

    def band(a):
        a = a.reshape(B, nb, BLOCK, Hkv, d)
        prev = jnp.concatenate([jnp.zeros_like(a[:, :1]), a[:, :-1]], axis=1)
        return jnp.concatenate([prev, a], axis=2)

    k_band, v_band = band(k), band(v)
    logits = jnp.einsum('bnqkgd,bnskd->bnkgqs', qb, k_band,
                        preferred_element_type=jnp.float32) * d ** -0.5
    blk = jnp.arange(nb)[:, None, None]
    t = blk * BLOCK + jnp.arange(BLOCK)[None, :, None]
    s = (blk - 1) * BLOCK + jnp.arange(2 * BLOCK)[None, None, :]
    dist = t - s
    valid = (dist >= 0) & (dist < WINDOW) & (s >= 0)
    slopes = alibi_slopes(Hq).reshape(Hkv, G)
    logits = logits - slopes[:, :, None, None] * dist[:, None, None].astype(jnp.float32)
    logits = jnp.where(valid[:, None, None], logits, -jnp.inf)
    sink = jnp.broadcast_to(sinks.astype(jnp.float32).reshape(Hkv, G, 1, 1), logits.shape[:-1] + (1,))
    p = jax.nn.softmax(jnp.concatenate([logits, sink], axis=-1), axis=-1)[..., :-1].astype(v.dtype)
    out = jnp.einsum('bnkgqs,bnskd->bnqkgd', p, v_band)
    return out.reshape(B, S, Hq * d)

def causal_block_attention(q, k, v, log_forget=None):
    B, S, H, dk = q.shape
    dv = v.shape[-1]
    nb = S // BLOCK
    scale = dk ** -0.5
    pos = jnp.arange(S)
    cum = None if log_forget is None else jnp.cumsum(log_forget, axis=1).swapaxes(1, 2)

    def one_block(i):
        q_i = lax.dynamic_slice_in_dim(q, i * BLOCK, BLOCK, axis=1)
        t = i * BLOCK + jnp.arange(BLOCK)
        logits = jnp.einsum('bqhd,bshd->bhqs', q_i, k, preferred_element_type=jnp.float32) * scale
        if cum is not None:
            c_i = lax.dynamic_slice_in_dim(cum, i * BLOCK, BLOCK, axis=2)
            logits = logits + c_i[..., :, None] - cum[:, :, None, :]
        logits = jnp.where(pos[None, :] <= t[:, None], logits, -jnp.inf)
        p = jax.nn.softmax(logits, axis=-1).astype(v.dtype)
        return jnp.einsum('bhqs,bshd->bqhd', p, v)

    out = lax.map(one_block, jnp.arange(nb))
    return out.swapaxes(0, 1).reshape(B, S, H * dv)

def dsa_attention(q, k, v, q_idx, k_idx, w_idx):
    B, S, H, d = q.shape
    nb = S // BLOCK
    top_k = min(DSA_TOPK_MAX, S // 4)
    slopes = alibi_slopes(H)
    kv = jnp.concatenate([k, v], axis=-1)
    pos = jnp.arange(S)
    w_idx = w_idx.astype(jnp.float32) * IDX_HEADS ** -0.5

    def one_block(i):
        sl = lambda a: lax.dynamic_slice_in_dim(a, i * BLOCK, BLOCK, axis=1)
        q_i, qi_i, w_i = sl(q), sl(q_idx), sl(w_idx)
        t = i * BLOCK + jnp.arange(BLOCK)
        dots = jnp.einsum('bqhe,bse->bqhs', qi_i, k_idx,
                          preferred_element_type=jnp.float32) * IDX_DIM ** -0.5
        score = jnp.einsum('bqh,bqhs->bqs', w_i, jax.nn.relu(dots))
        score = jnp.where(pos[None, None, :] <= t[None, :, None], score, -jnp.inf)
        _, idx = lax.top_k(score, top_k)
        kv_sel = jax.vmap(lambda a, j: a[j])(kv, idx)
        k_sel, v_sel = kv_sel[..., :d], kv_sel[..., d:]
        dist = (t[None, :, None] - idx).astype(jnp.float32)
        logits = jnp.einsum('bqhd,bqkd->bhqk', q_i, k_sel,
                            preferred_element_type=jnp.float32) * d ** -0.5
        logits = logits - slopes[None, :, None, None] * dist[:, None]
        logits = jnp.where(dist[:, None] >= 0, logits, -jnp.inf)
        p = jax.nn.softmax(logits, axis=-1).astype(v.dtype)
        return jnp.einsum('bhqk,bqkd->bqhd', p, v_sel)

    out = lax.map(one_block, jnp.arange(nb))
    return out.swapaxes(0, 1).reshape(B, S, H * d)

def even_mixer(x, w_in, b_f, sinks, w_o):
    B, S, _ = x.shape
    qa, ka, va, qb, kb, vb, fg = split_cols(x @ w_in, EVEN_SIZES)
    qa = qa.reshape(B, S, A_HEADS, HEAD_DIM_2)
    ka = ka.reshape(B, S, A_KV_HEADS, HEAD_DIM_2)
    va = va.reshape(B, S, A_KV_HEADS, HEAD_DIM_2)
    qb = qb.reshape(B, S, B_HEADS, HEAD_DIM_2)
    kb = kb.reshape(B, S, B_HEADS, HEAD_DIM_2)
    vb = vb.reshape(B, S, B_HEADS, HEAD_DIM_2)
    log_f = jax.nn.log_sigmoid((fg + b_f).astype(jnp.float32))
    out_a = sliding_window_sink_attention(qa, ka, va, sinks)
    out_b = causal_block_attention(qb, kb, vb, log_f)
    return jnp.concatenate([out_a, out_b], axis=-1) @ w_o

def odd_mixer(x, w_in, q_norm_g, kv_norm_g, w_uq, w_ukv, w_o):
    B, S, _ = x.shape
    qc, kc, vc, qi, ki, wi, cq, ckv, kr = split_cols(x @ w_in, ODD_SIZES)
    out_c = dsa_attention(qc.reshape(B, S, C_HEADS, HEAD_DIM_2), kc, vc,
                          qi.reshape(B, S, IDX_HEADS, IDX_DIM), ki, wi)
    pos = jnp.arange(S)
    q = (rms_norm_2(cq, q_norm_g) @ w_uq).reshape(B, S, D_HEADS, MLA_NOPE + MLA_ROPE)
    kv = (rms_norm_2(ckv, kv_norm_g) @ w_ukv).reshape(B, S, D_HEADS, MLA_NOPE + MLA_V)
    q = jnp.concatenate([q[..., :MLA_NOPE], rope(q[..., MLA_NOPE:], pos)], axis=-1)
    k_rope = jnp.broadcast_to(rope(kr, pos)[:, :, None, :], (B, S, D_HEADS, MLA_ROPE))
    k = jnp.concatenate([kv[..., :MLA_NOPE], k_rope], axis=-1)
    out_d = causal_block_attention(q, k, kv[..., MLA_NOPE:])
    return jnp.concatenate([out_c, out_d], axis=-1) @ w_o

def routed_moe(x, router_w, router_b, w_gate, w_up, w_down):
    B, S, D = x.shape
    xt = x.reshape(B * S, D)
    aff = jax.nn.sigmoid((xt @ router_w).astype(jnp.float32))
    sel = aff + router_b.astype(jnp.float32)
    grp_score = lax.top_k(sel.reshape(-1, N_GROUPS, EXPERTS_PER_GROUP), 2)[0].sum(-1)
    _, g_idx = lax.top_k(grp_score, TOPK_GROUPS)
    g_mask = jax.nn.one_hot(g_idx, N_GROUPS, dtype=jnp.float32).sum(1) > 0
    e_mask = jnp.repeat(g_mask, EXPERTS_PER_GROUP, axis=1)
    _, e_idx = lax.top_k(jnp.where(e_mask, sel, -jnp.inf), TOPK_EXPERTS)
    w = jnp.take_along_axis(aff, e_idx, axis=1)
    w = w / jnp.sum(w, axis=-1, keepdims=True)
    gates = jnp.einsum('nk,nke->ne', w, jax.nn.one_hot(e_idx, N_EXPERTS, dtype=jnp.float32)).astype(x.dtype)
    y = jnp.zeros_like(xt)
    for e in range(N_EXPERTS):
        h = jax.nn.silu(xt @ w_gate[e]) * (xt @ w_up[e])
        y = y + gates[:, e:e + 1] * (h @ w_down[e])
    return y.reshape(B, S, D)

def _col_scale(sizes, value_slots):
    return jnp.concatenate([jnp.full((n,), BETA if i in value_slots else 1.0, jnp.float32)
                            for i, n in enumerate(sizes)])

def second_inputs(seed: int = 0) -> dict:
    key = jax.random.key(seed)
    ks = jax.random.split(key, 20)
    nrm = lambda k, shape, scale: jax.random.normal(k, shape, jnp.float32) * scale
    even_in, odd_in = sum(EVEN_SIZES), sum(ODD_SIZES)
    ukv_scale = jnp.tile(jnp.concatenate([jnp.ones((MLA_NOPE,), jnp.float32),
                                          jnp.full((MLA_V,), BETA, jnp.float32)]), D_HEADS)
    return {
        'x': nrm(ks[0], (BATCH, SEQ, D_MODEL), 1.0),
        'even_w_in': nrm(ks[1], (N_EVEN, D_MODEL, even_in), D_MODEL ** -0.5) * _col_scale(EVEN_SIZES, EVEN_VALUE_SLOTS),
        'even_b_f': FOX_BIAS_INIT + nrm(ks[2], (N_EVEN, B_HEADS), 0.1),
        'even_sinks': nrm(ks[3], (N_EVEN, A_HEADS), 1.0),
        'odd_w_in': nrm(ks[4], (N_ODD, D_MODEL, odd_in), D_MODEL ** -0.5) * _col_scale(ODD_SIZES, ODD_VALUE_SLOTS),
        'odd_q_norm': 1.0 + nrm(ks[5], (N_ODD, MLA_Q_RANK), 0.02),
        'odd_kv_norm': 1.0 + nrm(ks[6], (N_ODD, MLA_KV_RANK), 0.02),
        'odd_w_uq': nrm(ks[7], (N_ODD, MLA_Q_RANK, D_HEADS * (MLA_NOPE + MLA_ROPE)), MLA_Q_RANK ** -0.5),
        'odd_w_ukv': nrm(ks[8], (N_ODD, MLA_KV_RANK, D_HEADS * (MLA_NOPE + MLA_V)), MLA_KV_RANK ** -0.5) * ukv_scale,
        'w_o': nrm(ks[9], (DEPTH_2, MIX_WIDTH, D_MODEL), MIX_WIDTH ** -0.5 * BETA),
        'ln_g': 1.0 + nrm(ks[10], (DEPTH_2, 2, D_MODEL), 0.02),
        'ln_b': nrm(ks[11], (DEPTH_2, 2, D_MODEL), 0.02),
        'router_w': nrm(ks[12], (D_MODEL, N_EXPERTS), D_MODEL ** -0.5),
        'router_b': nrm(ks[13], (N_EXPERTS,), 0.01),
        'moe_w_gate': nrm(ks[14], (DEPTH_2, N_EXPERTS, D_MODEL, D_FF_EXPERT), D_MODEL ** -0.5),
        'moe_w_up': nrm(ks[15], (DEPTH_2, N_EXPERTS, D_MODEL, D_FF_EXPERT), D_MODEL ** -0.5 * BETA),
        'moe_w_down': nrm(ks[16], (DEPTH_2, N_EXPERTS, D_FF_EXPERT, D_MODEL), D_FF_EXPERT ** -0.5 * BETA),
    }

def second_block(x, even_w_in, even_b_f, even_sinks, odd_w_in, odd_q_norm, odd_kv_norm, odd_w_uq,
              odd_w_ukv, w_o, ln_g, ln_b, router_w, router_b, moe_w_gate, moe_w_up, moe_w_down):
    for l in range(DEPTH_2):
        j = l // 2
        if l % 2 == 0:
            mix = even_mixer(x, even_w_in[j], even_b_f[j], even_sinks[j], w_o[l])
        else:
            mix = odd_mixer(x, odd_w_in[j], odd_q_norm[j], odd_kv_norm[j], odd_w_uq[j], odd_w_ukv[j], w_o[l])
        x = layer_norm(ALPHA * x + mix, ln_g[l, 0], ln_b[l, 0])
        ffn = routed_moe(x, router_w, router_b, moe_w_gate[l], moe_w_up[l], moe_w_down[l])
        x = layer_norm(ALPHA * x + ffn, ln_g[l, 1], ln_b[l, 1])
    return x


def setup_inputs(seed=0):
    out = dict(first_inputs(seed))
    for name, value in second_inputs(seed + 1).items():
        if name != "x":
            out[name + "_2"] = value
    return out


def reference(
    x, p, norm1_g, w_in, a_ln_g, a_ln_b, a_ws, a_bs, b_conv_w, b_conv_b, b_wa, b_ba, b_wx, b_bx,
    b_lam, c_lb, c_norm_g, d_w, d_scale, w_out, norm2_g, w_up, ffn_conv_w, ffn_conv_b, w_down,
    norm3_g, w_pe, w_pg, final_g, even_w_in_2, even_b_f_2, even_sinks_2, odd_w_in_2,
    odd_q_norm_2, odd_kv_norm_2, odd_w_uq_2, odd_w_ukv_2, w_o_2, ln_g_2, ln_b_2, router_w_2,
    router_b_2, moe_w_gate_2, moe_w_up_2, moe_w_down_2,
):
    x = first_block(
        x, p, norm1_g, w_in, a_ln_g, a_ln_b, a_ws, a_bs, b_conv_w, b_conv_b, b_wa, b_ba, b_wx,
        b_bx, b_lam, c_lb, c_norm_g, d_w, d_scale, w_out, norm2_g, w_up, ffn_conv_w, ffn_conv_b,
        w_down, norm3_g, w_pe, w_pg, final_g,
    )
    return second_block(
        x, even_w_in_2, even_b_f_2, even_sinks_2, odd_w_in_2, odd_q_norm_2, odd_kv_norm_2,
        odd_w_uq_2, odd_w_ukv_2, w_o_2, ln_g_2, ln_b_2, router_w_2, router_b_2, moe_w_gate_2,
        moe_w_up_2, moe_w_down_2,
    )


_drawn_inputs = setup_inputs


def setup_inputs(seed=0):
    import zlib

    import numpy as np

    out = dict(_drawn_inputs(seed))
    spreads = {}
    factors = {'a_ln_g': 6.037,
     'a_ln_b': 6.133,
     'b_ba': 8.0,
     'b_bx': 8.0,
     'c_norm_g': 4.901,
     'norm2_g': 2.77,
     'ffn_conv_b': 2.863,
     'norm3_g': 6.245,
     'even_b_f_2': 64.0,
     'even_sinks_2': 7.773,
     'odd_q_norm_2': 8.0,
     'odd_kv_norm_2': 8.0,
     'odd_w_uq_2': 3.002}
    for name, (base, spread) in spreads.items():
        noise = np.random.default_rng([zlib.crc32(name.encode()), seed]).standard_normal(out[name].shape)
        drawn = base * np.exp(spread * noise) if base else spread * noise
        out[name] = jnp.asarray(drawn.astype(out[name].dtype))
    for name, factor in factors.items():
        out[name] = (out[name] * factor).astype(out[name].dtype)
    return out
```

```python
from contextlib import ExitStack

import numpy as np

import concourse.bass as bass
import concourse.mybir as mybir

F32 = mybir.dt.float32
U32 = mybir.dt.uint32
I32 = mybir.dt.int32
ALU = mybir.AluOpType
ACT = mybir.ActivationFunctionType
AX = mybir.AxisListType

P = 128
T = 512
NT = T // P
D = 1024
KD = D // P
EPS = 1e-6
LN_EPS = 1e-5
NEG = -1e30
TAKEN = -3e38
BIG = 1e33
ALPHA = 4 ** 0.25
DFF = 2816
FT = DFF // P
E = 16
EF = 512
TOPK = 128
OVER = 2 * T // P - 1
SLOTS = E + OVER
HC = 8
NC = T // HC
RING = 6
SLOT = 4096
HD = 64
MLA = 96


def alibi_slopes(n):
    return (2.0 ** (-8.0 * np.arange(1, n + 1, dtype=np.float32) / n)).astype(np.float32)


def cols(v, width=P):
    return np.ascontiguousarray(v.reshape(-1, width).T)


def rows(v):
    return np.broadcast_to(v.reshape(1, -1), (P, v.size))


def blockdiag(w):
    out = np.zeros((P, 2, P), np.float32)
    for h in range(4):
        a = (h % 2) * HD
        out[a:a + HD, h // 2, a:a + HD] = w[h]
    return out.reshape(P, -1)


def pad_rows(a):
    out = np.zeros((P, a.shape[1]), np.float32)
    out[:a.shape[0]] = a
    return out


def packs(i):
    q = np.arange(P)
    f = np.float32
    ident = np.eye(P, dtype=f)
    causal = np.zeros((P, T), f)
    causal[:, T - P:][q[:, None] < q[None, :]] = NEG
    base = [
        ("ident", ident), ("causal", causal),
        ("before", (q[:, None] < q[None, :]).astype(f)), ("ones", np.ones((P, P), f)),
        ("expert_row", rows(np.arange(E, dtype=f) * P)),
        ("router_w", i["router_w_2"].reshape(KD, P, E).transpose(1, 0, 2).reshape(P, -1)),
        ("router_b", rows(i["router_b_2"])),
        ("over_row", rows(np.array([(E - k) * P for k in (1, 2, 3) for e in range(E)], f))),
        ("over_e", rows(np.array([e for k in (1, 2, 3) for e in range(E)], f))),
        ("over_need", rows(np.array([k * P for k in (1, 2, 3) for e in range(E)], f))),
        ("over_j", rows(np.arange(8, dtype=f))),
    ]
    half = (q[:, None] // HD == q[None, :] // HD).astype(f)
    hmask = np.where(np.arange(HC)[:, None] >= np.arange(HC)[None, :], 0.0, NEG).astype(f)
    pos = np.arange(1, 17, dtype=f)
    win = np.array([[2, 8], [4, 16]])[q // HD]
    inside = np.ones(T, f)
    inside[::HC] = 0
    one = [
        ("norm1", cols(i["norm1_g"])), ("norm2", cols(i["norm2_g"])), ("norm3", cols(i["norm3_g"])),
        ("half", half), ("halfmean", half / HD), ("hmask", rows(hmask)),
        ("chunk_of", (q[:, None] // HC == np.arange(P // HC)[None, :]).astype(f)),
        ("inside", rows(inside)),
        ("wstril", (q[:, None] <= q[None, :]).astype(f)),
        ("ws", i["a_ws"][0].transpose(2, 0, 1).reshape(P, -1)),
        ("bs", np.ascontiguousarray(i["a_bs"][0].T)),
        ("aln_g", rows(i["a_ln_g"])), ("aln_b", rows(i["a_ln_b"])),
        ("bconv_w", i["b_conv_w"][0].reshape(4, 2, P).transpose(2, 1, 0).reshape(P, -1)),
        ("bconv_b", cols(i["b_conv_b"])), ("ba", cols(i["b_ba"])), ("bx", cols(i["b_bx"])),
        ("lam", cols(i["b_lam"])), ("wa", blockdiag(i["b_wa"][0])), ("wx", blockdiag(i["b_wx"][0])),
        ("lb", cols(i["c_lb"])), ("cnorm", np.tile(i["c_norm_g"].reshape(HD, 1), (2, 1))),
        ("dw", blockdiag(i["d_w"][0])), ("dscale", cols(i["d_scale"])),
        ("count", (1 / np.minimum(pos[None, None, :], win[:, :, None].astype(f))).astype(f).reshape(P, -1)),
        ("window_share", (1 / win).astype(f)),
        ("fconv_w", i["ffn_conv_w"][0].reshape(3, 2 * FT, P).transpose(2, 1, 0).reshape(P, -1)),
        ("fconv_b", cols(i["ffn_conv_b"])),
    ]
    dist = q[:, None] + P - np.arange(2 * P)[None, :]
    slopes = alibi_slopes(8)
    window = [np.where((dist >= 0) & (dist < P), -s * dist, NEG) for s in slopes]
    pick = np.zeros((P, 8, P), f)
    for h in range(8):
        pick[h, h, :] = 1
    even = [
        ("window", np.concatenate(window, 1).astype(f)), ("pick", pick.reshape(P, -1)),
        ("fg_w", i["even_w_in_2"][0][:, 2304:].reshape(KD, P, 8).transpose(1, 0, 2).reshape(P, -1)),
        ("fg_b", pad_rows(i["even_b_f_2"].reshape(8, 1))), ("sinks", rows(i["even_sinks_2"])),
    ]
    ang = (np.arange(T, dtype=f)[None, :] * (f(10000.0) ** (-np.arange(16, dtype=f) / f(16)))[:, None]).astype(f)
    cos = np.ones((P, T), f)
    sin = np.zeros((P, T), f)
    for a in (HD, HD + 16):
        cos[a:a + 16] = np.cos(ang)
        sin[a:a + 16] = np.sin(ang)
    turn = np.zeros((P, MLA), f)
    for a in range(16):
        turn[HD + 16 + a, HD + a] = -1
        turn[HD + a, HD + 16 + a] = 1
    odd = [
        ("dist", (q[:, None] + T - P - np.arange(T)[None, :]).astype(f)),
        ("cos", cos), ("sin", sin), ("turn", turn),
        ("qnorm", cols(i["odd_q_norm_2"])), ("kvnorm", cols(i["odd_kv_norm_2"])),
    ]
    return {"base": base, "one": one, "even": even, "odd": odd}


def chunk_plan():
    plan = []
    for name, nk, ncols, step in (("w_in", 8, 2304, 512), ("w_out", 8, 1024, 512), ("w_up", 8, 2 * DFF, 512)):
        plan += [(name, 0, nk, c, min(step, ncols - c)) for c in range(0, ncols, step)]
    for half in (0, 1):
        plan += [("w_down", k, min(8, FT - k), half * 512, 512) for k in range(0, FT, 8)]
    plan += [("w_pg", 0, 8, 0, 512), ("w_pe", 0, 2, 0, 1024), ("w_pg", 0, 8, 512, 512)]
    plan += [("even_w_in_2", 0, 8, a, b - a) for a, b in ((0, 512), (512, 768), (768, 1280), (1280, 1792), (1792, 2304))]
    plan += [("w_o_even", 0, 8, c, 512) for c in (0, 512)]
    plan += ["experts0"]
    plan += [("odd_w_in_2", 0, 8, a, b - a) for a, b in ((0, 512), (512, 964), (964, 1380))]
    plan += [("odd_w_uq_2", 0, 2, 0, 768), ("odd_w_ukv_2", 0, 1, 0, 1024)]
    plan += [("w_o_odd", 0, 8, c, 512) for c in (0, 512)]
    plan += ["experts1"]
    return plan


STAGES = [
    "norm1", "project", "mixers", "hgrn", "mix_out", "norm2", "up", "down", "norm3", "gate",
    "final_norm", "even_in", "even_a", "even_b", "even_out", "route0", "experts0", "overflow0", "combine0",
    "odd_in", "index", "odd_c", "latent", "odd_d", "odd_out", "route1", "experts1", "overflow1", "combine1",
]


def build(nc, w, pk_shapes, out, stop=None):
    ctx = ExitStack()
    stages = STAGES[:STAGES.index(stop) + 1] if stop else STAGES

    with ctx:
        def sb(name, shape, dt=F32):
            return ctx.enter_context(nc.sbuf_tensor(name, shape, dt))

        def sem(name):
            return ctx.enter_context(nc.semaphore(name))

        banks = [ctx.enter_context(nc.psum_tensor(f"bank{b}", [P, 512], F32)) for b in range(8)]

        ring = sb("ring", [P, RING, SLOT])
        x = sb("x", [P, NT, D])
        xT = sb("xT", [P, KD, T])
        mixT = xT
        pack_area = {}
        width = {n: sum(s for _, s in v) for n, v in pk_shapes.items()}
        pack_area["base"] = sb("base", [P, width["base"]])
        overlay = sb("overlay", [P, max(width[n] for n in ("one", "even", "odd"))])
        for n in ("one", "even", "odd"):
            pack_area[n] = overlay[:, 0:width[n]]
        operand = {}
        for n, v in pk_shapes.items():
            at = 0
            for name, s in v:
                operand[name] = pack_area[n][:, at:at + s]
                at += s
        small = sb("small", [P, 256])
        token_id = sb("token_id", [P, NT], U32)
        place = sb("place", [P, 2, NT], U32)
        weight = sb("weight", [P, 2, NT])
        over_list = sb("over_list", [P, 8], I32)
        over_n = sb("over_n", [P, 2], I32)
        SCRATCH = 15360
        scratch = sb("scratch", [P, SCRATCH])

        class Area:

            def __init__(self, start=0):
                self.at = start

            def take(self, *shape):
                n = int(np.prod(shape))
                assert self.at + n <= SCRATCH, (self.at, shape)
                a = scratch[:, self.at:self.at + n]
                self.at += n
                if len(shape) == 1:
                    return a
                names = "abcd"[:len(shape)]
                return a.rearrange(f"p ({' '.join(names)}) -> p {' '.join(names)}",
                                   **{m: s for m, s in zip(names[1:], shape[1:])})

        ident, causal = operand["ident"], operand["causal"]
        x_dram = nc.dram_tensor("x_rows", (T, D), F32, kind="Internal").ap()
        y_dram = nc.dram_tensor("expert_rows", (SLOTS * P, D), F32, kind="Internal").ap()
        idx_dram = nc.dram_tensor("expert_tokens", ((SLOTS + 1) * P, 1), U32, kind="Internal").ap()

        met = sem("met")
        w_loaded = [sem(f"w_loaded{s}") for s in range(RING)]
        w_used = sem("w_used")
        x_loaded = sem("x_loaded")
        dve_step, act_step, pool_step = sem("dve_step"), sem("act_step"), sem("pool_step")
        pack_loaded = {n: sem(f"{n}_loaded") for n in pk_shapes}
        stored = sem("stored")

        class Flow:

            def __init__(self, name):
                self.mm, self.a, self.v, self.s = (sem(f"{name}_{m}") for m in ("mm", "act", "dve", "stats"))

        turns = [Flow("even_stage"), Flow("odd_stage")]
        flow = {s: turns[i % 2] for i, s in enumerate(STAGES)}

        chunks, first_expert_chunk, at = [], {}, 0
        for c in chunk_plan():
            if isinstance(c, str):
                first_expert_chunk[int(c[-1])] = at
                at += 3 * E
            else:
                chunks.append((at, c))
                at += 1
        by_name = {}
        for at, c in chunks:
            by_name.setdefault(c[0], []).append((at, c))
        total_chunks = first_expert_chunk[1] + 3 * E

        def slots_of(eng, l):
            n = eng.value_load(over_n[0:1, l:l + 1], min_val=0, max_val=OVER)
            return n, eng.value_load(over_n[0:1, 0:1], min_val=0, max_val=OVER) if l else 0

        def slot_view(at, c):
            nk, ncols = c[2], c[4]
            return ring[:, at % RING, 0:nk * ncols].rearrange("p (k n) -> p k n", k=nk)

        def others(bank_plan, k):
            j = k - 8
            return bank_plan[j], bank_plan[:j + 1].count(bank_plan[j])

        normed = Area().take(NT, D)
        a1 = Area()
        zA, zB, zC, zD = a1.take(NT, 512), a1.take(4, T), a1.take(8, T), a1.take(2, T)
        mixers_at, zC_at, zC_end = a1.at, 4096, 8192
        hidden = Area().take(FT, T)
        hidden_end = FT * T
        ae = Area()
        qA, kA, vA = ae.take(4, T), ae.take(T), ae.take(NT, P)
        qB, kB, vB = ae.take(4, T), ae.take(4, T), ae.take(NT, 512)
        negc, cT = ae.take(T), ae.take(NT, 8)
        ao = Area()
        qC, kC, vC, distsel = ao.take(4, T), ao.take(T), ao.take(NT, HD), ao.take(10, P)
        qI, kI, wI, cqkv = ao.take(2, T), ao.take(T), ao.take(NT, 4), ao.take(NT, 384)
        ad = Area()
        qD, kD, vD = ad.take(8, T), ad.take(8, T), ad.take(NT, 512)
        assert max(ae.at, ao.at, ad.at) <= 10240
        al = Area(10240)
        cqT, ckvT, krT = al.take(2, T), al.take(T), al.take(T)
        at_ = Area(12288)
        logits, probsT, heads_out = at_.take(2, T), at_.take(2, T), at_.take(2, 512)
        stat = small[:, 0:64]
        rowsG, rowsB = Area(8192).take(D), Area(8192 + D).take(D)
        y_rows = Area().take(2, NT, D)
        pT = Area(8192).take(2, T)
        gate_s, gate_t = Area(9216).take(2, 512), Area(10240).take(2, 512)
        conv = Area(hidden_end).take(4, T)
        alm = Area(12288)
        turned, raw = alm.take(2, T), alm.take(2, T)

        class Column:

            at = 64

            @classmethod
            def take(cls, n=1):
                a = small[:, cls.at:cls.at + n]
                cls.at += n
                assert cls.at <= 256
                return a

        sumsq, rstd, mean = Column.take(NT), Column.take(NT), Column.take(NT)
        mv = Column.take(2 * NT).rearrange("p (n t) -> p n t", t=2)
        bn = Column.take(12).rearrange("p (h t) -> p h t", t=6)
        lam_e, lam_s, lam_q, lam_p, lam_c = (Column.take(2) for _ in range(5))
        lb0, omlb = Column.take(2), Column.take(2)
        top8 = Column.take(8)
        rowmax, negmax, rowsum, sinkexp, recip = (Column.take(4) for _ in range(5))
        wide_stat = Column.take(4)

        F = flow
        PROJECT = "aaaa" + "vvaa" + "aaaa" + "vvaa" + "vv"
        EVEN_IN = "aaaa" + "vaaaa" + "vvvv" + "aaaa" + "vvvv" + "v"
        ODD_IN = "aaaa" + "v" + "aaaa" + "vv" + "v" + "aaaa" + "vvvv" + "v"
        UNITS = [(n, h) for n in range(NT) for h in range(8)]
        KIND = {"even_a": "A", "even_b": "B", "odd_c": "C", "odd_d": "D"}

        def span(kind, n):
            if kind == "A":
                return max(0, n - 1) * P, P * min(2, n + 1)
            return 0, (n + 1) * P

        def head_q(kind, n, h):
            t = slice(n * P, (n + 1) * P)
            if kind == "A":
                a = (h // 4) * HD
                return qA[a:a + HD, h % 4, t]
            if kind in "BC":
                a = (h % 2) * HD
                return (qB if kind == "B" else qC)[a:a + HD, h // 2, t]
            return qD[0:MLA, h, t]

        def head_k(kind, n, h):
            s0, w_ = span(kind, n)
            s = slice(s0, s0 + w_)
            if kind == "A":
                a = (h // 4) * HD
                return kA[a:a + HD, s]
            a = (h % 2) * HD
            if kind == "B":
                return kB[a:a + HD, h // 2, s]
            if kind == "C":
                return kC[a:a + HD, s]
            return kD[0:MLA, h, s]

        def head_v(kind, block_, h):
            if kind == "A":
                return vA[:, block_, (h // 4) * HD:(h // 4 + 1) * HD]
            if kind == "C":
                return vC[:, block_, :]
            return (vB if kind == "B" else vD)[:, block_, h * HD:(h + 1) * HD]


        scores_done, biased, shifted, probs_done = sem("scores_done"), sem("biased"), sem("shifted"), sem("probs_done")
        probsT_done, probsT_ready, out_done = sem("probsT_done"), sem("probsT_ready"), sem("out_done")
        out_ready, outT_done, outT_ready = sem("out_ready"), sem("outT_done"), sem("outT_ready")
        gathered = [sem("gathered0"), sem("gathered1")]
        xgT_done, xgT_ready = sem("xgT_done"), sem("xgT_ready")
        gate_up_done, silu_ready, h_ready = sem("gate_up_done"), sem("silu_ready"), sem("h_ready")
        hT_done, hT_ready, y_done = sem("hT_done"), sem("hT_ready"), sem("y_done")
        y_ready = sem("y_ready")
        y_stored = [sem("y_stored0"), sem("y_stored1")]
        rows_gathered = [sem(f"rows_gathered{n}") for n in range(NT)]
        idx_cleared, idx_loaded, x_stored = sem("idx_cleared"), sem("idx_loaded"), sem("x_stored")
        pT_loaded, rows_loaded, ids_loaded = sem("pT_loaded"), sem("rows_loaded"), sem("ids_loaded")
        val_scaled = sem("val_scaled")
        listed = sem("listed")
        M = {n: sem(n) for n in (
            "ws_masked", "conv_done", "gates_mm", "r_ready", "i_ready", "decay_ready", "decay_exp", "mult_in", "mult_ready",
            "spatial_mm", "vn_ready", "yA_ready", "yA_mm", "pooled", "yD_mm", "var_ready", "sd_ready",
            "lam_abs", "lam_exp", "lb_in", "lb_exp", "hg_gate", "hg_log", "hg_decays", "hg_exp", "hg_exps", "hg_kT_mm",
            "hg_kT", "hg_v_spread", "hg_state_mm", "hg_state_in", "hg_state", "hg_inter_mm", "hg_diff", "hg_decay",
            "hg_att", "hg_att_mm", "hg_used", "hg_square", "hg_mean_mm", "hg_mean", "hg_sd", "spread_used")}
        squares = Area(12288).take(NT, 384)
        odd_sq, odd_var = sem("odd_sq"), sem("odd_var")
        index_done = sem("index_done")
        flags, before_, step_k, hits = (Area(2048 + 512 * i).take(3, E) for i in range(4))
        picked_e, e_list, ranked = Area(4096).take(8, 3 * E), Area(4500).take(8), Area(4600).take(NT, E)
        ai = Area(12288)
        relu_d, score = ai.take(4, T), ai.take(2, T)
        am = Area(mixers_at)
        xc, pooled, log_decay, gate_i, decay, tanh_d = (am.take(2, T) for _ in range(6))
        sums0, sums1 = tanh_d, decay
        state = Area().take(NC, HD)
        ah = Area(zC_end)
        bb, qe, ke, decay_c = ah.take(T), ah.take(T), ah.take(T), ah.take(NC)
        keT, vT, v_spread = ah.take(NT, P), ah.take(NT, P), ah.take(2, P // HC, HD)
        pair_decay, pair_v = ah.take(1024), ah.take(1024)
        log_f, to_end = pair_decay[:, 0:T], pair_decay[:, T:2 * T]
        exp_b, exp_end = pair_v[:, 0:T], pair_v[:, T:2 * T]
        o_sq = qe
        LATENT = "v" + "av" * 8 + "a" * 8 + "v" * 4
        cum, soft = probsT[:, 0, :], logits[:, 0:2, :]
        fg_w = operand["fg_w"].rearrange("p (k h) -> p k h", k=KD)
        pick = operand["pick"].rearrange("p (h q) -> p h q", h=8)
        router_w = operand["router_w"].rearrange("p (k e) -> p k e", k=KD)
        ar = Area()
        aff, sel, chosen, first, second, tmp16, posn = (ar.take(NT, E) for _ in range(7))
        rank, trank = ar.take(NT, E), ar.take(NT, 4)
        gsum, gpick, cmp, wsum, r_place, total = ar.take(NT, 4), ar.take(NT, 4), ar.take(NT, 16), ar.take(NT), ar.take(2, NT), ar.take(E)
        idx_zero = sb("idx_zero", [P, SLOTS + 1], U32)
        y_zero = Area(SCRATCH - D).take(D)
        ea = Area()
        xg, y_sb = ea.take(2, D), ea.take(2, D)
        xgT, silu_g, hid, hidT = ea.take(KD, P), ea.take(EF), ea.take(EF), ea.take(4, P)
        idx_sb = sb("idx_sb", [P, SLOTS + 1], U32)
        idx_one = sb("idx_one", [P, 1], U32)
        over_w = ea.take(2, SLOT)
        y_cleared = sem("y_cleared")
        over = {n: sem(f"over_{n}") for n in ("idx", "in", "xT_mm", "xT", "gate_up_mm", "silu", "h", "hT_mm", "hT", "down_in",
                                              "y_mm", "y", "stored", "passed", "all_stored")}
        block = ctx.enter_context(nc.Block())

        @block.tensor
        def _(pe):
            meets = [0]

            def meet():
                meets[0] += 1
                pe.drain().then_inc(met, 1)
                pe.wait_ge(met, 4 * meets[0])
                pe.drain()

            def arrived(at):
                pe.wait_ge(w_loaded[at % RING], 16 * (at // RING + 1))

            def bank_emptied(f, plan, k):
                if k >= 8:
                    who, n = others(plan, k)
                    pe.wait_ge(f.a if who == "a" else f.v, n)

            def product(out_, pairs):
                for j, (lhsT, rhs) in enumerate(pairs):
                    mm = nc.tensor.matmul(out_, lhsT, rhs, start=(j == 0), stop=(j == len(pairs) - 1))
                return mm

            def flip(f, src, ready_v, n_tiles=KD):
                for k in range(n_tiles):
                    for n in range(NT):
                        if k == 0:
                            pe.wait_ge(f.v, ready_v + n)
                        mm = nc.tensor.transpose(banks[k][:, n * P:(n + 1) * P], src[:, n, k * P:(k + 1) * P], ident)
                    mm.then_inc(f.mm, 1)

            def norm(name):
                flip(F[name], normed, 1)

            def norm1():
                pe.wait_ge(pack_loaded["base"], 16)
                norm("norm1")

            def tokens(f, plan, k, at, c, n, c0, c1):
                w_ = slot_view(at, c)
                bank_emptied(f, plan, k)
                product(banks[k % 8][:, 0:c1 - c0],
                        [(xT[:, t, n * P:(n + 1) * P], w_[:, t, c0:c1]) for t in range(KD)]).then_inc(f.mm, 1)

            def features(f, plan, k, at, c, c0, m=P):
                w_ = slot_view(at, c)
                bank_emptied(f, plan, k)
                product(banks[k % 8][0:m, :],
                        [(w_[:, t, c0:c0 + m], xT[:, t, :]) for t in range(KD)]).then_inc(f.mm, 1)

            def project():
                f, k = F["project"], 0
                for j, (at, c) in enumerate(by_name["w_in"]):
                    arrived(at)
                    for g in range(2 if j == 4 else 4):
                        if j == 0:
                            tokens(f, PROJECT, k, at, c, g, 0, 512)
                        else:
                            features(f, PROJECT, k, at, c, g * P)
                        k += 1
                    release(f.mm, k)

            def release(done, value):
                pe.wait_ge(done, value)
                pe.sem_inc(w_used, 1)

            def mixers():
                pe.wait_ge(M["conv_done"], 2)
                for g, name in enumerate(("wa", "wx")):
                    for t in range(2):
                        nc.tensor.matmul(banks[2 * g + t][:, :], operand[name][:, t * P:(t + 1) * P], xc[:, t, :],
                                         start=True, stop=True).then_inc(M["gates_mm"], 1)
                pe.wait_ge(M["pooled"], 2)
                pe.wait_ge(M["i_ready"], 2)
                for t in range(2):
                    nc.tensor.matmul(banks[2 + t][:, :], operand["dw"][:, t * P:(t + 1) * P], pooled[:, t, :],
                                     start=True, stop=True).then_inc(M["yD_mm"], 1)
                pe.wait_ge(M["ws_masked"], 1)
                for n in range(NT):
                    pe.wait_ge(M["vn_ready"], n + 1)
                    for h in range(4):
                        mm = nc.tensor.matmul(banks[4 + n][:, h * HD:(h + 1) * HD], operand["ws"][:, h * P:(h + 1) * P],
                                              zA[:, n, 256 + h * HD:256 + (h + 1) * HD], start=True, stop=True)
                    mm.then_inc(M["spatial_mm"], 1)
                pe.wait_ge(M["r_ready"], 2)
                for t in range(2):
                    for n in range(NT):
                        pe.wait_ge(M["yA_ready"], n + 1)
                        mm = nc.tensor.transpose(banks[t][:, n * P:(n + 1) * P], zA[:, n, t * P:(t + 1) * P], ident)
                    mm.then_inc(M["yA_mm"], 1)

            def hgrn():
                for pr in range(2):
                    pe.wait_ge(M["hg_exps"], pr + 1)
                    if pr:
                        pe.wait_ge(M["hg_mean"], pr)
                    for n in range(NT):
                        mm = nc.tensor.transpose(banks[0][:, n * P:(n + 1) * P], ke[:, n * P:(n + 1) * P], ident)
                    mm.then_inc(M["hg_kT_mm"], 1)
                    for n in range(NT):
                        mm = nc.tensor.transpose(banks[1][:, n * P:(n + 1) * P], zC[:, 4 + pr, n * P:(n + 1) * P], ident)
                    mm.then_inc(M["hg_kT_mm"], 1)
                    pe.wait_ge(M["hg_kT"], 2 * pr + 1)
                    for n in range(NT):
                        pe.wait_ge(M["hg_v_spread"], 2 * (NT * pr + n + 1))
                        for half_ in range(2):
                            k = 2 * (NT * pr + n) + half_
                            if k >= 2:
                                pe.wait_ge(M["hg_state_in"], k - 1)
                            for hh in range(2):
                                mm = nc.tensor.matmul(
                                    banks[2 + half_][hh * HD:(hh + 1) * HD, :], keT[:, n, hh * HD:(hh + 1) * HD],
                                    v_spread[:, hh, half_ * 8:half_ * 8 + 8, :], start=True, stop=True)
                            mm.then_inc(M["hg_state_mm"], 1)
                        k = NT * pr + n
                        pe.wait_ge(M["hg_att"], k + 1)
                        if k >= 2:
                            pe.wait_ge(M["hg_used"], k - 1)
                        for b in range(2):
                            mm = nc.tensor.matmul(banks[4 + 2 * (k % 2) + b][:, :], operand["half"],
                                                  pair_decay[:, b * 512:(b + 1) * 512], start=True, stop=True)
                        mm.then_inc(M["hg_att_mm"], 1)
                    for c in range(NC):
                        if c % 8 == 0:
                            pe.wait_ge(M["hg_state"], 8 * pr + c // 8 + 1)
                        for hh in range(2):
                            r = slice(hh * HD, (hh + 1) * HD)
                            mm = nc.tensor.matmul(banks[1][r, c * HC:(c + 1) * HC], state[r, c, :],
                                                  qe[r, c * HC:(c + 1) * HC], start=True, stop=True)
                    mm.then_inc(M["hg_inter_mm"], 1)
                    pe.wait_ge(M["hg_square"], pr + 1)
                    nc.tensor.matmul(banks[0][:, :], operand["halfmean"], o_sq, start=True, stop=True)\
                        .then_inc(M["hg_mean_mm"], 1)

            def halves(name, chunk_name, lhs, plan):
                f = F[name]
                for half_, (at, c) in enumerate(by_name[chunk_name]):
                    arrived(at)
                    w_ = slot_view(at, c)
                    for n in range(NT):
                        k = NT * half_ + n
                        product(banks[k][:, :], [(lhs[:, t, n * P:(n + 1) * P], w_[:, t, :]) for t in range(KD)])\
                            .then_inc(f.mm, 1)
                    release(f.mm, NT * (half_ + 1))

            def mix_out():
                halves("mix_out", "w_out", mixT, "v" * 8)

            def up():
                f = F["up"]
                for j, (at, c) in enumerate(by_name["w_up"]):
                    arrived(at)
                    w_ = slot_view(at, c)
                    for g in range(4):
                        k = 4 * j + g
                        if k >= 8:
                            pe.wait_ge(f.v, k - 7)
                        product(banks[k % 8][:, :], [(w_[:, t, g * P:(g + 1) * P], xT[:, t, :]) for t in range(KD)])\
                            .then_inc(f.mm, 1)
                    release(f.mm, 4 * j + 4)

            def down():
                f = F["down"]
                for j, (at, c) in enumerate(by_name["w_down"]):
                    arrived(at)
                    w_ = slot_view(at, c)
                    half_, k0 = j // 3, c[1]
                    for n in range(NT):
                        for t in range(c[2]):
                            mm = nc.tensor.matmul(banks[4 * half_ + n][:, :], hidden[:, k0 + t, n * P:(n + 1) * P],
                                                  w_[:, t, :], start=(k0 + t == 0), stop=(k0 + t == FT - 1))
                        mm.then_inc(f.mm, 1)
                    release(f.mm, NT * (j + 1))

            def gate():
                f = F["gate"]
                (at_e, c_e), = by_name["w_pe"]
                arrived(at_e)
                pe.wait_ge(pT_loaded, 16)
                w_e = slot_view(at_e, c_e)
                for half_, (at, c) in enumerate(by_name["w_pg"]):
                    arrived(at)
                    w_g = slot_view(at, c)
                    for n in range(NT):
                        k = 2 * (NT * half_ + n)
                        bank_emptied(f, "va" * 8, k)
                        product(banks[k % 8][:, :], [(pT[:, t, n * P:(n + 1) * P],
                                                      w_e[:, t, half_ * 512:(half_ + 1) * 512]) for t in range(2)])\
                            .then_inc(f.mm, 1)
                        bank_emptied(f, "va" * 8, k + 1)
                        product(banks[(k + 1) % 8][:, :], [(xT[:, t, n * P:(n + 1) * P], w_g[:, t, :]) for t in range(KD)])\
                            .then_inc(f.mm, 1)
                    if half_ == 1:
                        release(f.mm, 16)
                    release(f.mm, 8 * (half_ + 1))

            def final_norm():
                flip(F["final_norm"], x, 1)

            def even_in():
                f, k = F["even_in"], 0
                pe.wait_ge(pack_loaded["even"], 16)
                for j, (at, c) in enumerate(by_name["even_w_in_2"]):
                    arrived(at)
                    if j == 1:
                        features(f, EVEN_IN, k, at, c, 0)
                        k += 1
                    for g in range(4):
                        if j == 1:
                            tokens(f, EVEN_IN, k, at, c, g, P, 2 * P)
                        elif j == 4:
                            tokens(f, EVEN_IN, k, at, c, g, 0, 512)
                        else:
                            features(f, EVEN_IN, k, at, c, g * P)
                        k += 1
                    release(f.mm, k)
                bank_emptied(f, EVEN_IN, k)
                product(banks[k % 8][0:8, :], [(fg_w[:, t, :], xT[:, t, :]) for t in range(KD)]).then_inc(f.mm, 1)
                pe.wait_ge(f.s, 3)
                for n in range(NT):
                    mm = nc.tensor.transpose(banks[(k + 1) % 8][:, n * 8:(n + 1) * 8], cum[0:8, n * P:(n + 1) * P],
                                             ident[0:8, 0:8])
                mm.then_inc(f.mm, 1)

            def attend(stage):
                kind = KIND[stage]
                base = 32 * list(KIND).index(stage)

                def score(i):
                    n, h = UNITS[i]
                    u = base + i
                    if u >= 2:
                        pe.wait_ge(biased, u - 1)
                    out_ = banks[u % 2][:, 0:span(kind, n)[1]]
                    if kind == "B":
                        nc.tensor.matmul(out_, head_q(kind, n, h), head_k(kind, n, h), start=True, stop=False)
                        mm = nc.tensor.matmul(out_, pick[0:8, h, :], negc[0:8, 0:span(kind, n)[1]],
                                              start=False, stop=True)
                    else:
                        mm = nc.tensor.matmul(out_, head_q(kind, n, h), head_k(kind, n, h), start=True, stop=True)
                    mm.then_inc(scores_done, 1)

                def turn_probs(i):
                    n, h = UNITS[i]
                    u = base + i
                    pe.wait_ge(probs_done, u + 1)
                    if u >= 2:
                        pe.wait_ge(probsT_ready, u - 1)
                    for b in range(span(kind, n)[1] // P):
                        mm = nc.tensor.transpose(banks[2 + u % 2][:, b * P:(b + 1) * P],
                                                 logits[:, u % 2, b * P:(b + 1) * P], ident)
                    mm.then_inc(probsT_done, 1)

                def weigh(i):
                    n, h = UNITS[i]
                    u = base + i
                    s0, w_ = span(kind, n)
                    pe.wait_ge(probsT_ready, u + 1)
                    if u >= 2:
                        pe.wait_ge(out_ready, u - 1)
                    for b in range(w_ // P):
                        mm = nc.tensor.matmul(banks[4 + u % 2][:, 0:HD], probsT[:, u % 2, b * P:(b + 1) * P],
                                              head_v(kind, s0 // P + b, h), start=(b == 0), stop=(b == w_ // P - 1))
                    mm.then_inc(out_done, 1)

                def turn_out(n):
                    g = base // 8 + n
                    pe.wait_ge(out_ready, base + 8 * (n + 1))
                    if g >= 2:
                        pe.wait_ge(outT_ready, g - 1)
                    for t in range(4):
                        mm = nc.tensor.transpose(banks[6 + g % 2][:, t * P:(t + 1) * P],
                                                 heads_out[:, g % 2, t * P:(t + 1) * P], ident)
                    mm.then_inc(outT_done, 1)

                for i in range(len(UNITS) + 4):
                    if i < len(UNITS):
                        score(i)
                    if 1 <= i <= len(UNITS):
                        turn_probs(i - 1)
                    if 2 <= i < len(UNITS) + 2:
                        weigh(i - 2)
                    if i >= 11 and (i - 11) % 8 == 0:
                        turn_out((i - 11) // 8)

            def even_out():
                halves("even_out", "w_o_even", mixT, "v" * 8)
                flip(F["even_out"], x, 9)

            def odd_out():
                halves("odd_out", "w_o_odd", mixT, "v" * 8)
                flip(F["odd_out"], x, 9)

            def route(l):
                f = F[f"route{l}"]
                for n in range(NT):
                    mm = product(banks[0][:, n * E:(n + 1) * E],
                                 [(xT[:, t, n * P:(n + 1) * P], router_w[:, t, :]) for t in range(KD)])
                mm.then_inc(f.mm, 1)
                pe.wait_ge(f.v, 1)
                for n in range(NT):
                    mm = product(banks[1][:, n * E:(n + 1) * E],
                                 [(operand["before"] if m == n else operand["ones"], chosen[:, m, :]) for m in range(n + 1)])
                mm = product(banks[1][:, NT * E:(NT + 1) * E], [(operand["ones"], chosen[:, m, :]) for m in range(NT)])
                mm.then_inc(f.mm, 1)

            def turn_x(b, landed_):
                pe.wait_ge(gathered[b], landed_)
                for g in range(2):
                    for t in range(4):
                        mm = nc.tensor.transpose(banks[g][:, t * P:(t + 1) * P],
                                                 xg[:, b, (4 * g + t) * P:(4 * g + t + 1) * P], ident)
                    mm.then_inc(xgT_done, 1)

            def expert(l, s, e, loads, b, next_landed):
                gate_w = ring[:, s[0], :].rearrange("p (k n) -> p k n", k=KD)
                up_w = ring[:, s[1], :].rearrange("p (k n) -> p k n", k=KD)
                down_w = ring[:, s[2], :].rearrange("p (k n) -> p k n", k=4)
                pe.wait_ge(xgT_ready, 2 * e + 2 + 2 * l)
                for j, w_ in enumerate((gate_w, up_w)):
                    pe.wait_ge(w_loaded[s[j]], loads[j])
                    product(banks[2 + j][:, :], [(xgT[:, t, :], w_[:, t, :]) for t in range(KD)])\
                        .then_inc(gate_up_done, 1)
                turn_x(1 - b, next_landed)
                pe.wait_ge(gate_up_done, 2 * e + 2)
                pe.sem_inc(w_used, 1)
                pe.sem_inc(w_used, 1)
                pe.wait_ge(h_ready, e + 1)
                for t in range(4):
                    mm = nc.tensor.transpose(banks[4][:, t * P:(t + 1) * P], hid[:, t * P:(t + 1) * P], ident)
                mm.then_inc(hT_done, 1)
                pe.wait_ge(hT_ready, e + 1)
                pe.wait_ge(w_loaded[s[2]], loads[2])
                for j in range(2):
                    pe.wait_ge(y_ready, 2 * e + 1 + j)
                    product(banks[5 + j][:, :], [(hidT[:, t, :], down_w[:, t, j * 512:(j + 1) * 512]) for t in range(4)])\
                        .then_inc(y_done, 1)
                pe.wait_ge(y_done, 2 * e + 2)
                pe.sem_inc(w_used, 1)

            def experts(l):
                c0 = first_expert_chunk[l]
                turn_x(0, 16 * (9 * l + 1))
                with pe.Fori(0, E // 2) as it:
                    for b in range(2):
                        cs = [c0 + 3 * b + j for j in range(3)]
                        expert(l, [c % RING for c in cs], it * 2 + (E * l + b),
                               [it * 16 + 16 * (c // RING + 1) for c in cs], b,
                               it * 16 + 16 * (8 * l + 1 + b * (l + 1)))

            def overflow(l):
                n, done = slots_of(pe, l)
                gate_w, up_w = (over_w[:, i, :].rearrange("p (k n) -> p k n", k=KD) for i in range(2))
                down_w = over_w[:, 0, :].rearrange("p (k n) -> p k n", k=4)
                with pe.If(n > 0):
                    with pe.Fori(0, n) as slot:
                        j = slot + done
                        pe.wait_ge(over["in"], j * 48 + 48)
                        for g in range(2):
                            for t in range(4):
                                mm = nc.tensor.transpose(banks[g][:, t * P:(t + 1) * P],
                                                         xg[:, 0, (4 * g + t) * P:(4 * g + t + 1) * P], ident)
                            mm.then_inc(over["xT_mm"], 1)
                        pe.wait_ge(over["xT"], j * 2 + 2)
                        for i, w_ in enumerate((gate_w, up_w)):
                            product(banks[2 + i][:, :], [(xgT[:, t, :], w_[:, t, :]) for t in range(KD)])\
                                .then_inc(over["gate_up_mm"], 1)
                        pe.wait_ge(over["h"], j + 1)
                        for t in range(4):
                            mm = nc.tensor.transpose(banks[4][:, t * P:(t + 1) * P], hid[:, t * P:(t + 1) * P], ident)
                        mm.then_inc(over["hT_mm"], 1)
                        pe.wait_ge(over["hT"], j + 1)
                        pe.wait_ge(over["down_in"], j * 16 + 16)
                        for i in range(2):
                            product(banks[5 + i][:, :], [(hidT[:, t, :], down_w[:, t, i * 512:(i + 1) * 512])
                                                         for t in range(4)]).then_inc(over["y_mm"], 1)

            def combine(l):
                if l == 0:
                    flip(F["combine0"], x, 1)

            def odd_in():
                f, k = F["odd_in"], 0
                (a0, c0), (a1_, c1), (a2, c2) = by_name["odd_w_in_2"]
                pe.wait_ge(pack_loaded["odd"], 16)
                arrived(a0)
                for g in range(4):
                    features(f, ODD_IN, k, a0, c0, g * P)
                    k += 1
                release(f.mm, k)
                arrived(a1_)
                features(f, ODD_IN, k, a1_, c1, 0, HD)
                k += 1
                for n in range(NT):
                    tokens(f, ODD_IN, k, a1_, c1, n, HD, 2 * HD)
                    k += 1
                for g in range(2):
                    features(f, ODD_IN, k, a1_, c1, P + g * P)
                    k += 1
                features(f, ODD_IN, k, a1_, c1, 384, HD)
                k += 1
                for n in range(NT):
                    tokens(f, ODD_IN, k, a1_, c1, n, 448, 452)
                    k += 1
                release(f.mm, k)
                arrived(a2)
                for n in range(NT):
                    tokens(f, ODD_IN, k, a2, c2, n, 0, 384)
                    k += 1
                features(f, ODD_IN, k, a2, c2, 320, MLA)
                k += 1
                release(f.mm, k)
                for t in range(3):
                    bank_emptied(f, ODD_IN + "vvv", k + t)
                    for n in range(NT):
                        pe.wait_ge(f.s, n + 1)
                        mm = nc.tensor.transpose(banks[(k + t) % 8][:, n * P:(n + 1) * P],
                                                 cqkv[:, n, t * P:(t + 1) * P], ident)
                    mm.then_inc(f.mm, 1)

            def index():
                f, k = F["index"], 0
                for n in range(1, NT):
                    for h in range(4):
                        if k >= 4:
                            pe.wait_ge(f.a, k - 3)
                        a = (h % 2) * HD
                        nc.tensor.matmul(banks[k % 4][:, 0:(n + 1) * P], qI[a:a + HD, h // 2, n * P:(n + 1) * P],
                                         kI[a:a + HD, 0:(n + 1) * P], start=True, stop=True).then_inc(f.mm, 1)
                        k += 1

            def latent():
                f = F["latent"]
                (aq, cq_), = by_name["odd_w_uq_2"]
                (akv, ckv_), = by_name["odd_w_ukv_2"]
                uq, ukv = slot_view(aq, cq_), slot_view(akv, ckv_)
                turn = operand["turn"][0:MLA, :]
                nc.tensor.matmul(banks[0][0:MLA, :], turn, krT[0:MLA, :], start=True, stop=True).then_inc(f.mm, 1)
                arrived(aq)
                k = 1
                for h in range(8):
                    bank_emptied(f, LATENT, k)
                    product(banks[k % 8][0:MLA, :], [(uq[:, t, h * MLA:(h + 1) * MLA], cqT[:, t, :]) for t in range(2)])\
                        .then_inc(f.mm, 1)
                    bank_emptied(f, LATENT, k + 1)
                    pe.wait_ge(f.a, h + 1)
                    nc.tensor.matmul(banks[(k + 1) % 8][0:MLA, :], turn, raw[0:MLA, h % 2, :], start=True, stop=True)\
                        .then_inc(f.mm, 1)
                    k += 2
                release(f.mm, k)
                arrived(akv)
                for h in range(8):
                    bank_emptied(f, LATENT, k)
                    nc.tensor.matmul(banks[k % 8][0:HD, :], ukv[:, 0, h * P:h * P + HD], ckvT, start=True, stop=True)\
                        .then_inc(f.mm, 1)
                    k += 1
                v_cols = ukv[:, 0, :].rearrange("p (h d) -> p h d", h=8)[:, :, HD:P]
                for n in range(NT):
                    bank_emptied(f, LATENT, k)
                    nc.tensor.matmul(banks[k % 8][:, :], ckvT[:, n * P:(n + 1) * P], v_cols, start=True, stop=True)\
                        .then_inc(f.mm, 1)
                    k += 1
                release(f.mm, k)

            run = {
                "norm1": norm1, "project": project, "mixers": mixers, "hgrn": hgrn, "mix_out": mix_out,
                "norm2": lambda: norm("norm2"), "up": up, "down": down, "norm3": lambda: norm("norm3"),
                "gate": gate, "final_norm": final_norm, "even_in": even_in,
                "even_a": lambda: attend("even_a"), "even_b": lambda: attend("even_b"), "even_out": even_out,
                "route0": lambda: route(0), "experts0": lambda: experts(0), "combine0": lambda: combine(0),
                "odd_in": odd_in, "index": index, "odd_c": lambda: attend("odd_c"), "latent": latent,
                "odd_d": lambda: attend("odd_d"), "odd_out": odd_out,
                "overflow0": lambda: overflow(0), "overflow1": lambda: overflow(1), "route1": lambda: route(1), "experts1": lambda: experts(1), "combine1": lambda: combine(1),
            }
            for s in stages:
                if s in run:
                    run[s]()
                meet()

        @block.scalar
        def _(act):
            meets = [0]
            steps = [0]

            def meet():
                meets[0] += 1
                act.drain().then_inc(met, 1)
                act.wait_ge(met, 4 * meets[0])
                act.drain()

            def step(ins):
                ins.then_inc(act_step, 1)
                steps[0] += 1
                act.wait_ge(act_step, steps[0])

            A = nc.scalar.activation

            def scaled(out_, in_, s):
                return A(out_, in_, ACT.Identity, scale=s) if s is not None else A(out_, in_, ACT.Copy)

            def unflip(f, mm0, g=None):
                for k in range(0, KD, 2):
                    act.wait_ge(f.mm, mm0 + k + 1)
                    scaled(xT[:, k, :], banks[k][:, :], g[:, k:k + 1] if g is not None else None).then_inc(f.a, 1)

            def root(f, n_s, col):
                act.wait_ge(f.s, n_s)
                A(rstd, col, ACT.Sqrt).then_inc(f.a, 1)

            def norm(name, g):
                f = F[name]
                if name == "norm1":
                    act.wait_ge(x_loaded, 16)
                for n in range(NT):
                    A(normed[:, n, :], x[:, n, :], ACT.Square, accum_out=sumsq[:, n:n + 1]).then_inc(f.a, 1)
                root(f, 1, rstd)
                if name == "norm1":
                    act.wait_ge(pack_loaded["one"], 16)
                unflip(f, 0, g)

            def evacuate(f, plan, jobs):
                for k, who in enumerate(plan):
                    if who == "a":
                        act.wait_ge(f.mm, k + 1)
                        ins = None
                        for out_, in_, func, s in jobs(k, banks[k % 8]):
                            ins = A(out_, in_, func, scale=s) if s is not None else A(out_, in_, func)
                        ins.then_inc(f.a, 1)

            def project():
                def jobs(k, bank):
                    if k < 4:
                        return [(zA[:, k, :], bank[:, :], ACT.Gelu_apprx_tanh, None)]
                    if k < 8:
                        return [(zB[:, k - 4, :], bank[:, :], ACT.Gelu_apprx_tanh, None)]
                    if k < 12:
                        return [(zC[:, k - 8, :], bank[:, :], ACT.Silu if k < 10 else ACT.Sigmoid, None)]
                    return [(zC[:, k - 8, :], bank[:, :], ACT.Silu, None)]
                evacuate(F["project"], PROJECT, jobs)

            def mixers():
                step(A(lam_e, operand["lam"], ACT.Abs))
                A(lam_e, lam_e, ACT.Exp, scale=-1.0).then_inc(M["lam_exp"], 1)
                act.wait_ge(M["lb_in"], 1)
                A(lb0, lb0, ACT.Exp).then_inc(M["lb_exp"], 1)
                act.wait_ge(M["gates_mm"], 4)
                for t in range(2):
                    A(log_decay[:, t, :], banks[t][:, :], ACT.Sigmoid, bias=operand["ba"][:, t:t + 1]).then_inc(M["r_ready"], 1)
                for t in range(2):
                    A(gate_i[:, t, :], banks[2 + t][:, :], ACT.Sigmoid, bias=operand["bx"][:, t:t + 1]).then_inc(M["i_ready"], 1)
                act.wait_ge(M["var_ready"], 1)
                A(rstd, rstd, ACT.Sqrt).then_inc(M["sd_ready"], 1)
                act.wait_ge(M["decay_ready"], 2)
                for t in range(2):
                    A(decay[:, t, :], log_decay[:, t, :], ACT.Exp)
                    A(tanh_d[:, t, :], log_decay[:, t, :], ACT.Tanh).then_inc(M["decay_exp"], 1)
                for t in range(2):
                    act.wait_ge(M["mult_in"], t + 1)
                    A(tanh_d[:, t, :], tanh_d[:, t, :], ACT.Sqrt, scale=-1.0).then_inc(M["mult_ready"], 1)
                for t in range(2):
                    act.wait_ge(M["yD_mm"], t + 1)
                    scaled(mixT[:, 6 + t, :], banks[2 + t][:, :], operand["dscale"][:, t:t + 1])
                for t in range(2):
                    act.wait_ge(M["yA_mm"], t + 1)
                    scaled(mixT[:, t, :], banks[t][:, :], None)

            def hgrn():
                for pr in range(2):
                    act.wait_ge(M["hg_gate"], pr + 1)
                    A(log_f, zC[:, 2 + pr, :], ACT.Ln).then_inc(M["hg_log"], 1)
                    act.wait_ge(M["hg_decays"], pr + 1)
                    A(exp_b, bb, ACT.Exp).then_inc(M["hg_exp"], 1)
                    A(exp_end, to_end, ACT.Exp).then_inc(M["hg_exp"], 1)
                    A(decay_c, bb[:, HC - 1::HC], ACT.Exp).then_inc(M["hg_exp"], 1)
                    act.wait_ge(M["hg_kT_mm"], 2 * pr + 2)
                    scaled(keT.rearrange("p a b -> p (a b)"), banks[0][:, :], None).then_inc(M["hg_kT"], 1)
                    scaled(vT.rearrange("p a b -> p (a b)"), banks[1][:, :], None).then_inc(M["hg_kT"], 1)
                    for i in range(8):
                        act.wait_ge(M["hg_state_mm"], 8 * pr + i + 1)
                        m = 8 if i < 7 else 7
                        c0 = 8 * i + 1
                        scaled(state[:, c0:c0 + m, :].rearrange("p a b -> p (a b)"), banks[2 + i % 2][:, 0:m * HD], None)\
                            .then_inc(M["hg_state_in"], 1)
                        if i % 2:
                            qt = i // 2
                            act.wait_ge(M["hg_diff"], NT * pr + qt + 1)
                            A(pair_decay, pair_decay, ACT.Exp).then_inc(M["hg_decay"], 1)
                    act.wait_ge(M["hg_mean"], pr + 1)
                    A(exp_b, exp_b, ACT.Sqrt).then_inc(M["hg_sd"], 1)

            def up():
                f = F["up"]
                w3 = operand["fconv_w"].rearrange("p (f t) -> p f t", t=3)
                for k in range(2 * FT + 1):
                    if k < 2 * FT:
                        act.wait_ge(f.mm, k + 1)
                        if 4 <= k < FT + 4:
                            act.wait_ge(f.s, k - 3)
                        if k - 4 >= FT:
                            act.wait_ge(val_scaled, k - 4 - FT + 1)
                        A(conv[:, k % 4, :], banks[k % 8][:, :], ACT.Identity, bias=operand["fconv_b"][:, k:k + 1],
                          scale=w3[:, k, 2:3]).then_inc(f.a, 1)
                    if 1 <= k <= FT:
                        act.wait_ge(f.v, k)
                        A(hidden[:, k - 1, :], conv[:, (k - 1) % 4, :], ACT.Gelu_apprx_tanh).then_inc(f.s, 1)

            def gate():
                f = F["gate"]
                for i in range(8):
                    act.wait_ge(f.mm, 2 * i + 2)
                    if i >= 2:
                        act.wait_ge(f.v, i - 1)
                    A(gate_s[:, i % 2, :], banks[(2 * i + 1) % 8][:, :], ACT.Sigmoid).then_inc(f.a, 1)

            def final_norm():
                norm("final_norm", None)

            def even_in():
                def jobs(k, bank):
                    if k < 4:
                        return [(qA[(h // 4) * HD:(h // 4 + 1) * HD, h % 4, :], bank[(h % 2) * HD:(h % 2 + 1) * HD, :],
                                 ACT.Copy, HD ** -0.5) for h in (2 * k, 2 * k + 1)]
                    if k < 9:
                        return [(vA[:, k - 5, :], bank[:, 0:P], ACT.Copy, None)]
                    return [(kB[:, k - 13, :], bank[:, :], ACT.Copy, None)]
                f = F["even_in"]
                evacuate(f, EVEN_IN, jobs)
                act.wait_ge(f.s, 1)
                step(A(soft[0:8, 1, :], soft[0:8, 0, :], ACT.Abs))
                step(A(soft[0:8, 1, :], soft[0:8, 1, :], ACT.Exp, scale=-1.0))
                A(soft[0:8, 1, :], soft[0:8, 1, :], ACT.Ln, bias=1.0).then_inc(f.a, 1)

            def attend(stage):
                kind = KIND[stage]
                base = 32 * list(KIND).index(stage)

                def soft_max(i):
                    n, h = UNITS[i]
                    u = base + i
                    w_ = span(kind, n)[1]
                    act.wait_ge(shifted, u + 1)
                    if kind == "A":
                        A(sinkexp[:, u % 4:u % 4 + 1], operand["sinks"][:, h:h + 1], ACT.Exp, bias=negmax[:, u % 4:u % 4 + 1])
                    A(logits[:, u % 2, 0:w_], logits[:, u % 2, 0:w_], ACT.Exp, bias=negmax[:, u % 4:u % 4 + 1],
                      accum_out=rowsum[:, u % 4:u % 4 + 1]).then_inc(probs_done, 1)

                def take_probs(i):
                    n, h = UNITS[i]
                    u = base + i
                    w_ = span(kind, n)[1]
                    act.wait_ge(probsT_done, u + 1)
                    if u >= 2:
                        act.wait_ge(out_done, u - 1)
                    A(probsT[:, u % 2, 0:w_], banks[2 + u % 2][:, 0:w_], ACT.Copy).then_inc(probsT_ready, 1)

                def take_out(n):
                    g = base // 8 + n
                    act.wait_ge(outT_done, g + 1)
                    t0 = 0 if kind in "AC" else 4
                    A(mixT[:, t0:t0 + 4, n * P:(n + 1) * P], banks[6 + g % 2][:, :].rearrange("p (t q) -> p t q", t=4),
                      ACT.Copy).then_inc(outT_ready, 1)

                for i in range(len(UNITS) + 4):
                    if i < len(UNITS):
                        soft_max(i)
                    if 1 <= i <= len(UNITS):
                        take_probs(i - 1)
                    if i >= 11 and (i - 11) % 8 == 0:
                        take_out((i - 11) // 8)

            def ln_part(name, flips):
                f = F[name]
                root(f, 1, rstd)
                if flips:
                    unflip(f, 8 if name.endswith("out") else 0)

            def route(l):
                f = F[f"route{l}"]
                act.wait_ge(f.mm, 1)
                A(aff.rearrange("p a b -> p (a b)"), banks[0][:, 0:NT * E], ACT.Sigmoid).then_inc(f.a, 1)

            def take_x(done):
                for g in range(2):
                    act.wait_ge(xgT_done, done + g + 1)
                    A(xgT[:, 4 * g:4 * g + 4, :].rearrange("p a b -> p (a b)"), banks[g][:, :], ACT.Copy).then_inc(xgT_ready, 1)

            def experts(l):
                if l == 0:
                    act.sem_inc(y_ready, 2)
                    act.sem_inc(y_stored[0], 16)
                    act.sem_inc(y_stored[1], 16)
                take_x(34 * l)
                with act.Fori(0, E // 2) as it:
                    for b in range(2):
                        e = it * 2 + (E * l + b)
                        act.wait_ge(gate_up_done, e * 2 + 1)
                        A(silu_g, banks[2][:, :], ACT.Silu).then_inc(silu_ready, 1)
                        take_x(it * 4 + (34 * l + 2 * b + 2))
                        act.wait_ge(y_stored[b], it * 16 + (128 * l + 16))
                        for j in range(2):
                            act.wait_ge(y_done, e * 2 + 1 + j)
                            A(y_sb[:, b, j * 512:(j + 1) * 512], banks[5 + j][:, :], ACT.Copy).then_inc(y_ready, 1)
                        act.wait_ge(y_ready, e * 2 + 4)
                        act.dma_start(y_dram[bass.ds(it * (2 * P) + b * P, P), :], y_sb[:, b, :]).then_inc(y_stored[b], 16)
                for b in range(2):
                    act.wait_ge(y_stored[b], 128 * (l + 1) + 16)

            def overflow(l):
                n, done = slots_of(act, l)
                with act.If(n > 0):
                    with act.Fori(0, n) as slot:
                        j = slot + done
                        for g in range(2):
                            act.wait_ge(over["xT_mm"], j * 2 + g + 1)
                            A(xgT[:, 4 * g:4 * g + 4, :].rearrange("p a b -> p (a b)"), banks[g][:, :], ACT.Copy)\
                                .then_inc(over["xT"], 1)
                        act.wait_ge(over["gate_up_mm"], j * 2 + 1)
                        A(silu_g, banks[2][:, :], ACT.Silu).then_inc(over["silu"], 1)
                        for g in range(2):
                            act.wait_ge(over["y_mm"], j * 2 + g + 1)
                            step_in(A(y_sb[:, 0, g * 512:(g + 1) * 512], banks[5 + g][:, :], ACT.Copy), j * 2 + g + 1)
                        act.dma_start(y_dram[bass.ds(slot * P + E * P, P), :], y_sb[:, 0, :]).then_inc(over["stored"], 16)
                    act.wait_ge(over["stored"], (n + done) * 16 + 16)
                    act.sem_inc(over["all_stored"], 1)

            def step_in(ins, value):
                ins.then_inc(over["y"], 1)
                act.wait_ge(over["y"], value)

            def odd_in():
                def jobs(k, bank):
                    if k < 4:
                        return [(qC[:, k, :], bank[:, :], ACT.Copy, HD ** -0.5)]
                    if k < 9:
                        return [(vC[:, k - 5, :], bank[:, 0:HD], ACT.Copy, None)]
                    return [(wI[:, k - 12, :], bank[:, 0:4], ACT.Copy, 0.5)]
                f = F["odd_in"]
                evacuate(f, ODD_IN, jobs)
                for n in range(NT):
                    act.wait_ge(f.v, 4 + n + 1)
                    A(squares[:, n, 0:256], cqkv[:, n, 0:256], ACT.Square, accum_out=sumsq[:, n:n + 1])
                    A(squares[:, n, 256:384], cqkv[:, n, 256:384], ACT.Square, accum_out=mean[:, n:n + 1]).then_inc(odd_sq, 1)
                act.wait_ge(odd_var, 1)
                A(rstd, sumsq, ACT.Sqrt)
                A(wide_stat, mean, ACT.Sqrt).then_inc(odd_sq, 1)

            def index():
                f, k = F["index"], 0
                for n in range(1, NT):
                    for h in range(4):
                        act.wait_ge(f.mm, k + 1)
                        if k >= 4:
                            act.wait_ge(f.v, k - 3)
                        A(relu_d[:, k % 4, 0:(n + 1) * P], banks[k % 4][:, 0:(n + 1) * P], ACT.Relu, scale=HD ** -0.5)\
                            .then_inc(f.a, 1)
                        k += 1

            def latent():
                f, k = F["latent"], 0
                for k, who in enumerate(LATENT):
                    if who != "a":
                        continue
                    act.wait_ge(f.mm, k + 1)
                    if k < 17:
                        h = (k - 1) // 2
                        if h >= 2:
                            act.wait_ge(f.s, h - 1)
                        A(raw[0:MLA, h % 2, :], banks[k % 8][0:MLA, :], ACT.Copy, scale=MLA ** -0.5).then_inc(f.a, 1)
                    else:
                        A(kD[0:HD, k - 17, :], banks[k % 8][0:HD, :], ACT.Copy).then_inc(f.a, 1)

            def start():
                act.dma_start(pack_area["base"][:, :], w["pack_base"]).then_inc(pack_loaded["base"], 16)
                act.dma_start(pack_area["one"], w["pack_one"]).then_inc(pack_loaded["one"], 16)

            run = {
                "norm1": lambda: norm("norm1", operand["norm1"]), "project": project, "mixers": mixers, "hgrn": hgrn,
                "norm2": lambda: norm("norm2", operand["norm2"]), "up": up,
                "norm3": lambda: norm("norm3", operand["norm3"]), "gate": gate, "final_norm": final_norm,
                "even_in": even_in, "even_a": lambda: attend("even_a"), "even_b": lambda: attend("even_b"),
                "even_out": lambda: ln_part("even_out", True), "route0": lambda: route(0),
                "experts0": lambda: experts(0), "combine0": lambda: ln_part("combine0", True),
                "odd_in": odd_in, "index": index, "odd_c": lambda: attend("odd_c"), "latent": latent,
                "odd_d": lambda: attend("odd_d"), "odd_out": lambda: ln_part("odd_out", True),
                "overflow0": lambda: overflow(0), "overflow1": lambda: overflow(1), "route1": lambda: route(1), "experts1": lambda: experts(1),
                "combine1": lambda: ln_part("combine1", False),
            }
            start()
            for s in stages:
                if s in run:
                    run[s]()
                meet()

        @block.vector
        def _(dve):
            meets = [0]
            steps = [0]
            V = nc.vector

            def meet():
                meets[0] += 1
                dve.drain().then_inc(met, 1)
                dve.wait_ge(met, 4 * meets[0])
                dve.drain()

            def step(ins):
                ins.then_inc(dve_step, 1)
                steps[0] += 1
                dve.wait_ge(dve_step, steps[0])

            def mul_add(out_, in0, s, in1):
                return V.scalar_tensor_tensor(out_, in0, s, in1, ALU.mult, ALU.add)

            def scaled(out_, in_, s):
                return V.tensor_scalar(out_, in_, s, None, ALU.mult) if s is not None else V.tensor_copy(out_, in_)

            def unflip(f, mm0, g=None):
                for k in range(1, KD, 2):
                    dve.wait_ge(f.mm, mm0 + k + 1)
                    scaled(xT[:, k, :], banks[k][:, :], g[:, k:k + 1] if g is not None else None)

            def norm(name, g):
                f = F[name]
                dve.wait_ge(f.a, NT)
                V.tensor_scalar(rstd, sumsq, 1.0 / D, EPS, ALU.mult, ALU.add).then_inc(f.s, 1)
                dve.wait_ge(f.a, NT + 1)
                step(V.reciprocal(rstd, rstd))
                if name == "final_norm":
                    dve.wait_ge(rows_loaded, 16)
                for n in range(NT):
                    if name == "final_norm":
                        V.scalar_tensor_tensor(x[:, n, :], x[:, n, :], rstd[:, n:n + 1], rowsG, ALU.mult, ALU.mult)\
                            .then_inc(f.v, 1)
                    else:
                        V.tensor_scalar(normed[:, n, :], x[:, n, :], rstd[:, n:n + 1], None, ALU.mult).then_inc(f.v, 1)
                if name == "norm1":
                    dve.wait_ge(pack_loaded["one"], 16)
                unflip(f, 0, g)

            def layer_norm(name, loads, flips):
                f = F[name]
                for n in range(NT):
                    for h in range(2):
                        step(V.bn_stats(bn[:, h, :], x[:, n, h * 512:(h + 1) * 512]))
                    step(V.bn_aggr(mv[:, n, :], bn.rearrange("p h t -> p (h t)")))
                V.tensor_scalar(rstd, mv[:, :, 1], LN_EPS, None, ALU.add).then_inc(f.s, 1)
                dve.wait_ge(f.a, 1)
                step(V.reciprocal(rstd, rstd))
                dve.wait_ge(rows_loaded, 16 * loads)
                for n in range(NT):
                    step(V.tensor_scalar(x[:, n, :], x[:, n, :], mv[:, n, 0:1], rstd[:, n:n + 1], ALU.subtract, ALU.mult))
                    step(V.tensor_tensor(x[:, n, :], x[:, n, :], rowsG, ALU.mult))
                    V.tensor_tensor(x[:, n, :], x[:, n, :], rowsB, ALU.add).then_inc(f.v, 1)
                if flips:
                    unflip(f, 8 if name.endswith("out") else 0)

            def residual(name, scale):
                f = F[name]
                for k in range(8):
                    dve.wait_ge(f.mm, (20 if k >= 4 else 8) + k % 4 + 1 if name == "down" else k + 1)
                    r = x[:, k % 4, (k // 4) * 512:(k // 4 + 1) * 512]
                    mul_add(r, r, scale, banks[k][:, :]).then_inc(f.v, 1)
                dve.wait_ge(f.v, 8)

            def evacuate(f, plan, jobs):
                for k, who in enumerate(plan):
                    if who == "v":
                        dve.wait_ge(f.mm, k + 1)
                        for out_, in_, s in jobs(k, banks[k % 8]):
                            ins = scaled(out_, in_, s)
                        ins.then_inc(f.v, 1)

            def project():
                def jobs(k, bank):
                    if k < 6:
                        return [(zB[:, k - 4, :], bank[:, :], None)]
                    if k < 14:
                        return [(zC[:, k - 8, :], bank[:, :], None)]
                    return [(zD[:, k - 16, :], bank[:, :], None)]
                evacuate(F["project"], PROJECT, jobs)

            def mixers():
                cw = operand["bconv_w"].rearrange("p (t k) -> p t k", k=4)
                for t in range(2):
                    step(V.tensor_scalar(xc[:, t, :], zB[:, t, :], cw[:, t, 3:4], operand["bconv_b"][:, t:t + 1],
                                         ALU.mult, ALU.add))
                    for s in (1, 2):
                        step(mul_add(xc[:, t, s:], zB[:, t, 0:T - s], cw[:, t, 3 - s:4 - s], xc[:, t, s:]))
                    mul_add(xc[:, t, 3:], zB[:, t, 0:T - 3], cw[:, t, 0:1], xc[:, t, 3:]).then_inc(M["conv_done"], 1)
                step(V.tensor_tensor(lb0, operand["lb"], operand["lb"], ALU.subtract))
                V.tensor_scalar(lb0, lb0, 0.0, None, ALU.add).then_inc(M["lb_in"], 1)
                for n in range(NT):
                    step(V.bn_stats(bn[:, 0, :], zA[:, n, 256:512]))
                    step(V.bn_aggr(mv[:, n, :], bn[:, 0, :]))
                V.tensor_scalar(rstd, mv[:, :, 1], EPS, None, ALU.add).then_inc(M["var_ready"], 1)
                V.tensor_copy(sums0[:, :, 0:1], zD[:, :, 0:1])
                step(V.tensor_tensor(sums0[:, :, 1:], zD[:, :, 1:], zD[:, :, 0:T - 1], ALU.add))
                V.tensor_copy(sums1[:, :, 0:2], sums0[:, :, 0:2])
                step(V.tensor_tensor(sums1[:, :, 2:], sums0[:, :, 2:], sums0[:, :, 0:T - 2], ALU.add))
                V.tensor_copy(sums0[:, 1, 0:4], sums1[:, 1, 0:4])
                step(V.tensor_tensor(sums0[:, 1, 4:], sums1[:, 1, 4:], sums1[:, 1, 0:T - 4], ALU.add))
                V.tensor_copy(sums1[:, 1, 0:8], sums0[:, 1, 0:8])
                step(V.tensor_tensor(sums1[:, 1, 8:], sums0[:, 1, 8:], sums0[:, 1, 0:T - 8], ALU.add))
                count = operand["count"].rearrange("p (t c) -> p t c", c=16)
                for half_, s in enumerate((sums0, sums1)):
                    r = slice(half_ * HD, (half_ + 1) * HD)
                    for t in range(2):
                        V.scalar_tensor_tensor(pooled[r, t, 16:], s[r, t, 16:], operand["window_share"][r, t:t + 1],
                                               zD[r, t, 16:], ALU.mult, ALU.subtract)
                    step(V.tensor_tensor(s[r, :, 0:16], s[r, :, 0:16], count[r, :, :], ALU.mult))
                    V.tensor_tensor(pooled[r, :, 0:16], s[r, :, 0:16], zD[r, :, 0:16], ALU.subtract)\
                        .then_inc(M["pooled"], 1)
                dve.wait_ge(M["lam_exp"], 1)
                step(V.tensor_scalar(lam_s, lam_e, 2.0, None, ALU.add))
                step(V.reciprocal(lam_s, lam_s))
                step(V.tensor_tensor(lam_s, lam_s, lam_e, ALU.mult))
                step(V.tensor_tensor(lam_q, lam_s, lam_s, ALU.mult))
                step(V.tensor_scalar(lam_p, lam_q, 1.0 / 17, None, ALU.mult))
                for m in (15, 13, 11, 9, 7, 5, 3):
                    step(V.scalar_tensor_tensor(lam_p, lam_p, 1.0 / m, lam_q, ALU.add, ALU.mult))
                step(V.scalar_tensor_tensor(lam_p, lam_p, 1.0, lam_s, ALU.add, ALU.mult))
                step(V.tensor_scalar(lam_c, operand["lam"], -1.0, 0.0, ALU.mult, ALU.max))
                step(mul_add(lam_c, lam_p, 2.0, lam_c))
                step(V.tensor_scalar(lam_c, lam_c, -8.0, None, ALU.mult))
                for t in range(2):
                    dve.wait_ge(M["r_ready"], t + 1)
                    V.tensor_scalar(log_decay[:, t, :], log_decay[:, t, :], lam_c[:, t:t + 1], None, ALU.mult)\
                        .then_inc(M["decay_ready"], 1)
                dve.wait_ge(M["sd_ready"], 1)
                step(V.reciprocal(rstd, rstd))
                for n in range(NT):
                    v_ = zA[:, n, 256:512]
                    step(V.tensor_scalar(v_, v_, mv[:, n, 0:1], rstd[:, n:n + 1], ALU.subtract, ALU.mult))
                    step(V.tensor_tensor(v_, v_, operand["aln_g"], ALU.mult))
                    V.tensor_tensor(v_, v_, operand["aln_b"], ALU.add).then_inc(M["vn_ready"], 1)
                for t in range(2):
                    dve.wait_ge(M["decay_exp"], t + 1)
                    step(V.tensor_tensor(log_decay[:, t, :], decay[:, t, :], decay[:, t, :], ALU.mult))
                    V.scalar_tensor_tensor(tanh_d[:, t, :], log_decay[:, t, :], 1.0, tanh_d[:, t, :], ALU.add, ALU.mult)\
                        .then_inc(M["mult_in"], 1)
                for t in range(2):
                    dve.wait_ge(M["i_ready"], t + 1)
                    step(V.tensor_tensor(gate_i[:, t, :], gate_i[:, t, :], xc[:, t, :], ALU.mult))
                    dve.wait_ge(M["mult_ready"], t + 1)
                    step(V.tensor_tensor(gate_i[:, t, :], gate_i[:, t, :], tanh_d[:, t, :], ALU.mult))
                    step(V.tensor_tensor_scan(log_decay[:, t, :], decay[:, t, :], gate_i[:, t, :], 0.0, ALU.mult, ALU.add))
                    V.tensor_tensor(mixT[:, 2 + t, :], log_decay[:, t, :], zB[:, 2 + t, :], ALU.mult)
                for n in range(NT):
                    dve.wait_ge(M["spatial_mm"], n + 1)
                    for h in range(4):
                        c = slice(h * HD, (h + 1) * HD)
                        ins = V.scalar_tensor_tensor(zA[:, n, c], banks[4 + n][:, c], operand["bs"][:, h:h + 1],
                                                     zA[:, n, c], ALU.add, ALU.mult)
                    ins.then_inc(M["yA_ready"], 1)
                dve.wait_ge(M["lb_exp"], 1)
                step(V.reciprocal(omlb, lb0))
                step(V.tensor_tensor(lb0, lb0, omlb, ALU.mult))
                step(V.tensor_tensor(lb0, lb0, lb0, ALU.subtract))
                step(V.tensor_scalar(omlb, lb0, -1.0, 1.0, ALU.mult, ALU.add))

            def hgrn():
                def chunks(a, q0=0, q=NC):
                    return a.rearrange("p (c j) -> p c j", j=HC)[:, q0:q0 + q, :]
                for pr in range(2):
                    f_ = zC[:, 2 + pr, :]
                    step(V.tensor_scalar(f_, f_, omlb[:, pr:pr + 1], lb0[:, pr:pr + 1], ALU.mult, ALU.add))
                    V.memset(state[:, 0, :], 0.0).then_inc(M["hg_gate"], 1)
                    dve.wait_ge(M["hg_log"], pr + 1)
                    V.tensor_scalar(f_, f_, -1.0, 1.0, ALU.mult, ALU.add)
                    step(V.tensor_tensor_scan(bb, operand["inside"], log_f, 0.0, ALU.mult, ALU.add))
                    V.tensor_tensor(chunks(to_end), chunks(bb)[:, :, HC - 1:HC].to_broadcast([P, NC, HC]), chunks(bb),
                                    ALU.subtract).then_inc(M["hg_decays"], 1)
                    dve.wait_ge(M["hg_exp"], 3 * pr + 3)
                    V.tensor_tensor(qe, zC[:, pr, :], exp_b, ALU.mult)
                    V.tensor_tensor(ke, f_, exp_end, ALU.mult).then_inc(M["hg_exps"], 1)
                    q4 = NC // NT
                    pd = pair_decay.rearrange("p (c t s) -> p c t s", t=HC, s=HC)
                    pv = pair_v.rearrange("p (c t s) -> p c t s", t=HC, s=HC)
                    shape = [P, q4, HC, HC]
                    hm = operand["hmask"].rearrange("p (t s) -> p t s", s=HC).unsqueeze(1).to_broadcast(shape)
                    next_state = [1]

                    def advance(n):
                        for _ in range(n):
                            c = next_state[0]
                            if c >= NC:
                                return
                            dve.wait_ge(M["hg_state_in"], 8 * pr + (c - 1) // 8 + 1)
                            if c % 8 == 7:
                                mul_add(state[:, c, :], state[:, c - 1, :], decay_c[:, c - 1:c], state[:, c, :])\
                                    .then_inc(M["hg_state"], 1)
                                dve.wait_ge(M["hg_state"], 8 * pr + c // 8 + 1)
                            else:
                                step(mul_add(state[:, c, :], state[:, c - 1, :], decay_c[:, c - 1:c], state[:, c, :]))
                            next_state[0] += 1

                    for qt in range(NT):
                        k = NT * pr + qt
                        c0 = q4 * qt
                        t0, t1 = c0 * HC, (c0 + q4) * HC
                        as_t = lambda a: chunks(a, c0, q4).unsqueeze(3).to_broadcast(shape)
                        as_s = lambda a: chunks(a, c0, q4).unsqueeze(2).to_broadcast(shape)
                        if qt:
                            dve.wait_ge(M["hg_att_mm"], k)
                        step(V.tensor_tensor(pd, as_t(bb), as_s(bb), ALU.subtract))
                        V.tensor_tensor(pd, pd, hm, ALU.min).then_inc(M["hg_diff"], 1)
                        advance(16 if qt else 0)
                        dve.wait_ge(M["hg_decay"], k + 1)
                        step(V.tensor_tensor(pd, pd, as_t(zC[:, pr, :]), ALU.mult))
                        V.tensor_tensor(pd, pd, as_s(f_), ALU.mult).then_inc(M["hg_att"], 1)
                        dve.wait_ge(M["hg_att_mm"], k + 1)
                        for b in range(2):
                            part = slice(b * q4 // 2, (b + 1) * q4 // 2)
                            att = banks[4 + 2 * (k % 2) + b][:, :].rearrange("p (c t s) -> p c t s", t=HC, s=HC)
                            ins = V.tensor_tensor(pv[:, part], att, as_s(zC[:, 4 + pr, :])[:, part], ALU.mult)
                        ins.then_inc(M["hg_used"], 1)
                        dve.wait_ge(M["hg_used"], k + 1)
                        V.tensor_reduce(mixT[:, 4 + pr, t0:t1], pair_v.rearrange("p (t s) -> p t s", s=HC), AX.X, ALU.add)
                    advance(NC)
                    dve.wait_ge(M["hg_inter_mm"], pr + 1)
                    o = mixT[:, 4 + pr, :]
                    step(V.tensor_tensor(o, banks[1][:, :], o, ALU.add))
                    V.tensor_tensor(o_sq, o, o, ALU.mult).then_inc(M["hg_square"], 1)
                    dve.wait_ge(M["hg_mean_mm"], pr + 1)
                    V.tensor_scalar(exp_b, banks[0][:, :], EPS, None, ALU.add).then_inc(M["hg_mean"], 1)
                    dve.wait_ge(M["hg_sd"], pr + 1)
                    step(V.reciprocal(exp_b, exp_b))
                    step(V.tensor_tensor(o, o, exp_b, ALU.mult))
                    step(V.scalar_tensor_tensor(o, o, operand["cnorm"][:, 0:1], zC[:, 6 + pr, :], ALU.mult, ALU.mult))

            def up():
                f = F["up"]
                w3 = operand["fconv_w"].rearrange("p (f t) -> p f t", t=3)
                for k in range(2 * FT):
                    c = conv[:, k % 4, :]
                    dve.wait_ge(f.a, k + 1)
                    step(mul_add(c[:, 1:], banks[k % 8][:, 0:T - 1], w3[:, k, 1:2], c[:, 1:]))
                    mul_add(c[:, 2:], banks[k % 8][:, 0:T - 2], w3[:, k, 0:1], c[:, 2:]).then_inc(f.v, 1)
                    if k >= FT:
                        dve.wait_ge(f.v, k + 1)
                        dve.wait_ge(f.s, k - FT + 1)
                        V.tensor_tensor(hidden[:, k - FT, :], hidden[:, k - FT, :], c, ALU.mult).then_inc(val_scaled, 1)

            def gate():
                f = F["gate"]
                for i in range(8):
                    dve.wait_ge(f.a, i + 1)
                    V.tensor_tensor(gate_t[:, i % 2, :], banks[(2 * i) % 8][:, :], gate_s[:, i % 2, :], ALU.mult)\
                        .then_inc(f.v, 1)
                    dve.wait_ge(f.v, i + 1)
                    r = x[:, i % 4, (i // 4) * 512:(i // 4 + 1) * 512]
                    V.tensor_tensor(r, r, gate_t[:, i % 2, :], ALU.add)

            def even_in():
                f = F["even_in"]

                def jobs(k, bank):
                    if k == 4:
                        return [(kA, bank[:, :], None)]
                    if k < 13:
                        return [(qB[:, k - 9, :], bank[:, :], HD ** -0.5)]
                    return [(vB[:, k - 17, :], bank[:, :], None)]
                evacuate(f, EVEN_IN[:21], jobs)
                dve.wait_ge(f.mm, 22)
                V.tensor_scalar(soft[0:8, 0, :], banks[21 % 8][0:8, :], operand["fg_b"][0:8, 0:1], None, ALU.add)\
                    .then_inc(f.s, 1)
                dve.wait_ge(f.a, EVEN_IN.count("a") + 1)
                V.scalar_tensor_tensor(soft[0:8, 0, :], soft[0:8, 0, :], 0.0, soft[0:8, 1, :], ALU.min, ALU.subtract)\
                    .then_inc(f.s, 1)
                dve.wait_ge(f.s, 2)
                V.tensor_tensor_scan(cum[0:8, :], soft[0:8, 0, :], soft[0:8, 0, :], 0.0, ALU.add, ALU.bypass)\
                    .then_inc(f.s, 1)
                dve.wait_ge(f.s, 3)
                V.tensor_scalar(negc[0:8, :], cum[0:8, :], -1.0, None, ALU.mult)
                dve.wait_ge(f.mm, 23)
                V.tensor_copy(cT.rearrange("p a b -> p (a b)"), banks[22 % 8][:, 0:32])

            def attend(stage):
                kind = KIND[stage]
                base = 32 * list(KIND).index(stage)
                slopes = alibi_slopes(8)

                def bias(i):
                    n, h = UNITS[i]
                    u = base + i
                    w_ = span(kind, n)[1]
                    c = slice(u % 4, u % 4 + 1)
                    l_, bank = logits[:, u % 2, 0:w_], banks[u % 2][:, 0:w_]
                    dve.wait_ge(scores_done, u + 1)
                    if u >= 2:
                        dve.wait_ge(probsT_done, u - 1)
                    mask = causal[:, T - w_:T]
                    if kind == "A":
                        ins = V.tensor_tensor(l_, bank, operand["window"][:, (h + 1) * 256 - w_:(h + 1) * 256], ALU.add)
                    elif kind == "B":
                        ins = V.scalar_tensor_tensor(l_, bank, cT[:, n, h:h + 1], mask, ALU.add, ALU.add)
                    elif kind == "C":
                        d0 = n * (n + 1) // 2
                        ins = mul_add(l_, distsel[:, d0:d0 + n + 1, :].rearrange("p a b -> p (a b)"), -float(slopes[h]), bank)
                    else:
                        ins = V.tensor_tensor(l_, bank, mask, ALU.add)
                    ins.then_inc(biased, 1)
                    dve.wait_ge(biased, u + 1)
                    step(V.tensor_reduce(rowmax[:, c], l_, AX.X, ALU.max))
                    low = operand["sinks"][:, h:h + 1] if kind == "A" else TAKEN
                    V.tensor_scalar(negmax[:, c], rowmax[:, c], low, -1.0, ALU.max, ALU.mult).then_inc(shifted, 1)

                def finish(i):
                    n, h = UNITS[i]
                    u = base + i
                    g = base // 8 + n
                    c = slice(u % 4, u % 4 + 1)
                    dve.wait_ge(out_done, u + 1)
                    if kind == "A":
                        step(V.tensor_tensor(recip[:, c], rowsum[:, c], sinkexp[:, c], ALU.add))
                        step(V.reciprocal(recip[:, c], recip[:, c]))
                    else:
                        step(V.reciprocal(recip[:, c], rowsum[:, c]))
                    if h == 0 and g >= 2:
                        dve.wait_ge(outT_done, g - 1)
                    V.tensor_scalar(heads_out[:, g % 2, h * HD:(h + 1) * HD], banks[4 + u % 2][:, 0:HD], recip[:, c], None,
                                    ALU.mult).then_inc(out_ready, 1)

                for i in range(len(UNITS) + 2):
                    if i < len(UNITS):
                        bias(i)
                    if i >= 2:
                        finish(i - 2)

            def route(l):
                f = F[f"route{l}"]
                wide = [P, NT, E]
                g4 = lambda a: a.rearrange("p n (g i) -> p (n g) i", i=4)
                flat = lambda a: a.rearrange("p a b -> p (a b)")
                dve.wait_ge(f.a, 1)
                step(V.tensor_tensor(sel, aff, operand["router_b"].unsqueeze(1).to_broadcast(wide), ALU.add))

                def ranks(a, r, tmp):
                    step(V.memset(r, 0.0))
                    for d in (1, 2, 3):
                        c = tmp[:, :, 0:4 - d]
                        step(V.tensor_tensor(c, a[:, :, 0:4 - d], a[:, :, d:4], ALU.is_ge))
                        step(V.tensor_tensor(r[:, :, d:4], r[:, :, d:4], c, ALU.add))
                        step(V.scalar_tensor_tensor(r[:, :, 0:4 - d], r[:, :, 0:4 - d], 1.0, c, ALU.add, ALU.subtract))

                ranks(g4(sel), g4(rank), g4(cmp))
                step(V.tensor_scalar(flat(tmp16), flat(rank), 2.0, None, ALU.is_lt))
                step(V.tensor_tensor(flat(tmp16), flat(tmp16), flat(sel), ALU.mult))
                step(V.tensor_reduce(flat(gsum), g4(tmp16), AX.X, ALU.add))
                ranks(gsum, trank, gpick)
                step(V.tensor_scalar(flat(gpick), flat(trank), 0.0, None, ALU.is_equal))
                picked = flat(gpick).unsqueeze(2).to_broadcast([P, NT * 4, 4])
                for j, m in enumerate((first, second)):
                    step(V.tensor_scalar(flat(m), flat(rank), float(j), None, ALU.is_equal))
                    step(V.tensor_tensor(g4(m), g4(m), picked, ALU.mult))
                V.tensor_tensor(flat(chosen), flat(first), flat(second), ALU.add).then_inc(f.v, 1)
                for j, m in enumerate((first, second)):
                    step(V.tensor_tensor(flat(tmp16), flat(m), flat(aff), ALU.mult))
                    step(V.tensor_reduce(weight[:, j, :], tmp16, AX.X, ALU.add))
                step(V.tensor_tensor(wsum, weight[:, 0, :], weight[:, 1, :], ALU.add))
                step(V.reciprocal(wsum, wsum))
                for j in range(2):
                    step(V.tensor_tensor(weight[:, j, :], weight[:, j, :], wsum, ALU.mult))
                dve.wait_ge(f.mm, 2)
                tot = banks[1][:, NT * E:(NT + 1) * E]
                need = operand["over_need"].rearrange("p (k e) -> p k e", e=E)
                step(V.tensor_tensor(flags, tot.unsqueeze(1).to_broadcast([P, 3, E]), need, ALU.is_gt))
                step(V.tensor_tensor_scan(flat(before_), flat(flags), flat(flags), 0.0, ALU.add, ALU.bypass))
                step(V.tensor_copy(over_n[:, l:l + 1], flat(before_)[:, 3 * E - 1:3 * E]))
                step(V.tensor_tensor(before_, before_, flags, ALU.subtract))
                step(V.tensor_tensor(picked_e, flat(before_).unsqueeze(1).to_broadcast([P, 8, 3 * E]),
                                     operand["over_j"].unsqueeze(2).to_broadcast([P, 8, 3 * E]), ALU.is_equal))
                step(V.tensor_tensor(flat(hits), flat(flags), operand["over_e"], ALU.mult))
                step(V.tensor_tensor(picked_e, picked_e, flat(hits).unsqueeze(1).to_broadcast([P, 8, 3 * E]), ALU.mult))
                step(V.tensor_reduce(e_list, picked_e, AX.X, ALU.add))
                step(V.tensor_copy(over_list[:, :], e_list))
                step(V.scalar_tensor_tensor(flat(before_), flat(before_), float(P), operand["over_row"], ALU.mult, ALU.add))
                step(V.tensor_tensor(step_k[:, 0, :], before_[:, 0, :], operand["expert_row"], ALU.subtract))
                step(V.tensor_tensor(step_k[:, 1:3, :], before_[:, 1:3, :], before_[:, 0:2, :], ALU.subtract))
                ranked_n = banks[1][:, 0:NT * E].rearrange("p (n e) -> p n e", e=E)
                step(V.tensor_copy(ranked, ranked_n))
                step(V.tensor_tensor(posn, ranked, operand["expert_row"].unsqueeze(1).to_broadcast(wide), ALU.add))
                for k in (1, 2, 3):
                    step(V.tensor_scalar(flat(tmp16), flat(ranked), float(k * P), None, ALU.is_ge))
                    step(V.tensor_tensor(tmp16, tmp16, step_k[:, k - 1, :].unsqueeze(1).to_broadcast(wide), ALU.mult))
                    step(V.tensor_tensor(flat(posn), flat(posn), flat(tmp16), ALU.add))
                for j, m in enumerate((first, second)):
                    step(V.tensor_tensor(flat(tmp16), flat(m), flat(posn), ALU.mult))
                    step(V.tensor_reduce(r_place[:, j, :], tmp16, AX.X, ALU.add))
                V.tensor_copy(place[:, :, :], r_place).then_inc(f.s, 1)

            def experts(l):
                with dve.Fori(0, E // 2) as it:
                    for b in range(2):
                        e = it * 2 + (E * l + b)
                        dve.wait_ge(gate_up_done, e * 2 + 2)
                        dve.wait_ge(silu_ready, e + 1)
                        V.tensor_tensor(hid, banks[3][:, :], silu_g, ALU.mult).then_inc(h_ready, 1)
                        dve.wait_ge(hT_done, e + 1)
                        V.tensor_copy(hidT.rearrange("p a b -> p (a b)"), banks[4][:, :]).then_inc(hT_ready, 1)

            def overflow(l):
                n, done = slots_of(dve, l)
                with dve.If(n > 0):
                    with dve.Fori(0, n) as slot:
                        j = slot + done
                        dve.wait_ge(over["gate_up_mm"], j * 2 + 2)
                        dve.wait_ge(over["silu"], j + 1)
                        V.tensor_tensor(hid, banks[3][:, :], silu_g, ALU.mult).then_inc(over["h"], 1)
                        dve.wait_ge(over["hT_mm"], j + 1)
                        V.tensor_copy(hidT.rearrange("p a b -> p (a b)"), banks[4][:, :]).then_inc(over["hT"], 1)

            def combine(l):
                for n in range(NT):
                    dve.wait_ge(rows_gathered[n], 32 * (l + 1))
                    step(V.tensor_scalar(y_rows[:, 0, n, :], y_rows[:, 0, n, :], weight[:, 0, n:n + 1], None, ALU.mult))
                    step(mul_add(y_rows[:, 0, n, :], y_rows[:, 1, n, :], weight[:, 1, n:n + 1], y_rows[:, 0, n, :]))
                    step(mul_add(x[:, n, :], x[:, n, :], ALPHA, y_rows[:, 0, n, :]))
                layer_norm(f"combine{l}", 3 + 4 * l + 2, l == 0)

            def odd_in():
                f = F["odd_in"]

                def jobs(k, bank):
                    if k == 4:
                        return [(kC[0:HD, :], bank[0:HD, :], None), (kC[HD:P, :], bank[0:HD, :], None)]
                    if k < 11:
                        return [(qI[:, k - 9, :], bank[:, :], None)]
                    if k == 11:
                        return [(kI[0:HD, :], bank[0:HD, :], None), (kI[HD:P, :], bank[0:HD, :], None)]
                    if k < 20:
                        return [(cqkv[:, k - 16, :], bank[:, 0:384], None)]
                    return [(krT[0:MLA, :], bank[0:MLA, :], None)]
                evacuate(f, ODD_IN, jobs)
                dve.wait_ge(odd_sq, NT)
                step(V.tensor_scalar(sumsq, sumsq, 1.0 / 256, EPS, ALU.mult, ALU.add))
                V.tensor_scalar(mean, mean, 1.0 / 128, EPS, ALU.mult, ALU.add).then_inc(odd_var, 1)
                dve.wait_ge(odd_sq, NT + 1)
                step(V.reciprocal(rstd, rstd))
                step(V.reciprocal(wide_stat, wide_stat))
                for n in range(NT):
                    V.tensor_scalar(cqkv[:, n, 0:256], cqkv[:, n, 0:256], rstd[:, n:n + 1], None, ALU.mult)
                    V.tensor_scalar(cqkv[:, n, 256:384], cqkv[:, n, 256:384], wide_stat[:, n:n + 1], None, ALU.mult)\
                        .then_inc(f.s, 1)
                for t in range(3):
                    dve.wait_ge(f.mm, 22 + t)
                    bank = banks[(21 + t) % 8][:, :]
                    if t < 2:
                        scaled(cqT[:, t, :], bank, operand["qnorm"][:, t:t + 1]).then_inc(f.v, 1)
                    else:
                        scaled(ckvT, bank, operand["kvnorm"][:, 0:1]).then_inc(f.v, 1)

            def index():
                f, k = F["index"], 0
                mul_add(distsel[:, 0, :], causal[:, T - P:T], -BIG / 1e30, operand["dist"][:, T - P:T])
                for n in range(1, NT):
                    w_ = (n + 1) * P
                    s = score[:, n % 2, 0:w_]
                    for h in range(4):
                        dve.wait_ge(f.a, k + 1)
                        if h == 0:
                            ins = V.tensor_scalar(s, relu_d[:, k % 4, 0:w_], wI[:, n, h:h + 1], None, ALU.mult)
                        else:
                            ins = mul_add(s, relu_d[:, k % 4, 0:w_], wI[:, n, h:h + 1], s)
                        k += 1
                        ins.then_inc(f.v, 1)
                        dve.wait_ge(f.v, k)
                    step(V.tensor_tensor(s, s, causal[:, T - w_:T], ALU.add))
                    for _ in range(TOPK // 8):
                        step(V.max(top8, s))
                        step(V.match_replace(s, top8, s, TAKEN))
                    d0 = n * (n + 1) // 2
                    step(V.tensor_scalar(s, s, -2e38, BIG, ALU.is_gt, ALU.mult))
                    V.tensor_tensor(distsel[:, d0:d0 + n + 1, :].rearrange("p a b -> p (a b)"), s,
                                    operand["dist"][:, T - w_:T], ALU.add)

            def latent():
                f = F["latent"]
                cos, sin = operand["cos"], operand["sin"]
                rope = slice(HD, MLA)
                for k, who in enumerate(LATENT):
                    if who != "v":
                        continue
                    dve.wait_ge(f.mm, k + 1)
                    bank = banks[k % 8]
                    if k == 0:
                        V.tensor_tensor(turned[rope, 0, :], bank[rope, :], sin[rope, :], ALU.mult).then_inc(f.v, 1)
                        step(V.tensor_tensor(krT[rope, :], krT[rope, :], cos[rope, :], ALU.mult))
                        step(V.tensor_tensor(krT[rope, :], krT[rope, :], turned[rope, 0, :], ALU.add))
                        V.tensor_copy(kD[rope, :, :], krT[rope, :].unsqueeze(1).to_broadcast([MLA - HD, 8, T]))
                    elif k < 17:
                        h = (k - 2) // 2
                        V.tensor_tensor(turned[0:MLA, h % 2, :], bank[0:MLA, :], sin[0:MLA, :], ALU.mult).then_inc(f.v, 1)
                        step(V.tensor_tensor(qD[0:MLA, h, :], raw[0:MLA, h % 2, :], cos[0:MLA, :], ALU.mult))
                        V.tensor_tensor(qD[0:MLA, h, :], qD[0:MLA, h, :], turned[0:MLA, h % 2, :], ALU.add).then_inc(f.s, 1)
                    else:
                        V.tensor_copy(vD[:, k - 25, :], bank[:, :]).then_inc(f.v, 1)

            def out_stage(name, loads):
                residual(name, ALPHA)
                layer_norm(name, loads, True)

            run = {
                "norm1": lambda: norm("norm1", operand["norm1"]), "project": project, "mixers": mixers, "hgrn": hgrn,
                "mix_out": lambda: residual("mix_out", 1.0), "norm2": lambda: norm("norm2", operand["norm2"]), "up": up,
                "down": lambda: residual("down", 1.0), "norm3": lambda: norm("norm3", operand["norm3"]), "gate": gate,
                "final_norm": lambda: norm("final_norm", None), "even_in": even_in,
                "even_a": lambda: attend("even_a"), "even_b": lambda: attend("even_b"),
                "even_out": lambda: out_stage("even_out", 3), "route0": lambda: route(0),
                "experts0": lambda: experts(0), "combine0": lambda: combine(0),
                "odd_in": odd_in, "index": index, "odd_c": lambda: attend("odd_c"), "latent": latent,
                "odd_d": lambda: attend("odd_d"), "odd_out": lambda: out_stage("odd_out", 7),
                "overflow0": lambda: overflow(0), "overflow1": lambda: overflow(1), "route1": lambda: route(1), "experts1": lambda: experts(1), "combine1": lambda: combine(1),
            }
            for s in stages:
                if s in run:
                    run[s]()
                meet()

        @block.gpsimd
        def _(pool):
            meets = [0]
            G = nc.gpsimd

            def meet(i):
                meets[0] += 1
                pool.drain().then_inc(met, 1)
                pool.wait_ge(met, 4 * meets[0])
                pool.drain()
                if i >= 0:
                    f = turns[i % 2]
                    for s in (f.mm, f.a, f.v, f.s):
                        pool.sem_clear(s)

            def load_rows(*names):
                for a, n in zip((rowsG, rowsB), names):
                    pool.dma_start(a, w[n]).then_inc(rows_loaded, 16)

            def project():
                G.memset(y_zero, 0.0).then_inc(pool_step, 1)
                pool.wait_ge(pool_step, 1)
                for j in range(OVER):
                    pool.dma_start(y_dram[(E + j) * P:(E + j + 1) * P, :], y_zero).then_inc(y_cleared, 16)
                G.memset(idx_zero[:, :], 0).then_inc(pool_step, 1)
                pool.dma_start(token_id[:, :], w["token_id"]).then_inc(ids_loaded, 16)
                pool.wait_ge(pool_step, 2)
                pool.dma_start(idx_dram.rearrange("(p c) o -> p (c o)", p=P), idx_zero[:, :]).then_inc(idx_cleared, 16)
                pool.wait_ge(y_cleared, 16 * OVER)

            def mixers():
                ws3 = operand["ws"].rearrange("p (h t) -> p h t", h=4)
                G.tensor_tensor(ws3, ws3, operand["wstril"].unsqueeze(1).to_broadcast([P, 4, P]), ALU.mult)\
                    .then_inc(M["ws_masked"], 1)

            def hgrn():
                of = operand["chunk_of"].unsqueeze(2).to_broadcast([P, P // HC, HD])
                for pr in range(2):
                    pool.wait_ge(M["hg_kT"], 2 * pr + 2)
                    for n in range(NT):
                        if pr or n:
                            pool.wait_ge(M["hg_state_mm"], 2 * (NT * pr + n))
                        for hh in range(2):
                            v_ = vT[:, n, hh * HD:(hh + 1) * HD].unsqueeze(1).to_broadcast([P, P // HC, HD])
                            G.tensor_tensor(v_spread[:, hh], v_, of, ALU.mult).then_inc(M["hg_v_spread"], 1)

            def norm3():
                pool.dma_start(pT.rearrange("p t q -> p (t q)"), w["pT"]).then_inc(pT_loaded, 16)

            def gate():
                pool.dma_start(pack_area["even"], w["pack_even"]).then_inc(pack_loaded["even"], 16)

            def out_stage(l, name):
                load_rows(f"ln_g_{l}_0", f"ln_b_{l}_0")
                f = F[name]
                pool.wait_ge(f.v, 12)
                pool.dma_start(x_dram.rearrange("(n p) d -> p n d", p=P), x[:, :, :]).then_inc(x_stored, 16)
                pool.wait_ge(x_stored, 16 * (l + 1))

            def route(l):
                if l == 0:
                    pool.dma_start(pack_area["odd"], w["pack_odd"]).then_inc(pack_loaded["odd"], 16)
                f = F[f"route{l}"]
                pool.wait_ge(f.s, 1)
                pool.wait_ge(ids_loaded, 16)
                pool.wait_ge(idx_cleared, 16)
                for n in range(NT):
                    for j in range(2):
                        pool.indirect_dma_start(idx_dram[:, :], bass.IndirectOffsetOnAxis(ap=place[:, j, n:n + 1], axis=0),
                                                token_id[:, n:n + 1], None).then_inc(listed, 16)
                pool.wait_ge(listed, 128 * (l + 1))
                pool.dma_start(idx_sb[:, :], idx_dram.rearrange("(e q) o -> q (e o)", q=P),
                               allow_slow_non_contiguous=True).then_inc(idx_loaded, 16)
                pool.wait_ge(idx_loaded, 16 * (l + 1))

            def experts(l):
                for e in range(E + 1):
                    if e >= 2:
                        pool.wait_ge(xgT_done, 34 * l + 2 * (e - 1))
                    pool.indirect_dma_start(xg[:, e % 2, :], None, x_dram[:, :],
                                            bass.IndirectOffsetOnAxis(ap=idx_sb[:, e:e + 1], axis=0))\
                        .then_inc(gathered[e % 2], 16)

            def overflow(l):
                if l == 0:
                    pool.sem_inc(over["stored"], 16)
                n, done = slots_of(pool, l)
                with pool.If(n > 0):
                    with pool.Fori(0, n) as slot:
                        j = slot + done
                        pool.wait_ge(over["stored"], j * 16 + 16)
                        G.tensor_copy(idx_one[:, :], idx_sb[:, bass.ds(slot + E, 1)]).then_inc(over["idx"], 1)
                        e = pool.value_load(over_list[0:1, bass.ds(slot, 1)], min_val=0, max_val=E - 1)
                        for i, name in enumerate(("moe_w_gate_2", "moe_w_up_2")):
                            src = w[name][l].rearrange("e (k p) n -> e p k n", p=P)[bass.ds(e, 1)]
                            pool.dma_start(over_w[:, i, :].rearrange("p (k n) -> p k n", k=KD), src[0]).then_inc(over["in"], 16)
                        pool.wait_ge(over["idx"], j + 1)
                        pool.sem_inc(over["passed"], 1)
                        pool.indirect_dma_start(xg[:, 0, :], None, x_dram[:, :],
                                                bass.IndirectOffsetOnAxis(ap=idx_one[:, 0:1], axis=0)).then_inc(over["in"], 16)
                        pool.wait_ge(over["gate_up_mm"], j * 2 + 2)
                        pool.sem_inc(over["passed"], 1)
                        src = w["moe_w_down_2"][l].rearrange("e (k p) n -> e p k n", p=P)[bass.ds(e, 1)]
                        pool.dma_start(over_w[:, 0, :].rearrange("p (k n) -> p k n", k=4), src[0]).then_inc(over["down_in"], 16)

            def combine(l):
                load_rows(f"ln_g_{l}_1", f"ln_b_{l}_1")
                for n in range(NT):
                    for j in range(2):
                        pool.indirect_dma_start(y_rows[:, j, n, :], None, y_dram[:, :],
                                                bass.IndirectOffsetOnAxis(ap=place[:, j, n:n + 1], axis=0))\
                            .then_inc(rows_gathered[n], 16)

            run = {
                "project": project, "mixers": mixers, "hgrn": hgrn, "norm3": norm3, "gate": gate,
                "final_norm": lambda: pool.dma_start(rowsG, w["final_g"]).then_inc(rows_loaded, 16),
                "even_out": lambda: out_stage(0, "even_out"), "route0": lambda: route(0),
                "experts0": lambda: experts(0), "combine0": lambda: combine(0),
                "odd_out": lambda: out_stage(1, "odd_out"), "overflow0": lambda: overflow(0), "overflow1": lambda: overflow(1), "route1": lambda: route(1),
                "experts1": lambda: experts(1), "combine1": lambda: combine(1),
            }
            for i, s in enumerate(stages):
                if s in run:
                    run[s]()
                meet(i)

        @block.sync
        def _(sp):
            sp.dma_start(x[:, :, :], w["x"][0].rearrange("(n p) d -> p n d", p=P)).then_inc(x_loaded, 16)

            def source(c):
                name, k0, nk, c0, nc_ = c
                if name.startswith("w_o_"):
                    m = w["w_o_2"][0 if name.endswith("even") else 1]
                else:
                    m = w[name][0]
                return m[k0 * P:(k0 + nk) * P, c0:c0 + nc_].rearrange("(k p) n -> p k n", p=P)

            def load(at, src, k):
                if at >= RING:
                    sp.wait_ge(w_used, at - RING + 1)
                dst = ring[:, at % RING, 0:src.shape[1] * src.shape[2]].rearrange("p (k n) -> p k n", k=src.shape[1])
                sp.dma_start(dst, src).then_inc(w_loaded[at % RING], 16)

            user = {"w_in": "project", "w_out": "mix_out", "w_up": "up", "w_down": "down", "w_pe": "gate", "w_pg": "gate",
                    "even_w_in_2": "even_in", "w_o_even": "even_out", "odd_w_in_2": "odd_in", "odd_w_uq_2": "latent",
                    "odd_w_ukv_2": "latent", "w_o_odd": "odd_out"}
            static = [(at, c) for at, c in chunks if user[c[0]] in stages]

            def load_experts(l):
                c0 = first_expert_chunk[l]
                with sp.Fori(0, E // 2) as it:
                    for b in range(2):
                        for j, name in enumerate(("moe_w_gate_2", "moe_w_up_2", "moe_w_down_2")):
                            at = c0 + 3 * b + j
                            sp.wait_ge(w_used, it * 6 + (at - RING + 1))
                            k = KD if j < 2 else 4
                            src = w[name][l].rearrange("e (k p) n -> e p k n", p=P)[bass.ds(it * 2 + b, 1)]
                            sp.dma_start(ring[:, at % RING, :].rearrange("p (k n) -> p k n", k=k), src[0])\
                                .then_inc(w_loaded[at % RING], 16)

            for at, c in static:
                if at < first_expert_chunk[0]:
                    load(at, source(c), c[2])
            if "experts0" in stages:
                load_experts(0)
                for at, c in static:
                    if at > first_expert_chunk[0]:
                        load(at, source(c), c[2])
            if "experts1" in stages:
                load_experts(1)
            sp.wait_ge(met, 4 * len(stages))
            sp.dma_start(out[0].rearrange("(n p) d -> p n d", p=P), x[:, :, :]).then_inc(stored, 16)
            sp.wait_ge(stored, 16)


BIG_INPUTS = ["x", "w_in", "w_out", "w_up", "w_down", "w_pe", "w_pg", "even_w_in_2", "odd_w_in_2", "odd_w_uq_2",
              "odd_w_ukv_2", "w_o_2", "moe_w_gate_2", "moe_w_up_2", "moe_w_down_2"]


def arrays_of(inputs):
    i = {k: np.asarray(v) for k, v in inputs.items()}
    pk = packs(i)
    arrays = {n: np.ascontiguousarray(i[n]) for n in BIG_INPUTS}
    for n, v in pk.items():
        arrays[f"pack_{n}"] = np.ascontiguousarray(np.concatenate([a for _, a in v], 1))
    arrays["pT"] = np.ascontiguousarray(i["p"][0, 0].reshape(T, 2, P).transpose(2, 1, 0)).reshape(P, -1)
    arrays["token_id"] = np.ascontiguousarray(np.arange(T, dtype=np.uint32).reshape(NT, P).T)
    arrays["final_g"] = np.ascontiguousarray(rows(i["final_g"]))
    for l in range(2):
        for j in range(2):
            arrays[f"ln_g_{l}_{j}"] = np.ascontiguousarray(rows(i["ln_g_2"][l, j]))
            arrays[f"ln_b_{l}_{j}"] = np.ascontiguousarray(rows(i["ln_b_2"][l, j]))
    return arrays, {n: [(m, a.shape[1]) for m, a in v] for n, v in pk.items()}


def program(nc, arrays, shapes, stop=None):
    w = {n: nc.dram_tensor(f"in_{n}", a.shape, mybir.dt.from_np(a.dtype), kind="ExternalInput").ap()
         for n, a in arrays.items()}
    out = nc.dram_tensor("out", (1, T, D), F32, kind="ExternalOutput").ap()
    build(nc, w, shapes, out, stop)
    return nc


def kernel(**inputs):
    from concourse import bacc
    from concourse.bass_utils import run_bass_kernel_spmd

    arrays, shapes = arrays_of(inputs)
    nc = program(bacc.Bacc("TRN2", target_bir_lowering=False, num_devices=1), arrays, shapes)
    r = run_bass_kernel_spmd(nc, [{f"in_{n}": a for n, a in arrays.items()}], core_ids=[0])
    return r.results[0]["out"]
```

```python
from contextlib import ExitStack

import numpy as np

import concourse.bass as bass
import concourse.mybir as mybir

F32 = mybir.dt.float32
U32 = mybir.dt.uint32
I32 = mybir.dt.int32
ALU = mybir.AluOpType
ACT = mybir.ActivationFunctionType
AX = mybir.AxisListType

P = 128
T = 512
NT = T // P
D = 1024
KD = D // P
EPS = 1e-6
LN_EPS = 1e-5
NEG = -1e30
TAKEN = -3e38
BIG = 1e33
ALPHA = 4 ** 0.25
DFF = 2816
FT = DFF // P
E = 16
EF = 512
TOPK = 128
OVER = 2 * T // P - 1
SLOTS = E + OVER
HC = 8
NC = T // HC
RING = 6
SLOT = 4096
HD = 64
MLA = 96


def alibi_slopes(n):
    return (2.0 ** (-8.0 * np.arange(1, n + 1, dtype=np.float32) / n)).astype(np.float32)


def cols(v, width=P):
    return np.ascontiguousarray(v.reshape(-1, width).T)


def rows(v):
    return np.broadcast_to(v.reshape(1, -1), (P, v.size))


def blockdiag(w):
    out = np.zeros((P, 2, P), np.float32)
    for h in range(4):
        a = (h % 2) * HD
        out[a:a + HD, h // 2, a:a + HD] = w[h]
    return out.reshape(P, -1)


def pad_rows(a):
    out = np.zeros((P, a.shape[1]), np.float32)
    out[:a.shape[0]] = a
    return out


def packs(i):
    q = np.arange(P)
    f = np.float32
    ident = np.eye(P, dtype=f)
    causal = np.zeros((P, T), f)
    causal[:, T - P:][q[:, None] < q[None, :]] = NEG
    base = [
        ("ident", ident), ("causal", causal),
        ("before", (q[:, None] < q[None, :]).astype(f)), ("ones", np.ones((P, P), f)),
        ("expert_row", rows(np.arange(E, dtype=f) * P)),
        ("router_w", i["router_w_2"].reshape(KD, P, E).transpose(1, 0, 2).reshape(P, -1)),
        ("router_b", rows(i["router_b_2"])),
        ("over_row", rows(np.array([(E - k) * P for k in (1, 2, 3) for e in range(E)], f))),
        ("over_e", rows(np.array([e for k in (1, 2, 3) for e in range(E)], f))),
        ("over_need", rows(np.array([k * P for k in (1, 2, 3) for e in range(E)], f))),
        ("over_j", rows(np.arange(8, dtype=f))),
    ]
    half = (q[:, None] // HD == q[None, :] // HD).astype(f)
    hmask = np.where(np.arange(HC)[:, None] >= np.arange(HC)[None, :], 0.0, NEG).astype(f)
    pos = np.arange(1, 17, dtype=f)
    win = np.array([[2, 8], [4, 16]])[q // HD]
    inside = np.ones(T, f)
    inside[::HC] = 0
    one = [
        ("norm1", cols(i["norm1_g"])), ("norm2", cols(i["norm2_g"])), ("norm3", cols(i["norm3_g"])),
        ("half", half), ("halfmean", half / HD), ("hmask", rows(hmask)),
        ("chunk_of", (q[:, None] // HC == np.arange(P // HC)[None, :]).astype(f)),
        ("inside", rows(inside)),
        ("wstril", (q[:, None] <= q[None, :]).astype(f)),
        ("ws", i["a_ws"][0].transpose(2, 0, 1).reshape(P, -1)),
        ("bs", np.ascontiguousarray(i["a_bs"][0].T)),
        ("aln_g", rows(i["a_ln_g"])), ("aln_b", rows(i["a_ln_b"])),
        ("bconv_w", i["b_conv_w"][0].reshape(4, 2, P).transpose(2, 1, 0).reshape(P, -1)),
        ("bconv_b", cols(i["b_conv_b"])), ("ba", cols(i["b_ba"])), ("bx", cols(i["b_bx"])),
        ("lam", cols(i["b_lam"])), ("wa", blockdiag(i["b_wa"][0])), ("wx", blockdiag(i["b_wx"][0])),
        ("lb", cols(i["c_lb"])), ("cnorm", np.tile(i["c_norm_g"].reshape(HD, 1), (2, 1))),
        ("dw", blockdiag(i["d_w"][0])), ("dscale", cols(i["d_scale"])),
        ("count", (1 / np.minimum(pos[None, None, :], win[:, :, None].astype(f))).astype(f).reshape(P, -1)),
        ("window_share", (1 / win).astype(f)),
        ("fconv_w", i["ffn_conv_w"][0].reshape(3, 2 * FT, P).transpose(2, 1, 0).reshape(P, -1)),
        ("fconv_b", cols(i["ffn_conv_b"])),
    ]
    dist = q[:, None] + P - np.arange(2 * P)[None, :]
    slopes = alibi_slopes(8)
    window = [np.where((dist >= 0) & (dist < P), -s * dist, NEG) for s in slopes]
    pick = np.zeros((P, 8, P), f)
    for h in range(8):
        pick[h, h, :] = 1
    even = [
        ("window", np.concatenate(window, 1).astype(f)), ("pick", pick.reshape(P, -1)),
        ("fg_w", i["even_w_in_2"][0][:, 2304:].reshape(KD, P, 8).transpose(1, 0, 2).reshape(P, -1)),
        ("fg_b", pad_rows(i["even_b_f_2"].reshape(8, 1))), ("sinks", rows(i["even_sinks_2"])),
    ]
    ang = (np.arange(T, dtype=f)[None, :] * (f(10000.0) ** (-np.arange(16, dtype=f) / f(16)))[:, None]).astype(f)
    cos = np.ones((P, T), f)
    sin = np.zeros((P, T), f)
    for a in (HD, HD + 16):
        cos[a:a + 16] = np.cos(ang)
        sin[a:a + 16] = np.sin(ang)
    turn = np.zeros((P, MLA), f)
    for a in range(16):
        turn[HD + 16 + a, HD + a] = -1
        turn[HD + a, HD + 16 + a] = 1
    odd = [
        ("dist", (q[:, None] + T - P - np.arange(T)[None, :]).astype(f)),
        ("cos", cos), ("sin", sin), ("turn", turn),
        ("qnorm", cols(i["odd_q_norm_2"])), ("kvnorm", cols(i["odd_kv_norm_2"])),
    ]
    return {"base": base, "one": one, "even": even, "odd": odd}


def chunk_plan():
    plan = []
    for name, nk, ncols, step in (("w_in", 8, 2304, 512), ("w_out", 8, 1024, 512), ("w_up", 8, 2 * DFF, 512)):
        plan += [(name, 0, nk, c, min(step, ncols - c)) for c in range(0, ncols, step)]
    for half in (0, 1):
        plan += [("w_down", k, min(8, FT - k), half * 512, 512) for k in range(0, FT, 8)]
    plan += [("w_pg", 0, 8, 0, 512), ("w_pe", 0, 2, 0, 1024), ("w_pg", 0, 8, 512, 512)]
    plan += [("even_w_in_2", 0, 8, a, b - a) for a, b in ((0, 512), (512, 768), (768, 1280), (1280, 1792), (1792, 2304))]
    plan += [("w_o_even", 0, 8, c, 512) for c in (0, 512)]
    plan += ["experts0"]
    plan += [("odd_w_in_2", 0, 8, a, b - a) for a, b in ((512, 964), (0, 512), (964, 1380))]
    plan += [("odd_w_uq_2", 0, 2, 0, 768), ("odd_w_ukv_2", 0, 1, 0, 1024)]
    plan += [("w_o_odd", 0, 8, c, 512) for c in (0, 512)]
    plan += ["experts1"]
    return plan


STAGES = [
    "norm1", "project", "mixers", "hgrn", "mix_out", "norm2", "up", "down", "norm3", "gate",
    "final_norm", "even_in", "even_a", "even_b", "even_out", "route0", "experts0", "overflow0", "combine0",
    "odd_in", "odd_c", "latent", "odd_d", "odd_out", "route1", "experts1", "overflow1", "combine1",
]


def build(nc, w, pk_shapes, out, stop=None):
    ctx = ExitStack()
    stages = STAGES[:STAGES.index(stop) + 1] if stop else STAGES

    with ctx:
        def sb(name, shape, dt=F32):
            return ctx.enter_context(nc.sbuf_tensor(name, shape, dt))

        def sem(name):
            return ctx.enter_context(nc.semaphore(name))

        banks = [ctx.enter_context(nc.psum_tensor(f"bank{b}", [P, 512], F32)) for b in range(8)]

        ring = sb("ring", [P, RING, SLOT])
        x = sb("x", [P, NT, D])
        xT = sb("xT", [P, KD, T])
        mixT = xT
        pack_area = {}
        width = {n: sum(s for _, s in v) for n, v in pk_shapes.items()}
        pack_area["base"] = sb("base", [P, width["base"]])
        overlay = sb("overlay", [P, max(width[n] for n in ("one", "even", "odd"))])
        for n in ("one", "even", "odd"):
            pack_area[n] = overlay[:, 0:width[n]]
        operand = {}
        for n, v in pk_shapes.items():
            at = 0
            for name, s in v:
                operand[name] = pack_area[n][:, at:at + s]
                at += s
        small = sb("small", [P, 256])
        token_id = sb("token_id", [P, NT], U32)
        place = sb("place", [P, 2, NT], U32)
        weight = sb("weight", [P, 2, NT])
        over_list = sb("over_list", [P, 8], I32)
        over_n = sb("over_n", [P, 2], I32)
        SCRATCH = 15360
        scratch = sb("scratch", [P, SCRATCH])

        class Area:

            def __init__(self, start=0):
                self.at = start

            def take(self, *shape):
                n = int(np.prod(shape))
                assert self.at + n <= SCRATCH, (self.at, shape)
                a = scratch[:, self.at:self.at + n]
                self.at += n
                if len(shape) == 1:
                    return a
                names = "abcd"[:len(shape)]
                return a.rearrange(f"p ({' '.join(names)}) -> p {' '.join(names)}",
                                   **{m: s for m, s in zip(names[1:], shape[1:])})

        ident, causal = operand["ident"], operand["causal"]
        x_dram = nc.dram_tensor("x_rows", (T, D), F32, kind="Internal").ap()
        y_dram = nc.dram_tensor("expert_rows", (SLOTS * P, D), F32, kind="Internal").ap()
        idx_dram = nc.dram_tensor("expert_tokens", ((SLOTS + 1) * P, 1), U32, kind="Internal").ap()

        met = sem("met")
        w_loaded = [sem(f"w_loaded{s}") for s in range(RING)]
        w_used = sem("w_used")
        x_loaded = sem("x_loaded")
        dve_step, act_step, pool_step = sem("dve_step"), sem("act_step"), sem("pool_step")
        pack_loaded = {n: sem(f"{n}_loaded") for n in pk_shapes}
        stored = sem("stored")

        class Flow:

            def __init__(self, name):
                self.mm, self.a, self.v, self.s = (sem(f"{name}_{m}") for m in ("mm", "act", "dve", "stats"))

        turns = [Flow("even_stage"), Flow("odd_stage")]
        flow = {s: turns[i % 2] for i, s in enumerate(STAGES)}

        chunks, first_expert_chunk, at = [], {}, 0
        for c in chunk_plan():
            if isinstance(c, str):
                first_expert_chunk[int(c[-1])] = at
                at += 3 * E
            else:
                chunks.append((at, c))
                at += 1
        by_name = {}
        for at, c in chunks:
            by_name.setdefault(c[0], []).append((at, c))
        total_chunks = first_expert_chunk[1] + 3 * E

        def slots_of(eng, l):
            n = eng.value_load(over_n[0:1, l:l + 1], min_val=0, max_val=OVER)
            return n, eng.value_load(over_n[0:1, 0:1], min_val=0, max_val=OVER) if l else 0

        def slot_view(at, c):
            nk, ncols = c[2], c[4]
            return ring[:, at % RING, 0:nk * ncols].rearrange("p (k n) -> p k n", k=nk)

        def others(bank_plan, k):
            j = k - 8
            return bank_plan[j], bank_plan[:j + 1].count(bank_plan[j])

        normed = Area().take(NT, D)
        a1 = Area()
        zA, zB, zC, zD = a1.take(NT, 512), a1.take(4, T), a1.take(8, T), a1.take(2, T)
        mixers_at, zC_at, zC_end = a1.at, 4096, 8192
        hidden = Area().take(FT, T)
        hidden_end = FT * T
        ae = Area()
        qA, kA, vA = ae.take(4, T), ae.take(2, T), ae.take(NT, P)
        qB, kB, vB = ae.take(4, T), ae.take(8, T), ae.take(NT, 512)
        negc = ae.take(T)
        ao = Area()
        qC, kC, vC, distsel = ao.take(4, T), ao.take(2, T), ao.take(NT, HD), ao.take(10, P)
        qI, kI, wI, cqkv = ao.take(2, T), ao.take(2, T), ao.take(NT, 4), ao.take(NT, 384)
        ad = Area()
        qD, kD, vD = ad.take(8, T), ad.take(8, T), ad.take(NT, 512)
        assert ae.at <= 12288 and max(ao.at, ad.at) <= 10240
        al = Area(10240)
        cqT, ckvT, krT = al.take(2, T), al.take(T), al.take(T)
        at_ = Area(12288)
        logits, probsT, heads_out = at_.take(2, T), at_.take(2, T), at_.take(2, 512)
        stat = small[:, 0:64]
        rowsG, rowsB = Area(8192).take(D), Area(8192 + D).take(D)
        y_rows = Area().take(2, NT, D)
        pT = Area(8192).take(2, T)
        gate_s, gate_t = Area(9216).take(2, 512), Area(10240).take(2, 512)
        conv = Area(hidden_end).take(4, T)
        alm = Area(12288)
        turned, raw = alm.take(2, T), alm.take(2, T)

        class Column:

            at = 64

            @classmethod
            def take(cls, n=1):
                a = small[:, cls.at:cls.at + n]
                cls.at += n
                assert cls.at <= 256
                return a

        sumsq, rstd, mean = Column.take(NT), Column.take(NT), Column.take(NT)
        mv = Column.take(2 * NT).rearrange("p (n t) -> p n t", t=2)
        bn = Column.take(12).rearrange("p (h t) -> p h t", t=6)
        lam_e, lam_s, lam_q, lam_p, lam_c = (Column.take(2) for _ in range(5))
        lb0, omlb = Column.take(2), Column.take(2)
        top8 = Column.take(8)
        rowmax, negmax, rowsum, sinkexp, recip = (Column.take(4) for _ in range(5))
        wide_stat = Column.take(4)
        cT = Column.take(8 * NT).rearrange("p (n h) -> p n h", h=8)

        F = flow
        PROJECT = "aaaa" + "vvaa" + "aaaa" + "vvaa" + "vv"
        EVEN_IN = "aaaa" + "vaaaa" + "vvvv" + "aaaa" + "vvvv" + "v"
        ODD_IN = "vvv" + "v" + "aaaa" + "aaaa" + "a" * 12 + "aaaa" + "aaaa" + "a"
        INDEX = [(n, h) for n in range(1, NT) for h in range(4)]
        UNITS = [(n, h) for n in range(NT) for h in range(8)]
        KIND = {"even_a": "A", "even_b": "B", "odd_c": "C", "odd_d": "D"}

        def span(kind, n):
            if kind == "A":
                return max(0, n - 1) * P, P * min(2, n + 1)
            return 0, (n + 1) * P

        def head_q(kind, n, h):
            t = slice(n * P, (n + 1) * P)
            if kind == "A":
                return qA[:, h % 4, t]
            if kind in "BC":
                return (qB if kind == "B" else qC)[:, h // 2, t]
            return qD[0:MLA, h, t]

        def head_k(kind, n, h):
            s0, w_ = span(kind, n)
            s = slice(s0, s0 + w_)
            if kind == "A":
                return kA[:, h // 4, s]
            if kind == "B":
                return kB[:, h, s]
            if kind == "C":
                return kC[:, h % 2, s]
            return kD[0:MLA, h, s]

        def head_v(kind, block_, h):
            if kind == "A":
                return vA[:, block_, (h // 4) * HD:(h // 4 + 1) * HD]
            if kind == "C":
                return vC[:, block_, :]
            return (vB if kind == "B" else vD)[:, block_, h * HD:(h + 1) * HD]


        scores_done, biased, shifted, probs_done = sem("scores_done"), sem("biased"), sem("shifted"), sem("probs_done")
        probsT_done, probsT_ready, out_done = sem("probsT_done"), sem("probsT_ready"), sem("out_done")
        out_ready, outT_done, outT_ready = sem("out_ready"), sem("outT_done"), sem("outT_ready")
        gathered = [sem("gathered0"), sem("gathered1")]
        xgT_done, xgT_ready = sem("xgT_done"), sem("xgT_ready")
        gate_up_done, silu_ready, h_ready = sem("gate_up_done"), sem("silu_ready"), sem("h_ready")
        hT_done, hT_ready, y_done = sem("hT_done"), sem("hT_ready"), sem("y_done")
        y_ready = sem("y_ready")
        y_stored = [sem("y_stored0"), sem("y_stored1")]
        rows_gathered = [sem(f"rows_gathered{n}") for n in range(NT)]
        idx_cleared, idx_loaded, x_stored = sem("idx_cleared"), sem("idx_loaded"), sem("x_stored")
        pT_loaded, rows_loaded, ids_loaded = sem("pT_loaded"), sem("rows_loaded"), sem("ids_loaded")
        val_scaled = sem("val_scaled")
        keys_cleared = sem("keys_cleared")
        listed = sem("listed")
        M = {n: sem(n) for n in (
            "ws_masked", "conv_done", "gates_mm", "r_ready", "i_ready", "decay_ready", "decay_exp", "mult_in", "mult_ready",
            "spatial_mm", "vn_ready", "yA_ready", "yA_mm", "pooled", "yD_mm", "var_ready", "sd_ready",
            "lam_exp", "lb_in", "lb_exp", "hg_gate", "hg_log", "hg_decays", "hg_exp", "hg_exps", "hg_kT_mm",
            "hg_kT", "hg_v_spread", "hg_state_mm", "hg_state_in", "hg_state", "hg_inter_mm", "hg_diff", "hg_decay",
            "hg_att", "hg_att_mm", "hg_used", "hg_square", "hg_mean_mm", "hg_mean", "hg_sd", "hg_decay_rows")}
        squares = Area(10240).take(NT, 384)
        odd_sq, odd_var = sem("odd_sq"), sem("odd_var")
        relu_used = sem("relu_used")
        flags, before_, step_k, hits = (Area(2048 + 512 * i).take(3, E) for i in range(4))
        picked_e, e_list, ranked = Area(4096).take(8, 3 * E), Area(4500).take(8), Area(4600).take(NT, E)
        ai = Area(12288)
        relu_d, score = ai.take(3, T), {n: ai.take((n + 1) * P) for n in range(1, NT)}
        am = Area(mixers_at)
        xc, pooled, log_decay, gate_i, decay, tanh_d = (am.take(2, T) for _ in range(6))
        sums0, sums1 = tanh_d, decay
        state = Area().take(HD, NC)
        ah = Area(zC_end)
        bb, qe, ke, decay_c = ah.take(T), ah.take(T), ah.take(T), ah.take(NC)
        keT, vT, v_spread = ah.take(NT, P), ah.take(NT, P), ah.take(2, P // HC, HD)
        decay_rows = v_spread.rearrange("p h c v -> p (h c v)")
        pairs = [ah.take(1024), ah.take(1024)]
        log_f, to_end = pairs[0][:, 0:T], pairs[0][:, T:2 * T]
        exp_b, exp_end = pairs[1][:, 0:T], pairs[1][:, T:2 * T]
        o_sq = qe
        LATENT = "v" + "av" * 8 + "a" * 8 + "v" * 4
        cum, soft = probsT[:, 0, :], logits[:, 0:2, :]
        fg_w = operand["fg_w"].rearrange("p (k h) -> p k h", k=KD)
        pick = operand["pick"].rearrange("p (h q) -> p h q", h=8)
        router_w = operand["router_w"].rearrange("p (k e) -> p k e", k=KD)
        ar = Area()
        aff, sel, chosen, first, second, tmp16, posn = (ar.take(NT, E) for _ in range(7))
        rank, trank = ar.take(NT, E), ar.take(NT, 4)
        gsum, gpick, cmp, wsum, r_place, total = ar.take(NT, 4), ar.take(NT, 4), ar.take(NT, 16), ar.take(NT), ar.take(2, NT), ar.take(E)
        idx_zero = sb("idx_zero", [P, SLOTS + 1], U32)
        y_zero = Area(SCRATCH - D).take(D)
        ea = Area()
        xg, y_sb = ea.take(2, D), ea.take(2, D)
        xgT, silu_g, hid, hidT = ea.take(KD, P), ea.take(EF), ea.take(EF), ea.take(4, P)
        idx_sb = sb("idx_sb", [P, SLOTS + 1], U32)
        idx_one = sb("idx_one", [P, 1], U32)
        over_w = ea.take(2, SLOT)
        y_cleared = sem("y_cleared")
        over = {n: sem(f"over_{n}") for n in ("idx", "in", "xT_mm", "xT", "gate_up_mm", "silu", "h", "hT_mm", "hT", "down_in",
                                              "y_mm", "y", "stored", "passed", "all_stored")}
        block = ctx.enter_context(nc.Block())

        @block.tensor
        def _(pe):
            meets = [0]

            def meet():
                meets[0] += 1
                pe.drain().then_inc(met, 1)
                pe.wait_ge(met, 4 * meets[0])
                pe.drain()

            def arrived(at):
                pe.wait_ge(w_loaded[at % RING], 16 * (at // RING + 1))

            def bank_emptied(f, plan, k):
                if k >= 8:
                    who, n = others(plan, k)
                    pe.wait_ge(f.a if who == "a" else f.v, n)

            def product(out_, pairs):
                for j, (lhsT, rhs) in enumerate(pairs):
                    mm = nc.tensor.matmul(out_, lhsT, rhs, start=(j == 0), stop=(j == len(pairs) - 1))
                return mm

            def flip(f, src, ready_v, n_tiles=KD):
                for k in range(n_tiles):
                    for n in range(NT):
                        if k == 0:
                            pe.wait_ge(f.v, ready_v + n)
                        mm = nc.tensor.transpose(banks[k][:, n * P:(n + 1) * P], src[:, n, k * P:(k + 1) * P], ident)
                    mm.then_inc(f.mm, 1)

            def norm(name):
                flip(F[name], normed, 1)

            def norm1():
                pe.wait_ge(pack_loaded["base"], 16)
                norm("norm1")

            def tokens(f, plan, k, at, c, n, c0, c1):
                w_ = slot_view(at, c)
                bank_emptied(f, plan, k)
                product(banks[k % 8][:, 0:c1 - c0],
                        [(xT[:, t, n * P:(n + 1) * P], w_[:, t, c0:c1]) for t in range(KD)]).then_inc(f.mm, 1)

            def features(f, plan, k, at, c, c0, m=P):
                w_ = slot_view(at, c)
                bank_emptied(f, plan, k)
                product(banks[k % 8][0:m, :],
                        [(w_[:, t, c0:c0 + m], xT[:, t, :]) for t in range(KD)]).then_inc(f.mm, 1)

            def project():
                f, k = F["project"], 0
                for j, (at, c) in enumerate(by_name["w_in"]):
                    arrived(at)
                    for g in range(2 if j == 4 else 4):
                        if j == 0:
                            tokens(f, PROJECT, k, at, c, g, 0, 512)
                        else:
                            features(f, PROJECT, k, at, c, g * P)
                        k += 1
                    release(f.mm, k)

            def release(done, value):
                pe.wait_ge(done, value)
                pe.sem_inc(w_used, 1)

            def mixers():
                pe.wait_ge(M["conv_done"], 2)
                for g, name in enumerate(("wa", "wx")):
                    for t in range(2):
                        nc.tensor.matmul(banks[2 * g + t][:, :], operand[name][:, t * P:(t + 1) * P], xc[:, t, :],
                                         start=True, stop=True).then_inc(M["gates_mm"], 1)
                pe.wait_ge(M["pooled"], 2)
                pe.wait_ge(M["i_ready"], 2)
                for t in range(2):
                    nc.tensor.matmul(banks[2 + t][:, :], operand["dw"][:, t * P:(t + 1) * P], pooled[:, t, :],
                                     start=True, stop=True).then_inc(M["yD_mm"], 1)
                pe.wait_ge(M["ws_masked"], 1)
                for n in range(NT):
                    pe.wait_ge(M["vn_ready"], n + 1)
                    for h in range(4):
                        mm = nc.tensor.matmul(banks[4 + n][:, h * HD:(h + 1) * HD], operand["ws"][:, h * P:(h + 1) * P],
                                              zA[:, n, 256 + h * HD:256 + (h + 1) * HD], start=True, stop=True)
                    mm.then_inc(M["spatial_mm"], 1)
                pe.wait_ge(M["r_ready"], 2)
                for t in range(2):
                    for n in range(NT):
                        pe.wait_ge(M["yA_ready"], n + 1)
                        mm = nc.tensor.transpose(banks[t][:, n * P:(n + 1) * P], zA[:, n, t * P:(t + 1) * P], ident)
                    mm.then_inc(M["yA_mm"], 1)

            def hgrn():
                for pr in range(2):
                    pe.wait_ge(M["hg_exps"], pr + 1)
                    if pr:
                        pe.wait_ge(M["hg_mean"], pr)
                    for n in range(NT):
                        mm = nc.tensor.transpose(banks[0][:, n * P:(n + 1) * P], ke[:, n * P:(n + 1) * P], ident)
                    mm.then_inc(M["hg_kT_mm"], 1)
                    for n in range(NT):
                        mm = nc.tensor.transpose(banks[1][:, n * P:(n + 1) * P], zC[:, 4 + pr, n * P:(n + 1) * P], ident)
                    mm.then_inc(M["hg_kT_mm"], 1)
                    pe.wait_ge(M["hg_kT"], 2 * pr + 1)
                    for n in range(NT + 1):
                        if n == 1:
                            pe.wait_ge(M["hg_kT"], 2 * pr + 2)
                        if 2 <= n < NT:
                            pe.wait_ge(M["hg_state_in"], 2 * (NT * pr + n - 1))
                        for hh in range(2 if n < NT else 0):
                            pe.wait_ge(M["hg_v_spread"], 2 * (NT * pr + n) + hh + 1)
                            for half_ in range(2):
                                mm = nc.tensor.matmul(
                                    banks[(2 + 2 * n + half_) % 4][hh * HD:(hh + 1) * HD, :],
                                    keT[:, n, hh * HD:(hh + 1) * HD],
                                    v_spread[:, hh, half_ * 8:half_ * 8 + 8, :], start=True, stop=True)
                            mm.then_inc(M["hg_state_mm"], 1)
                        if n == 0:
                            continue
                        k = NT * pr + n - 1
                        pe.wait_ge(M["hg_att"], k + 1)
                        if k >= 2:
                            pe.wait_ge(M["hg_used"], k - 1)
                        for b in range(2):
                            mm = nc.tensor.matmul(banks[4 + 2 * (k % 2) + b][:, :], operand["half"],
                                                  pairs[k % 2][:, b * 512:(b + 1) * 512], start=True, stop=True)
                        mm.then_inc(M["hg_att_mm"], 1)
                    pe.wait_ge(M["hg_state"], 2 * pr + 2)
                    for c in range(NC):
                        for hh in range(2):
                            r = slice(hh * HD, (hh + 1) * HD)
                            mm = nc.tensor.matmul(banks[1 + hh][r, c * HC:(c + 1) * HC], state[r, :, c],
                                                  qe[r, c * HC:(c + 1) * HC], start=True, stop=True)
                    mm.then_inc(M["hg_inter_mm"], 1)
                    pe.wait_ge(M["hg_square"], pr + 1)
                    nc.tensor.matmul(banks[0][:, :], operand["halfmean"], o_sq, start=True, stop=True)\
                        .then_inc(M["hg_mean_mm"], 1)

            def halves(name, chunk_name, lhs, plan):
                f = F[name]
                for half_, (at, c) in enumerate(by_name[chunk_name]):
                    arrived(at)
                    w_ = slot_view(at, c)
                    for n in range(NT):
                        k = NT * half_ + n
                        product(banks[k][:, :], [(lhs[:, t, n * P:(n + 1) * P], w_[:, t, :]) for t in range(KD)])\
                            .then_inc(f.mm, 1)
                    release(f.mm, NT * (half_ + 1))

            def mix_out():
                halves("mix_out", "w_out", mixT, "v" * 8)

            def up():
                f = F["up"]
                for j, (at, c) in enumerate(by_name["w_up"]):
                    arrived(at)
                    w_ = slot_view(at, c)
                    for g in range(4):
                        k = 4 * j + g
                        if k >= 8:
                            pe.wait_ge(f.v, k - 7)
                        product(banks[k % 8][:, :], [(w_[:, t, g * P:(g + 1) * P], xT[:, t, :]) for t in range(KD)])\
                            .then_inc(f.mm, 1)
                    release(f.mm, 4 * j + 4)

            def down():
                f = F["down"]
                for j, (at, c) in enumerate(by_name["w_down"]):
                    arrived(at)
                    w_ = slot_view(at, c)
                    half_, k0 = j // 3, c[1]
                    for n in range(NT):
                        for t in range(c[2]):
                            mm = nc.tensor.matmul(banks[4 * half_ + n][:, :], hidden[:, k0 + t, n * P:(n + 1) * P],
                                                  w_[:, t, :], start=(k0 + t == 0), stop=(k0 + t == FT - 1))
                        mm.then_inc(f.mm, 1)
                    release(f.mm, NT * (j + 1))

            def gate():
                f = F["gate"]
                (at_e, c_e), = by_name["w_pe"]
                arrived(at_e)
                pe.wait_ge(pT_loaded, 16)
                w_e = slot_view(at_e, c_e)
                for half_, (at, c) in enumerate(by_name["w_pg"]):
                    arrived(at)
                    w_g = slot_view(at, c)
                    for n in range(NT):
                        k = 2 * (NT * half_ + n)
                        bank_emptied(f, "va" * 8, k)
                        product(banks[k % 8][:, :], [(pT[:, t, n * P:(n + 1) * P],
                                                      w_e[:, t, half_ * 512:(half_ + 1) * 512]) for t in range(2)])\
                            .then_inc(f.mm, 1)
                        bank_emptied(f, "va" * 8, k + 1)
                        product(banks[(k + 1) % 8][:, :], [(xT[:, t, n * P:(n + 1) * P], w_g[:, t, :]) for t in range(KD)])\
                            .then_inc(f.mm, 1)
                    if half_ == 1:
                        release(f.mm, 16)
                    release(f.mm, 8 * (half_ + 1))

            def final_norm():
                flip(F["final_norm"], x, 1)

            def even_in():
                f, k = F["even_in"], 0
                pe.wait_ge(pack_loaded["even"], 16)
                for j, (at, c) in enumerate(by_name["even_w_in_2"]):
                    arrived(at)
                    if j == 1:
                        features(f, EVEN_IN, k, at, c, 0)
                        k += 1
                    for g in range(4):
                        if j == 1:
                            tokens(f, EVEN_IN, k, at, c, g, P, 2 * P)
                        elif j == 4:
                            tokens(f, EVEN_IN, k, at, c, g, 0, 512)
                        else:
                            features(f, EVEN_IN, k, at, c, g * P)
                        k += 1
                    release(f.mm, k)
                bank_emptied(f, EVEN_IN, k)
                product(banks[k % 8][0:8, :], [(fg_w[:, t, :], xT[:, t, :]) for t in range(KD)]).then_inc(f.mm, 1)
                pe.wait_ge(f.s, 3)
                for n in range(NT):
                    mm = nc.tensor.transpose(banks[(k + 1) % 8][:, n * 8:(n + 1) * 8], cum[0:8, n * P:(n + 1) * P],
                                             ident[0:8, 0:8])
                mm.then_inc(f.mm, 1)

            def attend(stage):
                kind = KIND[stage]
                base = 32 * list(KIND).index(stage)

                def score(i):
                    n, h = UNITS[i]
                    u = base + i
                    if u >= 2:
                        pe.wait_ge(biased, u - 1)
                    out_ = banks[u % 2][:, 0:span(kind, n)[1]]
                    if kind == "B":
                        nc.tensor.matmul(out_, head_q(kind, n, h), head_k(kind, n, h), start=True, stop=False)
                        mm = nc.tensor.matmul(out_, pick[:, h, :], negc[:, 0:span(kind, n)[1]],
                                              start=False, stop=True)
                    else:
                        mm = nc.tensor.matmul(out_, head_q(kind, n, h), head_k(kind, n, h), start=True, stop=True)
                    mm.then_inc(scores_done, 1)

                def turn_probs(i):
                    n, h = UNITS[i]
                    u = base + i
                    pe.wait_ge(probs_done, u + 1)
                    if u >= 2:
                        pe.wait_ge(probsT_ready, u - 1)
                    for b in range(span(kind, n)[1] // P):
                        mm = nc.tensor.transpose(banks[2 + u % 2][:, b * P:(b + 1) * P],
                                                 logits[:, u % 2, b * P:(b + 1) * P], ident)
                    mm.then_inc(probsT_done, 1)

                def weigh(i):
                    n, h = UNITS[i]
                    u = base + i
                    s0, w_ = span(kind, n)
                    pe.wait_ge(probsT_ready, u + 1)
                    if u >= 2:
                        pe.wait_ge(out_ready, u - 1)
                    for b in range(w_ // P):
                        mm = nc.tensor.matmul(banks[4 + u % 2][:, 0:HD], probsT[:, u % 2, b * P:(b + 1) * P],
                                              head_v(kind, s0 // P + b, h), start=(b == 0), stop=(b == w_ // P - 1))
                    mm.then_inc(out_done, 1)

                def turn_out(n):
                    g = base // 8 + n
                    pe.wait_ge(out_ready, base + 8 * (n + 1))
                    if g >= 2:
                        pe.wait_ge(outT_ready, g - 1)
                    for t in range(4):
                        mm = nc.tensor.transpose(banks[6 + g % 2][:, t * P:(t + 1) * P],
                                                 heads_out[:, g % 2, t * P:(t + 1) * P], ident)
                    mm.then_inc(outT_done, 1)

                for i in range(len(UNITS) + 4):
                    if i < len(UNITS):
                        score(i)
                    if 1 <= i <= len(UNITS):
                        turn_probs(i - 1)
                    if 2 <= i < len(UNITS) + 2:
                        weigh(i - 2)
                    if i >= 11 and (i - 11) % 8 == 0:
                        turn_out((i - 11) // 8)

            def even_out():
                halves("even_out", "w_o_even", mixT, "v" * 8)
                flip(F["even_out"], x, 9)

            def odd_out():
                halves("odd_out", "w_o_odd", mixT, "v" * 8)
                flip(F["odd_out"], x, 9)

            def route(l):
                f = F[f"route{l}"]
                for n in range(NT):
                    mm = product(banks[0][:, n * E:(n + 1) * E],
                                 [(xT[:, t, n * P:(n + 1) * P], router_w[:, t, :]) for t in range(KD)])
                mm.then_inc(f.mm, 1)
                pe.wait_ge(f.v, 1)
                for n in range(NT):
                    mm = product(banks[1][:, n * E:(n + 1) * E],
                                 [(operand["before"] if m == n else operand["ones"], chosen[:, m, :]) for m in range(n + 1)])
                mm = product(banks[1][:, NT * E:(NT + 1) * E], [(operand["ones"], chosen[:, m, :]) for m in range(NT)])
                mm.then_inc(f.mm, 1)

            def turn_x(b, landed_):
                pe.wait_ge(gathered[b], landed_)
                for g in range(2):
                    for t in range(4):
                        mm = nc.tensor.transpose(banks[g][:, t * P:(t + 1) * P],
                                                 xg[:, b, (4 * g + t) * P:(4 * g + t + 1) * P], ident)
                    mm.then_inc(xgT_done, 1)

            def weight_view(at, k):
                return ring[:, at % RING, :].rearrange("p (k n) -> p k n", k=k)

            def enter(l, e, at, loads, b, next_landed):
                pe.wait_ge(xgT_ready, 2 * e + 2 + 2 * l)
                for j in range(2):
                    pe.wait_ge(w_loaded[(at + j) % RING], loads + 16 * ((at + j) // RING))
                    w_ = weight_view(at + j, KD)
                    product(banks[2 + j][:, :], [(xgT[:, t, :], w_[:, t, :]) for t in range(KD)])\
                        .then_inc(gate_up_done, 1)
                turn_x(1 - b, next_landed)
                for j in range(2):
                    pe.wait_ge(gate_up_done, 2 * e + 1 + j)
                    pe.sem_inc(w_used, 1)

            def leave(e, at, loads):
                pe.wait_ge(hT_ready, e + 1)
                pe.wait_ge(w_loaded[at % RING], loads + 16 * (at // RING))
                w_ = weight_view(at, 4)
                for j in range(2):
                    pe.wait_ge(y_ready, 2 * e + 1 + j)
                    product(banks[5 + j][:, :], [(hidT[:, t, :], w_[:, t, j * 512:(j + 1) * 512]) for t in range(4)])\
                        .then_inc(y_done, 1)

            def turn_h(e):
                pe.wait_ge(h_ready, e + 1)
                for t in range(4):
                    mm = nc.tensor.transpose(banks[4][:, t * P:(t + 1) * P], hid[:, t * P:(t + 1) * P], ident)
                mm.then_inc(hT_done, 1)

            def experts(l):
                c0 = first_expert_chunk[l]
                turn_x(0, 16 * (9 * l + 1))
                enter(l, E * l, c0, 16, 0, 16 * (8 * l + 1))
                turn_h(E * l)
                with pe.Fori(0, E // 2 - 1) as it:
                    for b in range(2):
                        e = it * 2 + (E * l + b + 1)
                        at = c0 + 3 * b + 2
                        enter(l, e, at, it * 16 + 16, 1 - b, it * 16 + (16 * (9 * l + 2) if b == 0 else 16 * (8 * l + 2)))
                        leave(e - 1, at + 2, it * 16 + 16)
                        turn_h(e)
                        release(y_done, 2 * e)
                e = E * (l + 1) - 1
                at = c0 + 3 * (E - 1) - 1
                enter(l, e, at, 16, 1, 16 * (9 * l + 9))
                leave(e - 1, at + 2, 16)
                turn_h(e)
                release(y_done, 2 * e)
                leave(e, at + 3, 16)
                release(y_done, 2 * e + 2)

            def overflow(l):
                n, done = slots_of(pe, l)
                gate_w, up_w = (over_w[:, i, :].rearrange("p (k n) -> p k n", k=KD) for i in range(2))
                down_w = over_w[:, 0, :].rearrange("p (k n) -> p k n", k=4)
                with pe.If(n > 0):
                    with pe.Fori(0, n) as slot:
                        j = slot + done
                        pe.wait_ge(over["in"], j * 48 + 48)
                        for g in range(2):
                            for t in range(4):
                                mm = nc.tensor.transpose(banks[g][:, t * P:(t + 1) * P],
                                                         xg[:, 0, (4 * g + t) * P:(4 * g + t + 1) * P], ident)
                            mm.then_inc(over["xT_mm"], 1)
                        pe.wait_ge(over["xT"], j * 2 + 2)
                        for i, w_ in enumerate((gate_w, up_w)):
                            product(banks[2 + i][:, :], [(xgT[:, t, :], w_[:, t, :]) for t in range(KD)])\
                                .then_inc(over["gate_up_mm"], 1)
                        pe.wait_ge(over["h"], j + 1)
                        for t in range(4):
                            mm = nc.tensor.transpose(banks[4][:, t * P:(t + 1) * P], hid[:, t * P:(t + 1) * P], ident)
                        mm.then_inc(over["hT_mm"], 1)
                        pe.wait_ge(over["hT"], j + 1)
                        pe.wait_ge(over["down_in"], j * 16 + 16)
                        for i in range(2):
                            product(banks[5 + i][:, :], [(hidT[:, t, :], down_w[:, t, i * 512:(i + 1) * 512])
                                                         for t in range(4)]).then_inc(over["y_mm"], 1)

            def combine(l):
                if l == 0:
                    flip(F["combine0"], x, 1)

            def odd_in():
                f, k = F["odd_in"], 0
                (a0, c0), (a1_, c1), (a2, c2) = by_name["odd_w_in_2"]
                pe.wait_ge(pack_loaded["odd"], 16)
                arrived(a0)
                features(f, ODD_IN, 0, a0, c0, 384, HD)
                features(f, ODD_IN, 1, a0, c0, P)
                features(f, ODD_IN, 2, a0, c0, 2 * P)
                features(f, ODD_IN, 3, a0, c0, 0, HD)
                for n in range(NT):
                    tokens(f, ODD_IN, 4 + n, a0, c0, n, HD, 2 * HD)
                for n in range(NT):
                    tokens(f, ODD_IN, 8 + n, a0, c0, n, 448, 452)
                release(f.mm, 12)
                pe.wait_ge(f.v, 3)
                pe.wait_ge(keys_cleared, 2)
                k = 12
                for n, h in INDEX:
                    bank_emptied(f, ODD_IN, k)
                    nc.tensor.matmul(banks[k % 8][:, 0:(n + 1) * P], qI[:, h // 2, n * P:(n + 1) * P],
                                     kI[:, h % 2, 0:(n + 1) * P], start=True, stop=True).then_inc(f.mm, 1)
                    k += 1
                arrived(a1_)
                for g in range(4):
                    features(f, ODD_IN, k, a1_, c1, g * P)
                    k += 1
                release(f.mm, k)
                arrived(a2)
                for n in range(NT):
                    tokens(f, ODD_IN, k, a2, c2, n, 0, 384)
                    k += 1
                features(f, ODD_IN, k, a2, c2, 320, MLA)
                k += 1
                release(f.mm, k)
                for t in range(3):
                    bank_emptied(f, ODD_IN + "vvv", k + t)
                    for n in range(NT):
                        pe.wait_ge(f.s, n + 1)
                        mm = nc.tensor.transpose(banks[(k + t) % 8][:, n * P:(n + 1) * P],
                                                 cqkv[:, n, t * P:(t + 1) * P], ident)
                    mm.then_inc(f.mm, 1)

            def latent():
                f = F["latent"]
                (aq, cq_), = by_name["odd_w_uq_2"]
                (akv, ckv_), = by_name["odd_w_ukv_2"]
                uq, ukv = slot_view(aq, cq_), slot_view(akv, ckv_)
                turn = operand["turn"][0:MLA, :]
                nc.tensor.matmul(banks[0][0:MLA, :], turn, krT[0:MLA, :], start=True, stop=True).then_inc(f.mm, 1)
                arrived(aq)
                k = 1
                for h in range(8):
                    bank_emptied(f, LATENT, k)
                    product(banks[k % 8][0:MLA, :], [(uq[:, t, h * MLA:(h + 1) * MLA], cqT[:, t, :]) for t in range(2)])\
                        .then_inc(f.mm, 1)
                    bank_emptied(f, LATENT, k + 1)
                    pe.wait_ge(f.a, h + 1)
                    nc.tensor.matmul(banks[(k + 1) % 8][0:MLA, :], turn, raw[0:MLA, h % 2, :], start=True, stop=True)\
                        .then_inc(f.mm, 1)
                    k += 2
                release(f.mm, k)
                arrived(akv)
                for h in range(8):
                    bank_emptied(f, LATENT, k)
                    nc.tensor.matmul(banks[k % 8][0:HD, :], ukv[:, 0, h * P:h * P + HD], ckvT, start=True, stop=True)\
                        .then_inc(f.mm, 1)
                    k += 1
                v_cols = ukv[:, 0, :].rearrange("p (h d) -> p h d", h=8)[:, :, HD:P]
                for n in range(NT):
                    bank_emptied(f, LATENT, k)
                    nc.tensor.matmul(banks[k % 8][:, :], ckvT[:, n * P:(n + 1) * P], v_cols, start=True, stop=True)\
                        .then_inc(f.mm, 1)
                    k += 1
                release(f.mm, k)

            run = {
                "norm1": norm1, "project": project, "mixers": mixers, "hgrn": hgrn, "mix_out": mix_out,
                "norm2": lambda: norm("norm2"), "up": up, "down": down, "norm3": lambda: norm("norm3"),
                "gate": gate, "final_norm": final_norm, "even_in": even_in,
                "even_a": lambda: attend("even_a"), "even_b": lambda: attend("even_b"), "even_out": even_out,
                "route0": lambda: route(0), "experts0": lambda: experts(0), "combine0": lambda: combine(0),
                "odd_in": odd_in, "odd_c": lambda: attend("odd_c"), "latent": latent,
                "odd_d": lambda: attend("odd_d"), "odd_out": odd_out,
                "overflow0": lambda: overflow(0), "overflow1": lambda: overflow(1), "route1": lambda: route(1), "experts1": lambda: experts(1), "combine1": lambda: combine(1),
            }
            for s in stages:
                if s in run:
                    run[s]()
                meet()

        @block.scalar
        def _(act):
            meets = [0]
            steps = [0]

            def meet():
                meets[0] += 1
                act.drain().then_inc(met, 1)
                act.wait_ge(met, 4 * meets[0])
                act.drain()

            def step(ins):
                ins.then_inc(act_step, 1)
                steps[0] += 1
                act.wait_ge(act_step, steps[0])

            A = nc.scalar.activation

            def scaled(out_, in_, s):
                return A(out_, in_, ACT.Identity, scale=s) if s is not None else A(out_, in_, ACT.Copy)

            def unflip(f, mm0, g=None):
                for k in range(0, KD, 2):
                    act.wait_ge(f.mm, mm0 + k + 1)
                    scaled(xT[:, k, :], banks[k][:, :], g[:, k:k + 1] if g is not None else None).then_inc(f.a, 1)

            def root(f, n_s, col):
                act.wait_ge(f.s, n_s)
                A(rstd, col, ACT.Sqrt).then_inc(f.a, 1)

            def norm(name, g):
                f = F[name]
                if name == "norm1":
                    act.wait_ge(x_loaded, 16)
                for n in range(NT):
                    A(normed[:, n, :], x[:, n, :], ACT.Square, accum_out=sumsq[:, n:n + 1]).then_inc(f.a, 1)
                root(f, 1, rstd)
                if name == "norm1":
                    act.wait_ge(pack_loaded["one"], 16)
                unflip(f, 0, g)

            def evacuate(f, plan, jobs):
                for k, who in enumerate(plan):
                    if who == "a":
                        act.wait_ge(f.mm, k + 1)
                        ins = None
                        for out_, in_, func, s in jobs(k, banks[k % 8]):
                            ins = A(out_, in_, func, scale=s) if s is not None else A(out_, in_, func)
                        ins.then_inc(f.a, 1)

            def project():
                def jobs(k, bank):
                    if k < 4:
                        return [(zA[:, k, :], bank[:, :], ACT.Gelu_apprx_tanh, None)]
                    if k < 8:
                        return [(zB[:, k - 4, :], bank[:, :], ACT.Gelu_apprx_tanh, None)]
                    if k < 12:
                        return [(zC[:, k - 8, :], bank[:, :], ACT.Silu if k < 10 else ACT.Sigmoid, None)]
                    return [(zC[:, k - 8, :], bank[:, :], ACT.Silu, None)]
                evacuate(F["project"], PROJECT, jobs)

            def mixers():
                step(A(lam_e, operand["lam"], ACT.Abs))
                A(lam_e, lam_e, ACT.Exp, scale=-1.0).then_inc(M["lam_exp"], 1)
                act.wait_ge(M["lb_in"], 1)
                A(lb0, lb0, ACT.Exp).then_inc(M["lb_exp"], 1)
                act.wait_ge(M["gates_mm"], 4)
                for t in range(2):
                    A(log_decay[:, t, :], banks[t][:, :], ACT.Sigmoid, bias=operand["ba"][:, t:t + 1]).then_inc(M["r_ready"], 1)
                for t in range(2):
                    A(gate_i[:, t, :], banks[2 + t][:, :], ACT.Sigmoid, bias=operand["bx"][:, t:t + 1]).then_inc(M["i_ready"], 1)
                act.wait_ge(M["var_ready"], 1)
                A(rstd, rstd, ACT.Sqrt).then_inc(M["sd_ready"], 1)
                act.wait_ge(M["decay_ready"], 2)
                for t in range(2):
                    A(decay[:, t, :], log_decay[:, t, :], ACT.Exp)
                    A(tanh_d[:, t, :], log_decay[:, t, :], ACT.Tanh).then_inc(M["decay_exp"], 1)
                for t in range(2):
                    act.wait_ge(M["mult_in"], t + 1)
                    A(tanh_d[:, t, :], tanh_d[:, t, :], ACT.Sqrt, scale=-1.0).then_inc(M["mult_ready"], 1)
                for t in range(2):
                    act.wait_ge(M["yD_mm"], t + 1)
                    scaled(mixT[:, 6 + t, :], banks[2 + t][:, :], operand["dscale"][:, t:t + 1])
                for t in range(2):
                    act.wait_ge(M["yA_mm"], t + 1)
                    scaled(mixT[:, t, :], banks[t][:, :], None)

            def hgrn():
                for pr in range(2):
                    act.wait_ge(M["hg_gate"], pr + 1)
                    A(log_f, zC[:, 2 + pr, :], ACT.Ln).then_inc(M["hg_log"], 1)
                    act.wait_ge(M["hg_decays"], pr + 1)
                    A(exp_b, bb, ACT.Exp).then_inc(M["hg_exp"], 1)
                    A(exp_end, to_end, ACT.Exp).then_inc(M["hg_exp"], 1)
                    A(decay_c[:, 1:NC], bb[:, HC - 1:T - 1:HC], ACT.Exp).then_inc(M["hg_exp"], 1)
                    act.wait_ge(M["hg_kT_mm"], 2 * pr + 2)
                    scaled(keT.rearrange("p a b -> p (a b)"), banks[0][:, :], None).then_inc(M["hg_kT"], 1)
                    scaled(vT.rearrange("p a b -> p (a b)"), banks[1][:, :], None).then_inc(M["hg_kT"], 1)
                    def decay_of(qt):
                        act.wait_ge(M["hg_diff"], NT * pr + qt + 1)
                        A(pairs[qt % 2], pairs[qt % 2], ACT.Exp).then_inc(M["hg_decay"], 1)

                    decay_of(0)
                    decay_of(1)
                    for n in range(NT):
                        act.wait_ge(M["hg_state_mm"], 2 * (NT * pr + n) + 2)
                        for i in (2 * n, 2 * n + 1):
                            m = 8 if i < 7 else 7
                            c0 = 8 * i + 1
                            scaled(state[:, :, c0:c0 + m],
                                   banks[(2 + i) % 4][:, 0:m * HD].rearrange("p (c v) -> p v c", v=HD), None)\
                                .then_inc(M["hg_state_in"], 1)
                        if n in (1, 2):
                            decay_of(n + 1)
                    A(decay_rows.rearrange("p (v c) -> p v c", c=NC), decay_c.unsqueeze(1).to_broadcast([P, HD // 2, NC]),
                      ACT.Copy).then_inc(M["hg_decay_rows"], 1)
                    act.wait_ge(M["hg_mean"], pr + 1)
                    A(exp_b, exp_b, ACT.Sqrt).then_inc(M["hg_sd"], 1)

            def up():
                f = F["up"]
                w3 = operand["fconv_w"].rearrange("p (f t) -> p f t", t=3)
                for k in range(2 * FT + 1):
                    if k < 2 * FT:
                        act.wait_ge(f.mm, k + 1)
                        if 4 <= k < FT + 4:
                            act.wait_ge(f.s, k - 3)
                        if k - 4 >= FT:
                            act.wait_ge(val_scaled, k - 4 - FT + 1)
                        A(conv[:, k % 4, :], banks[k % 8][:, :], ACT.Identity, bias=operand["fconv_b"][:, k:k + 1],
                          scale=w3[:, k, 2:3]).then_inc(f.a, 1)
                    if 1 <= k <= FT:
                        act.wait_ge(f.v, k)
                        A(hidden[:, k - 1, :], conv[:, (k - 1) % 4, :], ACT.Gelu_apprx_tanh).then_inc(f.s, 1)

            def gate():
                f = F["gate"]
                for i in range(8):
                    act.wait_ge(f.mm, 2 * i + 2)
                    if i >= 2:
                        act.wait_ge(f.v, i - 1)
                    A(gate_s[:, i % 2, :], banks[(2 * i + 1) % 8][:, :], ACT.Sigmoid).then_inc(f.a, 1)

            def final_norm():
                norm("final_norm", None)

            def even_in():
                def jobs(k, bank):
                    if k < 4:
                        return [(qA[(h // 4) * HD:(h // 4 + 1) * HD, h % 4, :], bank[(h % 2) * HD:(h % 2 + 1) * HD, :],
                                 ACT.Copy, HD ** -0.5) for h in (2 * k, 2 * k + 1)]
                    if k < 9:
                        return [(vA[:, k - 5, :], bank[:, 0:P], ACT.Copy, None)]
                    return [(kB[r, 2 * (k - 13) + hh, :], bank[r, :], ACT.Copy, None)
                            for hh, r in enumerate((slice(0, HD), slice(HD, P)))]
                f = F["even_in"]
                evacuate(f, EVEN_IN, jobs)
                act.wait_ge(f.s, 1)
                step(A(soft[0:8, 1, :], soft[0:8, 0, :], ACT.Abs))
                step(A(soft[0:8, 1, :], soft[0:8, 1, :], ACT.Exp, scale=-1.0))
                A(soft[0:8, 1, :], soft[0:8, 1, :], ACT.Ln, bias=1.0).then_inc(f.a, 1)

            def attend(stage):
                kind = KIND[stage]
                base = 32 * list(KIND).index(stage)

                def soft_max(i):
                    n, h = UNITS[i]
                    u = base + i
                    w_ = span(kind, n)[1]
                    act.wait_ge(shifted, u + 1)
                    if kind == "A":
                        A(sinkexp[:, u % 4:u % 4 + 1], operand["sinks"][:, h:h + 1], ACT.Exp, bias=negmax[:, u % 4:u % 4 + 1])
                    A(logits[:, u % 2, 0:w_], logits[:, u % 2, 0:w_], ACT.Exp, bias=negmax[:, u % 4:u % 4 + 1],
                      accum_out=rowsum[:, u % 4:u % 4 + 1]).then_inc(probs_done, 1)

                def take_probs(i):
                    n, h = UNITS[i]
                    u = base + i
                    w_ = span(kind, n)[1]
                    act.wait_ge(probsT_done, u + 1)
                    if u >= 2:
                        act.wait_ge(out_done, u - 1)
                    A(probsT[:, u % 2, 0:w_], banks[2 + u % 2][:, 0:w_], ACT.Copy).then_inc(probsT_ready, 1)

                def take_out(n):
                    g = base // 8 + n
                    act.wait_ge(outT_done, g + 1)
                    t0 = 0 if kind in "AC" else 4
                    A(mixT[:, t0:t0 + 4, n * P:(n + 1) * P], banks[6 + g % 2][:, :].rearrange("p (t q) -> p t q", t=4),
                      ACT.Copy).then_inc(outT_ready, 1)

                for i in range(len(UNITS) + 4):
                    if i < len(UNITS):
                        soft_max(i)
                    if 1 <= i <= len(UNITS):
                        take_probs(i - 1)
                    if i >= 11 and (i - 11) % 8 == 0:
                        take_out((i - 11) // 8)

            def ln_part(name, flips):
                f = F[name]
                root(f, 1, rstd)
                if flips:
                    unflip(f, 8 if name.endswith("out") else 0)

            def route(l):
                f = F[f"route{l}"]
                act.wait_ge(f.mm, 1)
                A(aff.rearrange("p a b -> p (a b)"), banks[0][:, 0:NT * E], ACT.Sigmoid).then_inc(f.a, 1)

            def take_x(done):
                for g in range(2):
                    act.wait_ge(xgT_done, done + g + 1)
                    A(xgT[:, 4 * g:4 * g + 4, :].rearrange("p a b -> p (a b)"), banks[g][:, :], ACT.Copy).then_inc(xgT_ready, 1)

            def experts(l):
                if l == 0:
                    act.sem_inc(y_ready, 2)
                    act.sem_inc(y_stored[0], 16)
                    act.sem_inc(y_stored[1], 16)
                take_x(34 * l)
                enter(E * l, 34 * l + 2)
                with act.Fori(0, E // 2 - 1) as it:
                    for b in range(2):
                        e = it * 2 + (E * l + b + 1)
                        enter(e, it * 4 + (34 * l + 2 * b + 4))
                        leave(e - 1, b, it * 16 + (128 * l + 16), it * (2 * P) + b * P)
                e = E * (l + 1) - 1
                enter(e, 34 * l + 2 * E)
                leave(e - 1, 0, 128 * (l + 1), (E - 2) * P)
                leave(e, 1, 128 * (l + 1), (E - 1) * P)
                for b in range(2):
                    act.wait_ge(y_stored[b], 128 * (l + 1) + 16)

            def enter(e, turned_):
                act.wait_ge(gate_up_done, 2 * e + 1)
                A(silu_g, banks[2][:, :], ACT.Silu).then_inc(silu_ready, 1)
                take_x(turned_)

            def leave(e, b, stored_, row):
                act.wait_ge(y_stored[b], stored_)
                for j in range(2):
                    act.wait_ge(y_done, 2 * e + 1 + j)
                    A(y_sb[:, b, j * 512:(j + 1) * 512], banks[5 + j][:, :], ACT.Copy).then_inc(y_ready, 1)
                act.wait_ge(y_ready, 2 * e + 4)
                act.dma_start(y_dram[bass.ds(row, P), :], y_sb[:, b, :]).then_inc(y_stored[b], 16)

            def overflow(l):
                n, done = slots_of(act, l)
                with act.If(n > 0):
                    with act.Fori(0, n) as slot:
                        j = slot + done
                        for g in range(2):
                            act.wait_ge(over["xT_mm"], j * 2 + g + 1)
                            A(xgT[:, 4 * g:4 * g + 4, :].rearrange("p a b -> p (a b)"), banks[g][:, :], ACT.Copy)\
                                .then_inc(over["xT"], 1)
                        act.wait_ge(over["gate_up_mm"], j * 2 + 1)
                        A(silu_g, banks[2][:, :], ACT.Silu).then_inc(over["silu"], 1)
                        for g in range(2):
                            act.wait_ge(over["y_mm"], j * 2 + g + 1)
                            step_in(A(y_sb[:, 0, g * 512:(g + 1) * 512], banks[5 + g][:, :], ACT.Copy), j * 2 + g + 1)
                        act.dma_start(y_dram[bass.ds(slot * P + E * P, P), :], y_sb[:, 0, :]).then_inc(over["stored"], 16)
                    act.wait_ge(over["stored"], (n + done) * 16 + 16)
                    act.sem_inc(over["all_stored"], 1)

            def step_in(ins, value):
                ins.then_inc(over["y"], 1)
                act.wait_ge(over["y"], value)

            def odd_in():
                def jobs(k, bank):
                    if k < 8:
                        return [(vC[:, k - 4, :], bank[:, 0:HD], ACT.Copy, None)]
                    if k < 12:
                        return [(wI[:, k - 8, :], bank[:, 0:4], ACT.Copy, 0.5)]
                    if k < 24:
                        n, h = INDEX[k - 12]
                        if k >= 15:
                            act.wait_ge(relu_used, k - 14)
                        return [(relu_d[:, k % 3, 0:(n + 1) * P], bank[:, 0:(n + 1) * P], ACT.Relu, HD ** -0.5)]
                    if k < 28:
                        return [(qC[:, k - 24, :], bank[:, :], ACT.Copy, HD ** -0.5)]
                    if k < 32:
                        return [(cqkv[:, k - 28, :], bank[:, 0:384], ACT.Copy, None)]
                    return [(krT[0:MLA, :], bank[0:MLA, :], ACT.Copy, None)]
                f = F["odd_in"]
                evacuate(f, ODD_IN, jobs)
                for n in range(NT):
                    act.wait_ge(f.a, ODD_IN[:29 + n].count("a"))
                    A(squares[:, n, 0:256], cqkv[:, n, 0:256], ACT.Square, accum_out=sumsq[:, n:n + 1])
                    A(squares[:, n, 256:384], cqkv[:, n, 256:384], ACT.Square, accum_out=mean[:, n:n + 1]).then_inc(odd_sq, 1)
                act.wait_ge(odd_var, 1)
                A(rstd, sumsq, ACT.Sqrt)
                A(wide_stat, mean, ACT.Sqrt).then_inc(odd_sq, 1)

            def latent():
                f, k = F["latent"], 0
                for k, who in enumerate(LATENT):
                    if who != "a":
                        continue
                    act.wait_ge(f.mm, k + 1)
                    if k < 17:
                        h = (k - 1) // 2
                        if h >= 2:
                            act.wait_ge(f.s, h - 1)
                        A(raw[0:MLA, h % 2, :], banks[k % 8][0:MLA, :], ACT.Copy, scale=MLA ** -0.5).then_inc(f.a, 1)
                    else:
                        A(kD[0:HD, k - 17, :], banks[k % 8][0:HD, :], ACT.Copy).then_inc(f.a, 1)

            def start():
                act.dma_start(pack_area["base"][:, :], w["pack_base"]).then_inc(pack_loaded["base"], 16)
                act.dma_start(pack_area["one"], w["pack_one"]).then_inc(pack_loaded["one"], 16)

            run = {
                "norm1": lambda: norm("norm1", operand["norm1"]), "project": project, "mixers": mixers, "hgrn": hgrn,
                "norm2": lambda: norm("norm2", operand["norm2"]), "up": up,
                "norm3": lambda: norm("norm3", operand["norm3"]), "gate": gate, "final_norm": final_norm,
                "even_in": even_in, "even_a": lambda: attend("even_a"), "even_b": lambda: attend("even_b"),
                "even_out": lambda: ln_part("even_out", True), "route0": lambda: route(0),
                "experts0": lambda: experts(0), "combine0": lambda: ln_part("combine0", True),
                "odd_in": odd_in, "odd_c": lambda: attend("odd_c"), "latent": latent,
                "odd_d": lambda: attend("odd_d"), "odd_out": lambda: ln_part("odd_out", True),
                "overflow0": lambda: overflow(0), "overflow1": lambda: overflow(1), "route1": lambda: route(1), "experts1": lambda: experts(1),
                "combine1": lambda: ln_part("combine1", False),
            }
            start()
            for s in stages:
                if s in run:
                    run[s]()
                meet()

        @block.vector
        def _(dve):
            meets = [0]
            steps = [0]
            V = nc.vector

            def meet():
                meets[0] += 1
                dve.drain().then_inc(met, 1)
                dve.wait_ge(met, 4 * meets[0])
                dve.drain()

            def step(ins):
                ins.then_inc(dve_step, 1)
                steps[0] += 1
                dve.wait_ge(dve_step, steps[0])

            def mul_add(out_, in0, s, in1):
                return V.scalar_tensor_tensor(out_, in0, s, in1, ALU.mult, ALU.add)

            def scaled(out_, in_, s):
                return V.tensor_scalar(out_, in_, s, None, ALU.mult) if s is not None else V.tensor_copy(out_, in_)

            def unflip(f, mm0, g=None):
                for k in range(1, KD, 2):
                    dve.wait_ge(f.mm, mm0 + k + 1)
                    scaled(xT[:, k, :], banks[k][:, :], g[:, k:k + 1] if g is not None else None)

            def norm(name, g):
                f = F[name]
                dve.wait_ge(f.a, NT)
                V.tensor_scalar(rstd, sumsq, 1.0 / D, EPS, ALU.mult, ALU.add).then_inc(f.s, 1)
                dve.wait_ge(f.a, NT + 1)
                step(V.reciprocal(rstd, rstd))
                if name == "final_norm":
                    dve.wait_ge(rows_loaded, 16)
                for n in range(NT):
                    if name == "final_norm":
                        V.scalar_tensor_tensor(x[:, n, :], x[:, n, :], rstd[:, n:n + 1], rowsG, ALU.mult, ALU.mult)\
                            .then_inc(f.v, 1)
                    else:
                        V.tensor_scalar(normed[:, n, :], x[:, n, :], rstd[:, n:n + 1], None, ALU.mult).then_inc(f.v, 1)
                if name == "norm1":
                    dve.wait_ge(pack_loaded["one"], 16)
                unflip(f, 0, g)

            def layer_norm(name, loads, flips):
                f = F[name]
                for n in range(NT):
                    for h in range(2):
                        step(V.bn_stats(bn[:, h, :], x[:, n, h * 512:(h + 1) * 512]))
                    step(V.bn_aggr(mv[:, n, :], bn.rearrange("p h t -> p (h t)")))
                V.tensor_scalar(rstd, mv[:, :, 1], LN_EPS, None, ALU.add).then_inc(f.s, 1)
                dve.wait_ge(f.a, 1)
                step(V.reciprocal(rstd, rstd))
                dve.wait_ge(rows_loaded, 16 * loads)
                for n in range(NT):
                    step(V.tensor_scalar(x[:, n, :], x[:, n, :], mv[:, n, 0:1], rstd[:, n:n + 1], ALU.subtract, ALU.mult))
                    step(V.tensor_tensor(x[:, n, :], x[:, n, :], rowsG, ALU.mult))
                    V.tensor_tensor(x[:, n, :], x[:, n, :], rowsB, ALU.add).then_inc(f.v, 1)
                if flips:
                    unflip(f, 8 if name.endswith("out") else 0)

            def residual(name, scale):
                f = F[name]
                for k in range(8):
                    dve.wait_ge(f.mm, (20 if k >= 4 else 8) + k % 4 + 1 if name == "down" else k + 1)
                    r = x[:, k % 4, (k // 4) * 512:(k // 4 + 1) * 512]
                    mul_add(r, r, scale, banks[k][:, :]).then_inc(f.v, 1)
                dve.wait_ge(f.v, 8)

            def evacuate(f, plan, jobs):
                for k, who in enumerate(plan):
                    if who == "v":
                        dve.wait_ge(f.mm, k + 1)
                        for out_, in_, s in jobs(k, banks[k % 8]):
                            ins = scaled(out_, in_, s)
                        ins.then_inc(f.v, 1)

            def project():
                def jobs(k, bank):
                    if k < 6:
                        return [(zB[:, k - 4, :], bank[:, :], None)]
                    if k < 14:
                        return [(zC[:, k - 8, :], bank[:, :], None)]
                    return [(zD[:, k - 16, :], bank[:, :], None)]
                evacuate(F["project"], PROJECT, jobs)

            def mixers():
                cw = operand["bconv_w"].rearrange("p (t k) -> p t k", k=4)
                for t in range(2):
                    step(V.tensor_scalar(xc[:, t, :], zB[:, t, :], cw[:, t, 3:4], operand["bconv_b"][:, t:t + 1],
                                         ALU.mult, ALU.add))
                    for s in (1, 2):
                        step(mul_add(xc[:, t, s:], zB[:, t, 0:T - s], cw[:, t, 3 - s:4 - s], xc[:, t, s:]))
                    mul_add(xc[:, t, 3:], zB[:, t, 0:T - 3], cw[:, t, 0:1], xc[:, t, 3:]).then_inc(M["conv_done"], 1)
                step(V.tensor_tensor(lb0, operand["lb"], operand["lb"], ALU.subtract))
                V.tensor_scalar(lb0, lb0, 0.0, None, ALU.add).then_inc(M["lb_in"], 1)
                for n in range(NT):
                    step(V.bn_stats(bn[:, 0, :], zA[:, n, 256:512]))
                    step(V.bn_aggr(mv[:, n, :], bn[:, 0, :]))
                V.tensor_scalar(rstd, mv[:, :, 1], EPS, None, ALU.add).then_inc(M["var_ready"], 1)
                V.tensor_copy(sums0[:, :, 0:1], zD[:, :, 0:1])
                step(V.tensor_tensor(sums0[:, :, 1:], zD[:, :, 1:], zD[:, :, 0:T - 1], ALU.add))
                V.tensor_copy(sums1[:, :, 0:2], sums0[:, :, 0:2])
                step(V.tensor_tensor(sums1[:, :, 2:], sums0[:, :, 2:], sums0[:, :, 0:T - 2], ALU.add))
                V.tensor_copy(sums0[:, 1, 0:4], sums1[:, 1, 0:4])
                step(V.tensor_tensor(sums0[:, 1, 4:], sums1[:, 1, 4:], sums1[:, 1, 0:T - 4], ALU.add))
                V.tensor_copy(sums1[:, 1, 0:8], sums0[:, 1, 0:8])
                step(V.tensor_tensor(sums1[:, 1, 8:], sums0[:, 1, 8:], sums0[:, 1, 0:T - 8], ALU.add))
                count = operand["count"].rearrange("p (t c) -> p t c", c=16)
                for half_, s in enumerate((sums0, sums1)):
                    r = slice(half_ * HD, (half_ + 1) * HD)
                    for t in range(2):
                        V.scalar_tensor_tensor(pooled[r, t, 16:], s[r, t, 16:], operand["window_share"][r, t:t + 1],
                                               zD[r, t, 16:], ALU.mult, ALU.subtract)
                    step(V.tensor_tensor(s[r, :, 0:16], s[r, :, 0:16], count[r, :, :], ALU.mult))
                    V.tensor_tensor(pooled[r, :, 0:16], s[r, :, 0:16], zD[r, :, 0:16], ALU.subtract)\
                        .then_inc(M["pooled"], 1)
                dve.wait_ge(M["lam_exp"], 1)
                step(V.tensor_scalar(lam_s, lam_e, 2.0, None, ALU.add))
                step(V.reciprocal(lam_s, lam_s))
                step(V.tensor_tensor(lam_s, lam_s, lam_e, ALU.mult))
                step(V.tensor_tensor(lam_q, lam_s, lam_s, ALU.mult))
                step(V.tensor_scalar(lam_p, lam_q, 1.0 / 17, None, ALU.mult))
                for m in (15, 13, 11, 9, 7, 5, 3):
                    step(V.scalar_tensor_tensor(lam_p, lam_p, 1.0 / m, lam_q, ALU.add, ALU.mult))
                step(V.scalar_tensor_tensor(lam_p, lam_p, 1.0, lam_s, ALU.add, ALU.mult))
                step(V.tensor_scalar(lam_c, operand["lam"], -1.0, 0.0, ALU.mult, ALU.max))
                step(mul_add(lam_c, lam_p, 2.0, lam_c))
                step(V.tensor_scalar(lam_c, lam_c, -8.0, None, ALU.mult))
                for t in range(2):
                    dve.wait_ge(M["r_ready"], t + 1)
                    V.tensor_scalar(log_decay[:, t, :], log_decay[:, t, :], lam_c[:, t:t + 1], None, ALU.mult)\
                        .then_inc(M["decay_ready"], 1)
                dve.wait_ge(M["sd_ready"], 1)
                step(V.reciprocal(rstd, rstd))
                for n in range(NT):
                    v_ = zA[:, n, 256:512]
                    step(V.tensor_scalar(v_, v_, mv[:, n, 0:1], rstd[:, n:n + 1], ALU.subtract, ALU.mult))
                    step(V.tensor_tensor(v_, v_, operand["aln_g"], ALU.mult))
                    V.tensor_tensor(v_, v_, operand["aln_b"], ALU.add).then_inc(M["vn_ready"], 1)
                for t in range(2):
                    dve.wait_ge(M["decay_exp"], t + 1)
                    step(V.tensor_tensor(log_decay[:, t, :], decay[:, t, :], decay[:, t, :], ALU.mult))
                    V.scalar_tensor_tensor(tanh_d[:, t, :], log_decay[:, t, :], 1.0, tanh_d[:, t, :], ALU.add, ALU.mult)\
                        .then_inc(M["mult_in"], 1)
                for t in range(2):
                    dve.wait_ge(M["i_ready"], t + 1)
                    step(V.tensor_tensor(gate_i[:, t, :], gate_i[:, t, :], xc[:, t, :], ALU.mult))
                    dve.wait_ge(M["mult_ready"], t + 1)
                    step(V.tensor_tensor(gate_i[:, t, :], gate_i[:, t, :], tanh_d[:, t, :], ALU.mult))
                    step(V.tensor_tensor_scan(log_decay[:, t, :], decay[:, t, :], gate_i[:, t, :], 0.0, ALU.mult, ALU.add))
                    V.tensor_tensor(mixT[:, 2 + t, :], log_decay[:, t, :], zB[:, 2 + t, :], ALU.mult)
                for n in range(NT):
                    dve.wait_ge(M["spatial_mm"], n + 1)
                    for h in range(4):
                        c = slice(h * HD, (h + 1) * HD)
                        ins = V.scalar_tensor_tensor(zA[:, n, c], banks[4 + n][:, c], operand["bs"][:, h:h + 1],
                                                     zA[:, n, c], ALU.add, ALU.mult)
                    ins.then_inc(M["yA_ready"], 1)
                dve.wait_ge(M["lb_exp"], 1)
                step(V.reciprocal(omlb, lb0))
                step(V.tensor_tensor(lb0, lb0, omlb, ALU.mult))
                step(V.tensor_tensor(lb0, lb0, lb0, ALU.subtract))
                step(V.tensor_scalar(omlb, lb0, -1.0, 1.0, ALU.mult, ALU.add))

            def hgrn():
                def chunks(a, q0=0, q=NC):
                    return a.rearrange("p (c j) -> p c j", j=HC)[:, q0:q0 + q, :]
                for pr in range(2):
                    f_ = zC[:, 2 + pr, :]
                    step(V.tensor_scalar(f_, f_, omlb[:, pr:pr + 1], lb0[:, pr:pr + 1], ALU.mult, ALU.add))
                    V.memset(decay_c[:, 0:1], 0.0)
                    V.memset(state[:, :, 0:1], 0.0).then_inc(M["hg_gate"], 1)
                    dve.wait_ge(M["hg_log"], pr + 1)
                    V.tensor_scalar(f_, f_, -1.0, 1.0, ALU.mult, ALU.add)
                    step(V.tensor_tensor_scan(bb, operand["inside"], log_f, 0.0, ALU.mult, ALU.add))
                    V.tensor_tensor(chunks(to_end), chunks(bb)[:, :, HC - 1:HC].to_broadcast([P, NC, HC]), chunks(bb),
                                    ALU.subtract).then_inc(M["hg_decays"], 1)
                    dve.wait_ge(M["hg_exp"], 3 * pr + 3)
                    V.tensor_tensor(qe, zC[:, pr, :], exp_b, ALU.mult)
                    V.tensor_tensor(ke, f_, exp_end, ALU.mult).then_inc(M["hg_exps"], 1)
                    q4 = NC // NT
                    shape = [P, q4, HC, HC]
                    hm = operand["hmask"].rearrange("p (t s) -> p t s", s=HC).unsqueeze(1).to_broadcast(shape)

                    def quarter(qt):
                        c0 = q4 * qt
                        return (pairs[qt % 2].rearrange("p (c t s) -> p c t s", t=HC, s=HC),
                                lambda a: chunks(a, c0, q4).unsqueeze(3).to_broadcast(shape),
                                lambda a: chunks(a, c0, q4).unsqueeze(2).to_broadcast(shape))

                    def differ(qt):
                        pd, as_t, as_s = quarter(qt)
                        step(V.tensor_tensor(pd, as_t(bb), as_s(bb), ALU.subtract))
                        V.tensor_tensor(pd, pd, hm, ALU.min).then_inc(M["hg_diff"], 1)

                    def queries_keys(qt):
                        pd, as_t, as_s = quarter(qt)
                        dve.wait_ge(M["hg_decay"], NT * pr + qt + 1)
                        step(V.tensor_tensor(pd, pd, as_t(zC[:, pr, :]), ALU.mult))
                        V.tensor_tensor(pd, pd, as_s(f_), ALU.mult).then_inc(M["hg_att"], 1)

                    def values(qt):
                        pd, as_t, as_s = quarter(qt)
                        k = NT * pr + qt
                        dve.wait_ge(M["hg_att_mm"], k + 1)
                        for b in range(2):
                            part = slice(b * q4 // 2, (b + 1) * q4 // 2)
                            att = banks[4 + 2 * (k % 2) + b][:, :].rearrange("p (c t s) -> p c t s", t=HC, s=HC)
                            ins = V.tensor_tensor(pd[:, part], att, as_s(zC[:, 4 + pr, :])[:, part], ALU.mult)
                        ins.then_inc(M["hg_used"], 1)
                        dve.wait_ge(M["hg_used"], k + 1)
                        step(V.tensor_reduce(mixT[:, 4 + pr, qt * P:(qt + 1) * P],
                                             pairs[qt % 2].rearrange("p (t s) -> p t s", s=HC), AX.X, ALU.add))

                    differ(0)
                    differ(1)
                    queries_keys(0)
                    queries_keys(1)
                    values(0)
                    differ(2)
                    values(1)
                    differ(3)
                    queries_keys(2)
                    queries_keys(3)
                    dve.wait_ge(M["hg_state_in"], 8 * (pr + 1))
                    dve.wait_ge(M["hg_decay_rows"], pr + 1)
                    for i in range(2):
                        part = state[:, i * HD // 2:(i + 1) * HD // 2, :].rearrange("p v c -> p (v c)")
                        V.tensor_tensor_scan(part, decay_rows, part, 0.0, ALU.mult, ALU.add).then_inc(M["hg_state"], 1)
                    values(2)
                    values(3)
                    dve.wait_ge(M["hg_inter_mm"], pr + 1)
                    o = mixT[:, 4 + pr, :]
                    for hh in range(2):
                        r = slice(hh * HD, (hh + 1) * HD)
                        ins = V.tensor_tensor(o[r, :], banks[1 + hh][r, :], o[r, :], ALU.add)
                    step(ins)
                    V.tensor_tensor(o_sq, o, o, ALU.mult).then_inc(M["hg_square"], 1)
                    dve.wait_ge(M["hg_mean_mm"], pr + 1)
                    V.tensor_scalar(exp_b, banks[0][:, :], EPS, None, ALU.add).then_inc(M["hg_mean"], 1)
                    dve.wait_ge(M["hg_sd"], pr + 1)
                    step(V.reciprocal(exp_b, exp_b))
                    step(V.tensor_tensor(o, o, exp_b, ALU.mult))
                    step(V.scalar_tensor_tensor(o, o, operand["cnorm"][:, 0:1], zC[:, 6 + pr, :], ALU.mult, ALU.mult))

            def up():
                f = F["up"]
                w3 = operand["fconv_w"].rearrange("p (f t) -> p f t", t=3)
                for k in range(2 * FT):
                    c = conv[:, k % 4, :]
                    dve.wait_ge(f.a, k + 1)
                    step(mul_add(c[:, 1:], banks[k % 8][:, 0:T - 1], w3[:, k, 1:2], c[:, 1:]))
                    mul_add(c[:, 2:], banks[k % 8][:, 0:T - 2], w3[:, k, 0:1], c[:, 2:]).then_inc(f.v, 1)
                    if k >= FT:
                        dve.wait_ge(f.v, k + 1)
                        dve.wait_ge(f.s, k - FT + 1)
                        V.tensor_tensor(hidden[:, k - FT, :], hidden[:, k - FT, :], c, ALU.mult).then_inc(val_scaled, 1)

            def gate():
                f = F["gate"]
                for i in range(8):
                    dve.wait_ge(f.a, i + 1)
                    V.tensor_tensor(gate_t[:, i % 2, :], banks[(2 * i) % 8][:, :], gate_s[:, i % 2, :], ALU.mult)\
                        .then_inc(f.v, 1)
                    dve.wait_ge(f.v, i + 1)
                    r = x[:, i % 4, (i // 4) * 512:(i // 4 + 1) * 512]
                    V.tensor_tensor(r, r, gate_t[:, i % 2, :], ALU.add)

            def even_in():
                f = F["even_in"]

                def jobs(k, bank):
                    if k == 4:
                        return [(kA[r, hh, :], bank[r, :], None) for hh, r in enumerate((slice(0, HD), slice(HD, P)))]
                    if k < 13:
                        return [(qB[:, k - 9, :], bank[:, :], HD ** -0.5)]
                    return [(vB[:, k - 17, :], bank[:, :], None)]
                evacuate(f, EVEN_IN[:21], jobs)
                dve.wait_ge(f.mm, 22)
                V.tensor_scalar(soft[0:8, 0, :], banks[21 % 8][0:8, :], operand["fg_b"][0:8, 0:1], None, ALU.add)\
                    .then_inc(f.s, 1)
                dve.wait_ge(f.a, EVEN_IN.count("a") + 1)
                V.scalar_tensor_tensor(soft[0:8, 0, :], soft[0:8, 0, :], 0.0, soft[0:8, 1, :], ALU.min, ALU.subtract)\
                    .then_inc(f.s, 1)
                dve.wait_ge(f.s, 2)
                V.tensor_tensor_scan(cum[0:8, :], soft[0:8, 0, :], soft[0:8, 0, :], 0.0, ALU.add, ALU.bypass)\
                    .then_inc(f.s, 1)
                dve.wait_ge(f.s, 3)
                dve.wait_ge(keys_cleared, 1)
                V.tensor_scalar(negc[0:8, :], cum[0:8, :], -1.0, None, ALU.mult)
                dve.wait_ge(f.mm, 23)
                V.tensor_copy(cT.rearrange("p a b -> p (a b)"), banks[22 % 8][:, 0:32])

            def attend(stage):
                kind = KIND[stage]
                base = 32 * list(KIND).index(stage)
                slopes = alibi_slopes(8)

                def bias(i):
                    n, h = UNITS[i]
                    u = base + i
                    w_ = span(kind, n)[1]
                    c = slice(u % 4, u % 4 + 1)
                    l_, bank = logits[:, u % 2, 0:w_], banks[u % 2][:, 0:w_]
                    dve.wait_ge(scores_done, u + 1)
                    if u >= 2:
                        dve.wait_ge(probsT_done, u - 1)
                    mask = causal[:, T - w_:T]
                    if kind == "A":
                        ins = V.tensor_tensor(l_, bank, operand["window"][:, (h + 1) * 256 - w_:(h + 1) * 256], ALU.add)
                    elif kind == "B":
                        ins = V.scalar_tensor_tensor(l_, bank, cT[:, n, h:h + 1], mask, ALU.add, ALU.add)
                    elif kind == "C":
                        d0 = n * (n + 1) // 2
                        ins = mul_add(l_, distsel[:, d0:d0 + n + 1, :].rearrange("p a b -> p (a b)"), -float(slopes[h]), bank)
                    else:
                        ins = V.tensor_tensor(l_, bank, mask, ALU.add)
                    ins.then_inc(biased, 1)
                    dve.wait_ge(biased, u + 1)
                    step(V.tensor_reduce(rowmax[:, c], l_, AX.X, ALU.max))
                    low = operand["sinks"][:, h:h + 1] if kind == "A" else TAKEN
                    V.tensor_scalar(negmax[:, c], rowmax[:, c], low, -1.0, ALU.max, ALU.mult).then_inc(shifted, 1)

                def finish(i):
                    n, h = UNITS[i]
                    u = base + i
                    g = base // 8 + n
                    c = slice(u % 4, u % 4 + 1)
                    dve.wait_ge(out_done, u + 1)
                    if kind == "A":
                        step(V.tensor_tensor(recip[:, c], rowsum[:, c], sinkexp[:, c], ALU.add))
                        step(V.reciprocal(recip[:, c], recip[:, c]))
                    else:
                        step(V.reciprocal(recip[:, c], rowsum[:, c]))
                    if h == 0 and g >= 2:
                        dve.wait_ge(outT_done, g - 1)
                    V.tensor_scalar(heads_out[:, g % 2, h * HD:(h + 1) * HD], banks[4 + u % 2][:, 0:HD], recip[:, c], None,
                                    ALU.mult).then_inc(out_ready, 1)

                for i in range(len(UNITS) + 2):
                    if i < len(UNITS):
                        bias(i)
                    if i >= 2:
                        finish(i - 2)

            def route(l):
                f = F[f"route{l}"]
                wide = [P, NT, E]
                g4 = lambda a: a.rearrange("p n (g i) -> p (n g) i", i=4)
                flat = lambda a: a.rearrange("p a b -> p (a b)")
                dve.wait_ge(f.a, 1)
                step(V.tensor_tensor(sel, aff, operand["router_b"].unsqueeze(1).to_broadcast(wide), ALU.add))

                def ranks(a, r, tmp):
                    step(V.memset(r, 0.0))
                    for d in (1, 2, 3):
                        c = tmp[:, :, 0:4 - d]
                        step(V.tensor_tensor(c, a[:, :, 0:4 - d], a[:, :, d:4], ALU.is_ge))
                        step(V.tensor_tensor(r[:, :, d:4], r[:, :, d:4], c, ALU.add))
                        step(V.scalar_tensor_tensor(r[:, :, 0:4 - d], r[:, :, 0:4 - d], 1.0, c, ALU.add, ALU.subtract))

                ranks(g4(sel), g4(rank), g4(cmp))
                step(V.tensor_scalar(flat(tmp16), flat(rank), 2.0, None, ALU.is_lt))
                step(V.tensor_tensor(flat(tmp16), flat(tmp16), flat(sel), ALU.mult))
                step(V.tensor_reduce(flat(gsum), g4(tmp16), AX.X, ALU.add))
                ranks(gsum, trank, gpick)
                step(V.tensor_scalar(flat(gpick), flat(trank), 0.0, None, ALU.is_equal))
                picked = flat(gpick).unsqueeze(2).to_broadcast([P, NT * 4, 4])
                for j, m in enumerate((first, second)):
                    step(V.tensor_scalar(flat(m), flat(rank), float(j), None, ALU.is_equal))
                    step(V.tensor_tensor(g4(m), g4(m), picked, ALU.mult))
                V.tensor_tensor(flat(chosen), flat(first), flat(second), ALU.add).then_inc(f.v, 1)
                for j, m in enumerate((first, second)):
                    step(V.tensor_tensor(flat(tmp16), flat(m), flat(aff), ALU.mult))
                    step(V.tensor_reduce(weight[:, j, :], tmp16, AX.X, ALU.add))
                step(V.tensor_tensor(wsum, weight[:, 0, :], weight[:, 1, :], ALU.add))
                step(V.reciprocal(wsum, wsum))
                for j in range(2):
                    step(V.tensor_tensor(weight[:, j, :], weight[:, j, :], wsum, ALU.mult))
                dve.wait_ge(f.mm, 2)
                tot = banks[1][:, NT * E:(NT + 1) * E]
                need = operand["over_need"].rearrange("p (k e) -> p k e", e=E)
                step(V.tensor_tensor(flags, tot.unsqueeze(1).to_broadcast([P, 3, E]), need, ALU.is_gt))
                step(V.tensor_tensor_scan(flat(before_), flat(flags), flat(flags), 0.0, ALU.add, ALU.bypass))
                step(V.tensor_copy(over_n[:, l:l + 1], flat(before_)[:, 3 * E - 1:3 * E]))
                step(V.tensor_tensor(before_, before_, flags, ALU.subtract))
                step(V.tensor_tensor(picked_e, flat(before_).unsqueeze(1).to_broadcast([P, 8, 3 * E]),
                                     operand["over_j"].unsqueeze(2).to_broadcast([P, 8, 3 * E]), ALU.is_equal))
                step(V.tensor_tensor(flat(hits), flat(flags), operand["over_e"], ALU.mult))
                step(V.tensor_tensor(picked_e, picked_e, flat(hits).unsqueeze(1).to_broadcast([P, 8, 3 * E]), ALU.mult))
                step(V.tensor_reduce(e_list, picked_e, AX.X, ALU.add))
                step(V.tensor_copy(over_list[:, :], e_list))
                step(V.scalar_tensor_tensor(flat(before_), flat(before_), float(P), operand["over_row"], ALU.mult, ALU.add))
                step(V.tensor_tensor(step_k[:, 0, :], before_[:, 0, :], operand["expert_row"], ALU.subtract))
                step(V.tensor_tensor(step_k[:, 1:3, :], before_[:, 1:3, :], before_[:, 0:2, :], ALU.subtract))
                ranked_n = banks[1][:, 0:NT * E].rearrange("p (n e) -> p n e", e=E)
                step(V.tensor_copy(ranked, ranked_n))
                step(V.tensor_tensor(posn, ranked, operand["expert_row"].unsqueeze(1).to_broadcast(wide), ALU.add))
                for k in (1, 2, 3):
                    step(V.tensor_scalar(flat(tmp16), flat(ranked), float(k * P), None, ALU.is_ge))
                    step(V.tensor_tensor(tmp16, tmp16, step_k[:, k - 1, :].unsqueeze(1).to_broadcast(wide), ALU.mult))
                    step(V.tensor_tensor(flat(posn), flat(posn), flat(tmp16), ALU.add))
                for j, m in enumerate((first, second)):
                    step(V.tensor_tensor(flat(tmp16), flat(m), flat(posn), ALU.mult))
                    step(V.tensor_reduce(r_place[:, j, :], tmp16, AX.X, ALU.add))
                V.tensor_copy(place[:, :, :], r_place).then_inc(f.s, 1)

            def experts(l):
                with dve.Fori(0, E // 2) as it:
                    for b in range(2):
                        e = it * 2 + (E * l + b)
                        dve.wait_ge(gate_up_done, e * 2 + 2)
                        dve.wait_ge(silu_ready, e + 1)
                        V.tensor_tensor(hid, banks[3][:, :], silu_g, ALU.mult).then_inc(h_ready, 1)
                        dve.wait_ge(hT_done, e + 1)
                        V.tensor_copy(hidT.rearrange("p a b -> p (a b)"), banks[4][:, :]).then_inc(hT_ready, 1)

            def overflow(l):
                n, done = slots_of(dve, l)
                with dve.If(n > 0):
                    with dve.Fori(0, n) as slot:
                        j = slot + done
                        dve.wait_ge(over["gate_up_mm"], j * 2 + 2)
                        dve.wait_ge(over["silu"], j + 1)
                        V.tensor_tensor(hid, banks[3][:, :], silu_g, ALU.mult).then_inc(over["h"], 1)
                        dve.wait_ge(over["hT_mm"], j + 1)
                        V.tensor_copy(hidT.rearrange("p a b -> p (a b)"), banks[4][:, :]).then_inc(over["hT"], 1)

            def combine(l):
                for n in range(NT):
                    dve.wait_ge(rows_gathered[n], 32 * (l + 1))
                    step(V.tensor_scalar(y_rows[:, 0, n, :], y_rows[:, 0, n, :], weight[:, 0, n:n + 1], None, ALU.mult))
                    step(mul_add(y_rows[:, 0, n, :], y_rows[:, 1, n, :], weight[:, 1, n:n + 1], y_rows[:, 0, n, :]))
                    step(mul_add(x[:, n, :], x[:, n, :], ALPHA, y_rows[:, 0, n, :]))
                layer_norm(f"combine{l}", 3 + 4 * l + 2, l == 0)

            def odd_in():
                f = F["odd_in"]

                def jobs(k, bank):
                    if k == 0:
                        return [(kI[0:HD, 0, :], bank[0:HD, :], None), (kI[HD:P, 1, :], bank[0:HD, :], None)]
                    if k < 3:
                        return [(qI[:, k - 1, :], bank[:, :], None)]
                    return [(kC[0:HD, 0, :], bank[0:HD, :], None), (kC[HD:P, 1, :], bank[0:HD, :], None)]
                evacuate(f, ODD_IN, jobs)
                mul_add(distsel[:, 0, :], causal[:, T - P:T], -BIG / 1e30, operand["dist"][:, T - P:T])
                for i, (n, h) in enumerate(INDEX):
                    w_ = (n + 1) * P
                    dve.wait_ge(f.a, 8 + i + 1)
                    if h == 0:
                        ins = V.tensor_scalar(score[n], relu_d[:, i % 3, 0:w_], wI[:, n, h:h + 1], None, ALU.mult)
                    else:
                        ins = mul_add(score[n], relu_d[:, i % 3, 0:w_], wI[:, n, h:h + 1], score[n])
                    ins.then_inc(relu_used, 1)
                    dve.wait_ge(relu_used, i + 1)
                for n in range(1, NT):
                    w_ = (n + 1) * P
                    s = score[n]
                    step(V.tensor_tensor(s, s, causal[:, T - w_:T], ALU.add))
                    for _ in range(TOPK // 8):
                        step(V.max(top8, s))
                        step(V.match_replace(s, top8, s, TAKEN))
                    d0 = n * (n + 1) // 2
                    step(V.tensor_scalar(s, s, -2e38, BIG, ALU.is_gt, ALU.mult))
                    V.tensor_tensor(distsel[:, d0:d0 + n + 1, :].rearrange("p a b -> p (a b)"), s,
                                    operand["dist"][:, T - w_:T], ALU.add)
                dve.wait_ge(odd_sq, NT)
                step(V.tensor_scalar(sumsq, sumsq, 1.0 / 256, EPS, ALU.mult, ALU.add))
                V.tensor_scalar(mean, mean, 1.0 / 128, EPS, ALU.mult, ALU.add).then_inc(odd_var, 1)
                dve.wait_ge(odd_sq, NT + 1)
                step(V.reciprocal(rstd, rstd))
                step(V.reciprocal(wide_stat, wide_stat))
                for n in range(NT):
                    V.tensor_scalar(cqkv[:, n, 0:256], cqkv[:, n, 0:256], rstd[:, n:n + 1], None, ALU.mult)
                    V.tensor_scalar(cqkv[:, n, 256:384], cqkv[:, n, 256:384], wide_stat[:, n:n + 1], None, ALU.mult)\
                        .then_inc(f.s, 1)
                for t in range(3):
                    dve.wait_ge(f.mm, 34 + t)
                    bank = banks[(33 + t) % 8][:, :]
                    if t < 2:
                        scaled(cqT[:, t, :], bank, operand["qnorm"][:, t:t + 1]).then_inc(f.v, 1)
                    else:
                        scaled(ckvT, bank, operand["kvnorm"][:, 0:1]).then_inc(f.v, 1)

            def latent():
                f = F["latent"]
                cos, sin = operand["cos"], operand["sin"]
                rope = slice(HD, MLA)
                for k, who in enumerate(LATENT):
                    if who != "v":
                        continue
                    dve.wait_ge(f.mm, k + 1)
                    bank = banks[k % 8]
                    if k == 0:
                        V.tensor_tensor(turned[rope, 0, :], bank[rope, :], sin[rope, :], ALU.mult).then_inc(f.v, 1)
                        step(V.tensor_tensor(krT[rope, :], krT[rope, :], cos[rope, :], ALU.mult))
                        step(V.tensor_tensor(krT[rope, :], krT[rope, :], turned[rope, 0, :], ALU.add))
                        V.tensor_copy(kD[rope, :, :], krT[rope, :].unsqueeze(1).to_broadcast([MLA - HD, 8, T]))
                    elif k < 17:
                        h = (k - 2) // 2
                        V.tensor_tensor(turned[0:MLA, h % 2, :], bank[0:MLA, :], sin[0:MLA, :], ALU.mult).then_inc(f.v, 1)
                        step(V.tensor_tensor(qD[0:MLA, h, :], raw[0:MLA, h % 2, :], cos[0:MLA, :], ALU.mult))
                        V.tensor_tensor(qD[0:MLA, h, :], qD[0:MLA, h, :], turned[0:MLA, h % 2, :], ALU.add).then_inc(f.s, 1)
                    else:
                        V.tensor_copy(vD[:, k - 25, :], bank[:, :]).then_inc(f.v, 1)

            def out_stage(name, loads):
                residual(name, ALPHA)
                layer_norm(name, loads, True)

            run = {
                "norm1": lambda: norm("norm1", operand["norm1"]), "project": project, "mixers": mixers, "hgrn": hgrn,
                "mix_out": lambda: residual("mix_out", 1.0), "norm2": lambda: norm("norm2", operand["norm2"]), "up": up,
                "down": lambda: residual("down", 1.0), "norm3": lambda: norm("norm3", operand["norm3"]), "gate": gate,
                "final_norm": lambda: norm("final_norm", None), "even_in": even_in,
                "even_a": lambda: attend("even_a"), "even_b": lambda: attend("even_b"),
                "even_out": lambda: out_stage("even_out", 3), "route0": lambda: route(0),
                "experts0": lambda: experts(0), "combine0": lambda: combine(0),
                "odd_in": odd_in, "odd_c": lambda: attend("odd_c"), "latent": latent,
                "odd_d": lambda: attend("odd_d"), "odd_out": lambda: out_stage("odd_out", 7),
                "overflow0": lambda: overflow(0), "overflow1": lambda: overflow(1), "route1": lambda: route(1), "experts1": lambda: experts(1), "combine1": lambda: combine(1),
            }
            for s in stages:
                if s in run:
                    run[s]()
                meet()

        @block.gpsimd
        def _(pool):
            meets = [0]
            G = nc.gpsimd
            steps = [2]

            def meet(i):
                meets[0] += 1
                pool.drain().then_inc(met, 1)
                pool.wait_ge(met, 4 * meets[0])
                pool.drain()
                if i >= 0:
                    f = turns[i % 2]
                    for s in (f.mm, f.a, f.v, f.s):
                        pool.sem_clear(s)

            def step(ins):
                ins.then_inc(pool_step, 1)
                steps[0] += 1
                pool.wait_ge(pool_step, steps[0])

            def load_rows(*names):
                for a, n in zip((rowsG, rowsB), names):
                    pool.dma_start(a, w[n]).then_inc(rows_loaded, 16)

            def project():
                G.memset(y_zero, 0.0).then_inc(pool_step, 1)
                pool.wait_ge(pool_step, 1)
                for j in range(OVER):
                    pool.dma_start(y_dram[(E + j) * P:(E + j + 1) * P, :], y_zero).then_inc(y_cleared, 16)
                G.memset(idx_zero[:, :], 0).then_inc(pool_step, 1)
                pool.dma_start(token_id[:, :], w["token_id"]).then_inc(ids_loaded, 16)
                pool.wait_ge(pool_step, 2)
                pool.dma_start(idx_dram.rearrange("(p c) o -> p (c o)", p=P), idx_zero[:, :]).then_inc(idx_cleared, 16)
                pool.wait_ge(y_cleared, 16 * OVER)

            def mixers():
                ws3 = operand["ws"].rearrange("p (h t) -> p h t", h=4)
                G.tensor_tensor(ws3, ws3, operand["wstril"].unsqueeze(1).to_broadcast([P, 4, P]), ALU.mult)\
                    .then_inc(M["ws_masked"], 1)

            def hgrn():
                of = operand["chunk_of"].unsqueeze(2).to_broadcast([P, P // HC, HD])
                for pr in range(2):
                    pool.wait_ge(M["hg_kT"], 2 * pr + 2)
                    if pr:
                        pool.wait_ge(M["hg_state"], 2 * pr)
                    for n in range(NT):
                        for hh in range(2):
                            if pr or n:
                                pool.wait_ge(M["hg_state_mm"], 2 * (NT * pr + n - 1) + hh + 1)
                            v_ = vT[:, n, hh * HD:(hh + 1) * HD].unsqueeze(1).to_broadcast([P, P // HC, HD])
                            G.tensor_tensor(v_spread[:, hh], v_, of, ALU.mult).then_inc(M["hg_v_spread"], 1)

            def norm3():
                pool.dma_start(pT.rearrange("p t q -> p (t q)"), w["pT"]).then_inc(pT_loaded, 16)

            def gate():
                pool.dma_start(pack_area["even"], w["pack_even"]).then_inc(pack_loaded["even"], 16)

            def clear_halves(tiles):
                step(G.memset(tiles[HD:P, 0::2, :], 0.0))
                step(G.memset(tiles[0:HD, 1::2, :], 0.0))

            def even_in():
                G.memset(negc, 0.0).then_inc(keys_cleared, 1)
                pool.wait_ge(keys_cleared, 1)
                clear_halves(kA)
                clear_halves(kB)

            def odd_in():
                clear_halves(kI)
                pool.sem_inc(keys_cleared, 1)
                clear_halves(kC)

            def out_stage(l, name):
                load_rows(f"ln_g_{l}_0", f"ln_b_{l}_0")
                f = F[name]
                pool.wait_ge(f.v, 12)
                pool.dma_start(x_dram.rearrange("(n p) d -> p n d", p=P), x[:, :, :]).then_inc(x_stored, 16)
                pool.wait_ge(x_stored, 16 * (l + 1))

            def route(l):
                if l == 0:
                    pool.dma_start(pack_area["odd"], w["pack_odd"]).then_inc(pack_loaded["odd"], 16)
                f = F[f"route{l}"]
                pool.wait_ge(f.s, 1)
                pool.wait_ge(ids_loaded, 16)
                pool.wait_ge(idx_cleared, 16)
                for n in range(NT):
                    for j in range(2):
                        pool.indirect_dma_start(idx_dram[:, :], bass.IndirectOffsetOnAxis(ap=place[:, j, n:n + 1], axis=0),
                                                token_id[:, n:n + 1], None).then_inc(listed, 16)
                pool.wait_ge(listed, 128 * (l + 1))
                pool.dma_start(idx_sb[:, :], idx_dram.rearrange("(e q) o -> q (e o)", q=P),
                               allow_slow_non_contiguous=True).then_inc(idx_loaded, 16)
                pool.wait_ge(idx_loaded, 16 * (l + 1))

            def experts(l):
                for e in range(E + 1):
                    if e >= 2:
                        pool.wait_ge(xgT_done, 34 * l + 2 * (e - 1))
                    pool.indirect_dma_start(xg[:, e % 2, :], None, x_dram[:, :],
                                            bass.IndirectOffsetOnAxis(ap=idx_sb[:, e:e + 1], axis=0))\
                        .then_inc(gathered[e % 2], 16)

            def overflow(l):
                if l == 0:
                    pool.sem_inc(over["stored"], 16)
                n, done = slots_of(pool, l)
                with pool.If(n > 0):
                    with pool.Fori(0, n) as slot:
                        j = slot + done
                        pool.wait_ge(over["stored"], j * 16 + 16)
                        G.tensor_copy(idx_one[:, :], idx_sb[:, bass.ds(slot + E, 1)]).then_inc(over["idx"], 1)
                        e = pool.value_load(over_list[0:1, bass.ds(slot, 1)], min_val=0, max_val=E - 1)
                        for i, name in enumerate(("moe_w_gate_2", "moe_w_up_2")):
                            src = w[name][l].rearrange("e (k p) n -> e p k n", p=P)[bass.ds(e, 1)]
                            pool.dma_start(over_w[:, i, :].rearrange("p (k n) -> p k n", k=KD), src[0]).then_inc(over["in"], 16)
                        pool.wait_ge(over["idx"], j + 1)
                        pool.sem_inc(over["passed"], 1)
                        pool.indirect_dma_start(xg[:, 0, :], None, x_dram[:, :],
                                                bass.IndirectOffsetOnAxis(ap=idx_one[:, 0:1], axis=0)).then_inc(over["in"], 16)
                        pool.wait_ge(over["gate_up_mm"], j * 2 + 2)
                        pool.sem_inc(over["passed"], 1)
                        src = w["moe_w_down_2"][l].rearrange("e (k p) n -> e p k n", p=P)[bass.ds(e, 1)]
                        pool.dma_start(over_w[:, 0, :].rearrange("p (k n) -> p k n", k=4), src[0]).then_inc(over["down_in"], 16)

            def combine(l):
                load_rows(f"ln_g_{l}_1", f"ln_b_{l}_1")
                for n in range(NT):
                    for j in range(2):
                        pool.indirect_dma_start(y_rows[:, j, n, :], None, y_dram[:, :],
                                                bass.IndirectOffsetOnAxis(ap=place[:, j, n:n + 1], axis=0))\
                            .then_inc(rows_gathered[n], 16)

            run = {
                "project": project, "mixers": mixers, "hgrn": hgrn, "norm3": norm3, "gate": gate,
                "final_norm": lambda: pool.dma_start(rowsG, w["final_g"]).then_inc(rows_loaded, 16),
                "even_in": even_in, "odd_in": odd_in,
                "even_out": lambda: out_stage(0, "even_out"), "route0": lambda: route(0),
                "experts0": lambda: experts(0), "combine0": lambda: combine(0),
                "odd_out": lambda: out_stage(1, "odd_out"), "overflow0": lambda: overflow(0), "overflow1": lambda: overflow(1), "route1": lambda: route(1),
                "experts1": lambda: experts(1), "combine1": lambda: combine(1),
            }
            for i, s in enumerate(stages):
                if s in run:
                    run[s]()
                meet(i)

        @block.sync
        def _(sp):
            sp.dma_start(x[:, :, :], w["x"][0].rearrange("(n p) d -> p n d", p=P)).then_inc(x_loaded, 16)

            def source(c):
                name, k0, nk, c0, nc_ = c
                if name.startswith("w_o_"):
                    m = w["w_o_2"][0 if name.endswith("even") else 1]
                else:
                    m = w[name][0]
                return m[k0 * P:(k0 + nk) * P, c0:c0 + nc_].rearrange("(k p) n -> p k n", p=P)

            def load(at, src, k):
                if at >= RING:
                    sp.wait_ge(w_used, at - RING + 1)
                dst = ring[:, at % RING, 0:src.shape[1] * src.shape[2]].rearrange("p (k n) -> p k n", k=src.shape[1])
                sp.dma_start(dst, src).then_inc(w_loaded[at % RING], 16)

            user = {"w_in": "project", "w_out": "mix_out", "w_up": "up", "w_down": "down", "w_pe": "gate", "w_pg": "gate",
                    "even_w_in_2": "even_in", "w_o_even": "even_out", "odd_w_in_2": "odd_in", "odd_w_uq_2": "latent",
                    "odd_w_ukv_2": "latent", "w_o_odd": "odd_out"}
            static = [(at, c) for at, c in chunks if user[c[0]] in stages]

            def load_experts(l):
                c0 = first_expert_chunk[l]
                views = {n: w[n][l].rearrange("e (k p) n -> e p k n", p=P) for n in EXPERT_W}

                def load_expert(name, e, at, freed):
                    sp.wait_ge(w_used, freed + at - RING + 1)
                    k = 4 if name == "moe_w_down_2" else KD
                    sp.dma_start(ring[:, at % RING, :].rearrange("p (k n) -> p k n", k=k), views[name][bass.ds(e, 1)][0])\
                        .then_inc(w_loaded[at % RING], 16)

                g, u, d = EXPERT_W
                load_expert(g, 0, c0, 0)
                load_expert(u, 0, c0 + 1, 0)
                with sp.Fori(0, E // 2 - 1) as it:
                    for b in range(2):
                        for j, (name, e) in enumerate(((g, b + 1), (u, b + 1), (d, b))):
                            load_expert(name, it * 2 + e, c0 + 3 * b + 2 + j, it * 6)
                for j, (name, e) in enumerate(((g, E - 1), (u, E - 1), (d, E - 2), (d, E - 1))):
                    load_expert(name, e, c0 + 3 * E - 4 + j, 0)

            for at, c in static:
                if at < first_expert_chunk[0]:
                    load(at, source(c), c[2])
            if "experts0" in stages:
                load_experts(0)
                for at, c in static:
                    if at > first_expert_chunk[0]:
                        load(at, source(c), c[2])
            if "experts1" in stages:
                load_experts(1)
            sp.wait_ge(met, 4 * len(stages))
            sp.dma_start(out[0].rearrange("(n p) d -> p n d", p=P), x[:, :, :]).then_inc(stored, 16)
            sp.wait_ge(stored, 16)


EXPERT_W = ["moe_w_gate_2", "moe_w_up_2", "moe_w_down_2"]
BIG_INPUTS = ["x", "w_in", "w_out", "w_up", "w_down", "w_pe", "w_pg", "even_w_in_2", "odd_w_in_2", "odd_w_uq_2",
              "odd_w_ukv_2", "w_o_2", "moe_w_gate_2", "moe_w_up_2", "moe_w_down_2"]


def arrays_of(inputs):
    i = {k: np.asarray(v) for k, v in inputs.items()}
    pk = packs(i)
    arrays = {n: np.ascontiguousarray(i[n]) for n in BIG_INPUTS}
    for n, v in pk.items():
        arrays[f"pack_{n}"] = np.ascontiguousarray(np.concatenate([a for _, a in v], 1))
    arrays["pT"] = np.ascontiguousarray(i["p"][0, 0].reshape(T, 2, P).transpose(2, 1, 0)).reshape(P, -1)
    arrays["token_id"] = np.ascontiguousarray(np.arange(T, dtype=np.uint32).reshape(NT, P).T)
    arrays["final_g"] = np.ascontiguousarray(rows(i["final_g"]))
    for l in range(2):
        for j in range(2):
            arrays[f"ln_g_{l}_{j}"] = np.ascontiguousarray(rows(i["ln_g_2"][l, j]))
            arrays[f"ln_b_{l}_{j}"] = np.ascontiguousarray(rows(i["ln_b_2"][l, j]))
    return arrays, {n: [(m, a.shape[1]) for m, a in v] for n, v in pk.items()}


def program(nc, arrays, shapes, stop=None):
    w = {n: nc.dram_tensor(f"in_{n}", a.shape, mybir.dt.from_np(a.dtype), kind="ExternalInput").ap()
         for n, a in arrays.items()}
    out = nc.dram_tensor("out", (1, T, D), F32, kind="ExternalOutput").ap()
    build(nc, w, shapes, out, stop)
    return nc


def kernel(**inputs):
    from concourse import bacc
    from concourse.bass_utils import run_bass_kernel_spmd

    arrays, shapes = arrays_of(inputs)
    nc = program(bacc.Bacc("TRN2", target_bir_lowering=False, num_devices=1), arrays, shapes)
    r = run_bass_kernel_spmd(nc, [{f"in_{n}": a for n, a in arrays.items()}], core_ids=[0])
    return r.results[0]["out"]
```

```python
from contextlib import ExitStack

import numpy as np

import concourse.bass as bass
import concourse.mybir as mybir

F32 = mybir.dt.float32
U32 = mybir.dt.uint32
I32 = mybir.dt.int32
ALU = mybir.AluOpType
ACT = mybir.ActivationFunctionType
AX = mybir.AxisListType

P = 128
T = 512
NT = T // P
D = 1024
KD = D // P
EPS = 1e-6
LN_EPS = 1e-5
NEG = -1e30
TAKEN = -3e38
BIG = 1e33
ALPHA = 4 ** 0.25
DFF = 2816
FT = DFF // P
E = 16
EF = 512
TOPK = 128
OVER = 2 * T // P - 1
SLOTS = E + OVER
HC = 8
NC = T // HC
RING = 6
SLOT = 4096
HD = 64
MLA = 96


def alibi_slopes(n):
    return (2.0 ** (-8.0 * np.arange(1, n + 1, dtype=np.float32) / n)).astype(np.float32)


def cols(v, width=P):
    return np.ascontiguousarray(v.reshape(-1, width).T)


def rows(v):
    return np.broadcast_to(v.reshape(1, -1), (P, v.size))


def blockdiag(w):
    out = np.zeros((P, 2, P), np.float32)
    for h in range(4):
        a = (h % 2) * HD
        out[a:a + HD, h // 2, a:a + HD] = w[h]
    return out.reshape(P, -1)


def pad_rows(a):
    out = np.zeros((P, a.shape[1]), np.float32)
    out[:a.shape[0]] = a
    return out


def packs(i):
    q = np.arange(P)
    f = np.float32
    ident = np.eye(P, dtype=f)
    causal = np.zeros((P, T), f)
    causal[:, T - P:][q[:, None] < q[None, :]] = NEG
    base = [
        ("ident", ident), ("causal", causal),
        ("before", (q[:, None] < q[None, :]).astype(f)), ("ones", np.ones((P, P), f)),
        ("expert_row", rows(np.arange(E, dtype=f) * P)),
        ("router_w", i["router_w_2"].reshape(KD, P, E).transpose(1, 0, 2).reshape(P, -1)),
        ("router_b", rows(i["router_b_2"])),
        ("over_row", rows(np.array([(E - k) * P for k in (1, 2, 3) for e in range(E)], f))),
        ("over_e", rows(np.array([e for k in (1, 2, 3) for e in range(E)], f))),
        ("over_need", rows(np.array([k * P for k in (1, 2, 3) for e in range(E)], f))),
        ("over_j", rows(np.arange(8, dtype=f))),
    ]
    half = (q[:, None] // HD == q[None, :] // HD).astype(f)
    hmask = np.where(np.arange(HC)[:, None] >= np.arange(HC)[None, :], 0.0, NEG).astype(f)
    pos = np.arange(1, 17, dtype=f)
    win = np.array([[2, 8], [4, 16]])[q // HD]
    inside = np.ones(T, f)
    inside[::HC] = 0
    one = [
        ("norm1", cols(i["norm1_g"])), ("norm2", cols(i["norm2_g"])), ("norm3", cols(i["norm3_g"])),
        ("half", half), ("halfmean", half / HD), ("hmask", rows(hmask)),
        ("chunk_of", (q[:, None] // HC == np.arange(P // HC)[None, :]).astype(f)),
        ("inside", rows(inside)),
        ("wstril", (q[:, None] <= q[None, :]).astype(f)),
        ("ws", i["a_ws"][0].transpose(2, 0, 1).reshape(P, -1)),
        ("bs", np.ascontiguousarray(i["a_bs"][0].T)),
        ("aln_g", rows(i["a_ln_g"])), ("aln_b", rows(i["a_ln_b"])),
        ("bconv_w", i["b_conv_w"][0].reshape(4, 2, P).transpose(2, 1, 0).reshape(P, -1)),
        ("bconv_b", cols(i["b_conv_b"])), ("ba", cols(i["b_ba"])), ("bx", cols(i["b_bx"])),
        ("lam", cols(i["b_lam"])), ("wa", blockdiag(i["b_wa"][0])), ("wx", blockdiag(i["b_wx"][0])),
        ("lb", cols(i["c_lb"])), ("cnorm", np.tile(i["c_norm_g"].reshape(HD, 1), (2, 1))),
        ("dw", blockdiag(i["d_w"][0])), ("dscale", cols(i["d_scale"])),
        ("count", (1 / np.minimum(pos[None, None, :], win[:, :, None].astype(f))).astype(f).reshape(P, -1)),
        ("window_share", (1 / win).astype(f)),
        ("fconv_w", i["ffn_conv_w"][0].reshape(3, 2 * FT, P).transpose(2, 1, 0).reshape(P, -1)),
        ("fconv_b", cols(i["ffn_conv_b"])),
    ]
    dist = q[:, None] + P - np.arange(2 * P)[None, :]
    slopes = alibi_slopes(8)
    window = [np.where((dist >= 0) & (dist < P), -s * dist, NEG) for s in slopes]
    pick = np.zeros((P, 8, P), f)
    for h in range(8):
        pick[h, h, :] = 1
    even = [
        ("window", np.concatenate(window, 1).astype(f)), ("pick", pick.reshape(P, -1)),
        ("fg_w", i["even_w_in_2"][0][:, 2304:].reshape(KD, P, 8).transpose(1, 0, 2).reshape(P, -1)),
        ("fg_b", pad_rows(i["even_b_f_2"].reshape(8, 1))), ("sinks", rows(i["even_sinks_2"])),
    ]
    ang = (np.arange(T, dtype=f)[None, :] * (f(10000.0) ** (-np.arange(16, dtype=f) / f(16)))[:, None]).astype(f)
    cos = np.ones((P, T), f)
    sin = np.zeros((P, T), f)
    for a in (HD, HD + 16):
        cos[a:a + 16] = np.cos(ang)
        sin[a:a + 16] = np.sin(ang)
    turn = np.zeros((P, MLA), f)
    for a in range(16):
        turn[HD + 16 + a, HD + a] = -1
        turn[HD + a, HD + 16 + a] = 1
    odd = [
        ("dist", (q[:, None] + T - P - np.arange(T)[None, :]).astype(f)),
        ("cos", cos), ("sin", sin), ("turn", turn),
        ("qnorm", cols(i["odd_q_norm_2"])), ("kvnorm", cols(i["odd_kv_norm_2"])),
    ]
    return {"base": base, "one": one, "even": even, "odd": odd}


def chunk_plan():
    plan = []
    for name, nk, ncols, step in (("w_in", 8, 2304, 512), ("w_out", 8, 1024, 512), ("w_up", 8, 2 * DFF, 512)):
        plan += [(name, 0, nk, c, min(step, ncols - c)) for c in range(0, ncols, step)]
    for half in (0, 1):
        plan += [("w_down", k, min(8, FT - k), half * 512, 512) for k in range(0, FT, 8)]
    plan += [("w_pg", 0, 8, 0, 512), ("w_pe", 0, 2, 0, 1024), ("w_pg", 0, 8, 512, 512)]
    plan += [("even_w_in_2", 0, 8, a, b - a) for a, b in ((0, 512), (512, 768), (768, 1280), (1280, 1792), (1792, 2304))]
    plan += [("w_o_even", 0, 8, c, 512) for c in (0, 512)]
    plan += ["experts0"]
    plan += [("odd_w_in_2", 0, 8, a, b - a) for a, b in ((512, 964), (964, 1380), (0, 512))]
    plan += [("odd_w_uq_2", 0, 2, 0, 768), ("odd_w_ukv_2", 0, 1, 0, 1024)]
    plan += [("w_o_odd", 0, 8, c, 512) for c in (0, 512)]
    plan += ["experts1"]
    return plan


STAGES = [
    "norm1", "project", "mixers", "hgrn", "mix_out", "up", "down", "gate",
    "even_in", "even_a", "even_b", "even_out", "route0", "experts0", "overflow0", "combine0",
    "odd_in", "odd_c", "latent", "odd_d", "odd_out", "route1", "experts1", "overflow1", "combine1",
]


def build(nc, w, pk_shapes, out, stop=None):
    ctx = ExitStack()
    stages = STAGES[:STAGES.index(stop) + 1] if stop else STAGES

    with ctx:
        def sb(name, shape, dt=F32):
            return ctx.enter_context(nc.sbuf_tensor(name, shape, dt))

        def sem(name):
            return ctx.enter_context(nc.semaphore(name))

        banks = [ctx.enter_context(nc.psum_tensor(f"bank{b}", [P, 512], F32)) for b in range(8)]

        ring = sb("ring", [P, RING, SLOT])
        x = sb("x", [P, NT, D])
        xT = sb("xT", [P, KD, T])
        mixT = xT
        pack_area = {}
        width = {n: sum(s for _, s in v) for n, v in pk_shapes.items()}
        pack_area["base"] = sb("base", [P, width["base"]])
        overlay = sb("overlay", [P, max(width[n] for n in ("one", "even", "odd"))])
        for n in ("one", "even", "odd"):
            pack_area[n] = overlay[:, 0:width[n]]
        operand = {}
        for n, v in pk_shapes.items():
            at = 0
            for name, s in v:
                operand[name] = pack_area[n][:, at:at + s]
                at += s
        small = sb("small", [P, 256])
        token_id = sb("token_id", [P, NT], U32)
        place = sb("place", [P, 2, NT], U32)
        weight = sb("weight", [P, 2, NT])
        over_list = sb("over_list", [P, 8], I32)
        over_n = sb("over_n", [P, 2], I32)
        SCRATCH = 15360
        scratch = sb("scratch", [P, SCRATCH])

        class Area:

            def __init__(self, start=0):
                self.at = start

            def take(self, *shape):
                n = int(np.prod(shape))
                assert self.at + n <= SCRATCH, (self.at, shape)
                a = scratch[:, self.at:self.at + n]
                self.at += n
                if len(shape) == 1:
                    return a
                names = "abcd"[:len(shape)]
                return a.rearrange(f"p ({' '.join(names)}) -> p {' '.join(names)}",
                                   **{m: s for m, s in zip(names[1:], shape[1:])})

        ident, causal = operand["ident"], operand["causal"]
        x_dram = nc.dram_tensor("x_rows", (T, D), F32, kind="Internal").ap()
        y_dram = nc.dram_tensor("expert_rows", (SLOTS * P, D), F32, kind="Internal").ap()
        idx_dram = nc.dram_tensor("expert_tokens", ((SLOTS + 1) * P, 1), U32, kind="Internal").ap()

        met = sem("met")
        w_loaded = [sem(f"w_loaded{s}") for s in range(RING)]
        w_used = sem("w_used")
        x_loaded = sem("x_loaded")
        dve_step, act_step, pool_step = sem("dve_step"), sem("act_step"), sem("pool_step")
        pack_loaded = {n: sem(f"{n}_loaded") for n in pk_shapes}
        stored = sem("stored")

        class Flow:

            def __init__(self, name):
                self.mm, self.a, self.v, self.s = (sem(f"{name}_{m}") for m in ("mm", "act", "dve", "stats"))

        turns = [Flow("even_stage"), Flow("odd_stage")]
        flow = {s: turns[i % 2] for i, s in enumerate(STAGES)}

        chunks, first_expert_chunk, at = [], {}, 0
        for c in chunk_plan():
            if isinstance(c, str):
                first_expert_chunk[int(c[-1])] = at
                at += 3 * E
            else:
                chunks.append((at, c))
                at += 1
        by_name = {}
        for at, c in chunks:
            by_name.setdefault(c[0], []).append((at, c))
        total_chunks = first_expert_chunk[1] + 3 * E

        def slots_of(eng, l):
            n = eng.value_load(over_n[0:1, l:l + 1], min_val=0, max_val=OVER)
            return n, eng.value_load(over_n[0:1, 0:1], min_val=0, max_val=OVER) if l else 0

        def slot_view(at, c):
            nk, ncols = c[2], c[4]
            return ring[:, at % RING, 0:nk * ncols].rearrange("p (k n) -> p k n", k=nk)

        def others(bank_plan, k):
            j = k - 8
            return bank_plan[j], bank_plan[:j + 1].count(bank_plan[j])

        normed = Area().take(NT, D)
        tile_normed = Area(FT * T).take(2, D)
        a1 = Area()
        zA, zB, zC, zD = a1.take(NT, 512), a1.take(4, T), a1.take(8, T), a1.take(2, T)
        mixers_at, zC_end = a1.at, 8192
        hidden = Area().take(FT, T)
        hidden_end = FT * T
        ae = Area()
        qA, kA, vA = ae.take(4, T), ae.take(2, T), ae.take(NT, P)
        qB, kB, vB = ae.take(4, T), ae.take(8, T), ae.take(NT, 512)
        negc = ae.take(T)
        ao = Area()
        qC, kC, vC, distsel = ao.take(4, T), ao.take(2, T), ao.take(NT, HD), ao.take(10, P)
        qI, kI, wI, cqkv = ao.take(2, T), ao.take(2, T), ao.take(NT, 4), ao.take(NT, 384)
        ad = Area()
        qD, kD, vD = ad.take(8, T), ad.take(8, T), ad.take(NT, 512)
        assert ae.at <= 12288 and max(ao.at, ad.at) <= 10240
        al = Area(10240)
        cqT, ckvT, krT = al.take(2, T), al.take(T), al.take(T)
        at_ = Area(12288)
        logits, probsT, heads_out = at_.take(3, T), at_.take(2, T), at_.take(512)
        stat = small[:, 0:64]
        rowsG, rowsB = Area(8192).take(D), Area(8192 + D).take(D)
        y_rows = Area().take(2, NT, D)
        pT = Area(FT * T + 2 * D).take(2, T)
        gate_s, gate_t = Area(9216).take(2, 512), Area(10240).take(2, 512)
        conv = Area(hidden_end).take(4, T)
        alm = Area(12288)
        turned, raw = alm.take(2, T), alm.take(2, T)

        class Column:

            at = 64

            @classmethod
            def take(cls, n=1):
                a = small[:, cls.at:cls.at + n]
                cls.at += n
                assert cls.at <= 256
                return a

        sumsq, rstd, mean = Column.take(NT), Column.take(NT), Column.take(NT)
        mv = Column.take(2 * NT).rearrange("p (n t) -> p n t", t=2)
        bn = Column.take(12).rearrange("p (h t) -> p h t", t=6)
        lam_e, lam_s, lam_q, lam_p, lam_c = (Column.take(2) for _ in range(5))
        lb0, omlb = Column.take(2), Column.take(2)
        top8 = Column.take(8)
        rowmax, negmax, recip = (Column.take(8) for _ in range(3))
        rowsum, sinkexp = (Column.take(16).rearrange("p (b h) -> p b h", b=2) for _ in range(2))
        wide_stat = Column.take(4)
        cT = Column.take(8 * NT).rearrange("p (n h) -> p n h", h=8)

        F = flow
        PROJECT = "aaaa" + "vvaa" + "aaaa" + "vvaa" + "vv"
        EVEN_IN = "aaaa" + "vaaaa" + "vvvv" + "aaaa" + "vvvv" + "v"
        ODD_IN = "vvv" + "aaaa" + "a" * 12 + "a" + "aaaa" + "aaaa" + "aaaa" + "a"
        INDEX = [(n, h) for n in range(1, NT) for h in range(4)]
        UNITS = [(n, h) for n in range(NT) for h in range(8)]
        KIND = {"even_a": "A", "even_b": "B", "odd_c": "C", "odd_d": "D"}

        def span(kind, n):
            if kind == "A":
                return max(0, n - 1) * P, P * min(2, n + 1)
            return 0, (n + 1) * P

        def head_q(kind, n, h):
            t = slice(n * P, (n + 1) * P)
            if kind == "A":
                return qA[:, h % 4, t]
            if kind in "BC":
                return (qB if kind == "B" else qC)[:, h // 2, t]
            return qD[0:MLA, h, t]

        def head_k(kind, n, h):
            s0, w_ = span(kind, n)
            s = slice(s0, s0 + w_)
            if kind == "A":
                return kA[:, h // 4, s]
            if kind == "B":
                return kB[:, h, s]
            if kind == "C":
                return kC[:, h % 2, s]
            return kD[0:MLA, h, s]

        def head_v(kind, block_, h):
            if kind == "A":
                return vA[:, block_, (h // 4) * HD:(h // 4 + 1) * HD]
            if kind == "C":
                return vC[:, block_, :]
            return (vB if kind == "B" else vD)[:, block_, h * HD:(h + 1) * HD]


        scores_done, biased, shifted, probs_done = sem("scores_done"), sem("biased"), sem("shifted"), sem("probs_done")
        probsT_done, probsT_ready, out_done = sem("probsT_done"), sem("probsT_ready"), sem("out_done")
        out_ready, outT_done, outT_ready = sem("out_ready"), sem("outT_done"), sem("outT_ready")
        gathered = [sem("gathered0"), sem("gathered1")]
        xgT_done, xgT_ready = sem("xgT_done"), sem("xgT_ready")
        gate_up_done, silu_ready, h_ready = sem("gate_up_done"), sem("silu_ready"), sem("h_ready")
        hT_done, hT_ready, y_done = sem("hT_done"), sem("hT_ready"), sem("y_done")
        y_ready = sem("y_ready")
        y_stored = [sem("y_stored0"), sem("y_stored1")]
        rows_gathered = [sem(f"rows_gathered{n}") for n in range(NT)]
        idx_cleared, idx_loaded, x_stored = sem("idx_cleared"), sem("idx_loaded"), sem("x_stored")
        pT_loaded, rows_loaded, ids_loaded = sem("pT_loaded"), sem("rows_loaded"), sem("ids_loaded")
        val_scaled = sem("val_scaled")
        NORMS = ["mix_out", "down", "gate", "even_out", "combine0", "odd_out", "combine1"]
        FEATURE_GAIN = {"mix_out": operand["norm2"], "down": operand["norm3"]}
        norm_base = {s: NT * i for i, s in enumerate(NORMS)}
        first_weighed, tile_gained = sem("first_weighed"), sem("tile_gained")
        tile_var, tile_sd, tile_ready = sem("tile_var"), sem("tile_sd"), sem("tile_ready")
        tile_turned, tile_taken, routed = sem("tile_turned"), sem("tile_taken"), sem("routed")

        def turn_bank(stage, n):
            return 2 * n if stage in ("gate", "combine0") else 2 * (n % 2)
        keys_cleared = sem("keys_cleared")
        listed = sem("listed")
        M = {n: sem(n) for n in (
            "ws_masked", "conv_done", "gates_mm", "r_ready", "i_ready", "decay_ready", "decay_exp", "mult_in", "mult_ready",
            "spatial_mm", "vn_ready", "yA_ready", "yA_mm", "pooled", "yD_mm", "var_ready", "sd_ready",
            "lam_exp", "lb_in", "lb_exp", "hg_gate", "hg_log", "hg_decays", "hg_exp", "hg_exps", "hg_kT_mm",
            "hg_kT", "hg_v_spread", "hg_state_mm", "hg_state_in", "hg_state", "hg_inter_mm", "hg_diff", "hg_decay",
            "hg_att", "hg_att_mm", "hg_used", "hg_square", "hg_mean_mm", "hg_mean", "hg_sd", "hg_decay_rows")}
        squares = Area(10240).take(NT, 384)
        odd_sq, odd_var = sem("odd_sq"), sem("odd_var")
        relu_used = sem("relu_used")
        flags, before_, step_k, hits, slot_row = (Area(2048 + 256 * i).take(3, E) for i in range(5))
        picked_e, e_list, ranked = Area(4096).take(8, 3 * E), Area(4500).take(8), Area(4600).take(NT, E)
        ai = Area(12288)
        relu_d, score = ai.take(3, T), {n: ai.take((n + 1) * P) for n in range(1, NT)}
        am = Area(mixers_at)
        xc, pooled, log_decay, gate_i, decay, tanh_d = (am.take(2, T) for _ in range(6))
        sums0, sums1 = tanh_d, decay
        state = Area().take(HD, NC)
        ah = Area(zC_end)
        bb, qe, ke, decay_c = ah.take(T), ah.take(T), ah.take(T), ah.take(NC)
        keT, vT, v_spread = ah.take(NT, P), ah.take(NT, P), ah.take(2, P // HC, HD)
        decay_rows = v_spread.rearrange("p h c v -> p (h c v)")
        pairs = [ah.take(1024), ah.take(1024)]
        log_f, to_end = pairs[0][:, 0:T], pairs[0][:, T:2 * T]
        exp_b, exp_end = pairs[1][:, 0:T], pairs[1][:, T:2 * T]
        o_sq = qe
        LATENT = "v" + "av" * 8 + "a" * 8 + "v" * 4
        cum, soft = probsT[:, 0, :], logits[:, 0:2, :]
        fg_w = operand["fg_w"].rearrange("p (k h) -> p k h", k=KD)
        pick = operand["pick"].rearrange("p (h q) -> p h q", h=8)
        router_w = operand["router_w"].rearrange("p (k e) -> p k e", k=KD)
        ar = Area()
        aff, sel, chosen, first, second, tmp16, posn = (ar.take(NT, E) for _ in range(7))
        rank, trank = ar.take(NT, E), ar.take(NT, 4)
        gsum, gpick, cmp, wsum, r_place, total = ar.take(NT, 4), ar.take(NT, 4), ar.take(NT, 16), ar.take(NT), ar.take(2, NT), ar.take(E)
        idx_zero = sb("idx_zero", [P, SLOTS + 1], U32)
        y_zero = Area(SCRATCH - D).take(D)
        ea = Area()
        xg, y_sb = ea.take(2, D), ea.take(2, D)
        xgT, silu_g, hid, hidT = ea.take(KD, P), ea.take(EF), ea.take(EF), ea.take(4, P)
        idx_sb = sb("idx_sb", [P, SLOTS + 1], U32)
        idx_one = sb("idx_one", [P, 1], U32)
        over_w = ea.take(2, SLOT)
        y_cleared = sem("y_cleared")
        over = {n: sem(f"over_{n}") for n in ("idx", "in", "xT_mm", "xT", "gate_up_mm", "silu", "h", "hT_mm", "hT", "down_in",
                                              "y_mm", "y", "stored", "passed", "all_stored")}
        block = ctx.enter_context(nc.Block())

        @block.tensor
        def _(pe):
            meets = [0]

            def meet():
                meets[0] += 1
                pe.drain().then_inc(met, 1)
                pe.wait_ge(met, 4 * meets[0])
                pe.drain()

            def arrived(at):
                pe.wait_ge(w_loaded[at % RING], 16 * (at // RING + 1))

            def bank_emptied(f, plan, k):
                if k >= 8:
                    who, n = others(plan, k)
                    pe.wait_ge(f.a if who == "a" else f.v, n)

            def product(out_, pairs):
                for j, (lhsT, rhs) in enumerate(pairs):
                    mm = nc.tensor.matmul(out_, lhsT, rhs, start=(j == 0), stop=(j == len(pairs) - 1))
                return mm

            def flip(f, src, ready_v, n_tiles=KD):
                for k in range(n_tiles):
                    for n in range(NT):
                        if k == 0:
                            pe.wait_ge(f.v, ready_v + n)
                        mm = nc.tensor.transpose(banks[k][:, n * P:(n + 1) * P], src[:, n, k * P:(k + 1) * P], ident)
                    mm.then_inc(f.mm, 1)

            def turn_tile(stage, n):
                base = norm_base[stage] + n
                pe.wait_ge(tile_ready, base + 1)
                if n >= 2 and turn_bank(stage, n) == turn_bank(stage, n - 2):
                    pe.wait_ge(tile_taken, base - 1)
                src = tile_normed[:, n % 2, :] if stage in FEATURE_GAIN else x[:, n, :]
                for j in range(2):
                    for t in range(4):
                        mm = nc.tensor.transpose(banks[turn_bank(stage, n) + j][:, t * P:(t + 1) * P],
                                                 src[:, (4 * j + t) * P:(4 * j + t + 1) * P], ident)
                mm.then_inc(tile_turned, 1)

            def route_tile(stage, n):
                if stage not in ("even_out", "odd_out"):
                    return
                pe.wait_ge(tile_taken, norm_base[stage] + n + 1)
                product(banks[4][:, n * E:(n + 1) * E],
                        [(xT[:, t, n * P:(n + 1) * P], router_w[:, t, :]) for t in range(KD)]).then_inc(routed, 1)

            def turn_behind(stage, n):
                if n >= 2:
                    turn_tile(stage, n - 2)
                if n == NT - 1:
                    route_tile(stage, n - 3)
                    turn_tile(stage, n - 1)
                    route_tile(stage, n - 2)
                    turn_tile(stage, n)
                    route_tile(stage, n - 1)
                    route_tile(stage, n)

            def norm1():
                pe.wait_ge(pack_loaded["base"], 16)
                flip(F["norm1"], normed, 1)

            def tokens(f, plan, k, at, c, n, c0, c1):
                w_ = slot_view(at, c)
                bank_emptied(f, plan, k)
                product(banks[k % 8][:, 0:c1 - c0],
                        [(xT[:, t, n * P:(n + 1) * P], w_[:, t, c0:c1]) for t in range(KD)]).then_inc(f.mm, 1)

            def features(f, plan, k, at, c, c0, m=P):
                w_ = slot_view(at, c)
                bank_emptied(f, plan, k)
                product(banks[k % 8][0:m, :],
                        [(w_[:, t, c0:c0 + m], xT[:, t, :]) for t in range(KD)]).then_inc(f.mm, 1)

            def project():
                f, k = F["project"], 0
                for j, (at, c) in enumerate(by_name["w_in"]):
                    arrived(at)
                    for g in range(2 if j == 4 else 4):
                        if j == 0:
                            tokens(f, PROJECT, k, at, c, g, 0, 512)
                        else:
                            features(f, PROJECT, k, at, c, g * P)
                        k += 1
                    release(f.mm, k)

            def release(done, value):
                pe.wait_ge(done, value)
                pe.sem_inc(w_used, 1)

            def mixers():
                pe.wait_ge(M["conv_done"], 2)
                for g, name in enumerate(("wa", "wx")):
                    for t in range(2):
                        nc.tensor.matmul(banks[2 * g + t][:, :], operand[name][:, t * P:(t + 1) * P], xc[:, t, :],
                                         start=True, stop=True).then_inc(M["gates_mm"], 1)
                pe.wait_ge(M["pooled"], 2)
                pe.wait_ge(M["i_ready"], 2)
                for t in range(2):
                    nc.tensor.matmul(banks[2 + t][:, :], operand["dw"][:, t * P:(t + 1) * P], pooled[:, t, :],
                                     start=True, stop=True).then_inc(M["yD_mm"], 1)
                pe.wait_ge(M["ws_masked"], 1)
                for n in range(NT):
                    pe.wait_ge(M["vn_ready"], n + 1)
                    for h in range(4):
                        mm = nc.tensor.matmul(banks[4 + n][:, h * HD:(h + 1) * HD], operand["ws"][:, h * P:(h + 1) * P],
                                              zA[:, n, 256 + h * HD:256 + (h + 1) * HD], start=True, stop=True)
                    mm.then_inc(M["spatial_mm"], 1)
                pe.wait_ge(M["r_ready"], 2)
                for t in range(2):
                    for n in range(NT):
                        pe.wait_ge(M["yA_ready"], n + 1)
                        mm = nc.tensor.transpose(banks[t][:, n * P:(n + 1) * P], zA[:, n, t * P:(t + 1) * P], ident)
                    mm.then_inc(M["yA_mm"], 1)

            def hgrn():
                for pr in range(2):
                    pe.wait_ge(M["hg_exps"], pr + 1)
                    if pr:
                        pe.wait_ge(M["hg_mean"], pr)
                    for n in range(NT):
                        mm = nc.tensor.transpose(banks[0][:, n * P:(n + 1) * P], ke[:, n * P:(n + 1) * P], ident)
                    mm.then_inc(M["hg_kT_mm"], 1)
                    for n in range(NT):
                        mm = nc.tensor.transpose(banks[1][:, n * P:(n + 1) * P], zC[:, 4 + pr, n * P:(n + 1) * P], ident)
                    mm.then_inc(M["hg_kT_mm"], 1)
                    pe.wait_ge(M["hg_kT"], 2 * pr + 1)
                    for n in range(NT + 1):
                        if n == 1:
                            pe.wait_ge(M["hg_kT"], 2 * pr + 2)
                        if 2 <= n < NT:
                            pe.wait_ge(M["hg_state_in"], 2 * (NT * pr + n - 1))
                        for hh in range(2 if n < NT else 0):
                            pe.wait_ge(M["hg_v_spread"], 2 * (NT * pr + n) + hh + 1)
                            for half_ in range(2):
                                mm = nc.tensor.matmul(
                                    banks[(2 + 2 * n + half_) % 4][hh * HD:(hh + 1) * HD, :],
                                    keT[:, n, hh * HD:(hh + 1) * HD],
                                    v_spread[:, hh, half_ * 8:half_ * 8 + 8, :], start=True, stop=True)
                            mm.then_inc(M["hg_state_mm"], 1)
                        if n == 0:
                            continue
                        k = NT * pr + n - 1
                        pe.wait_ge(M["hg_att"], k + 1)
                        if k >= 2:
                            pe.wait_ge(M["hg_used"], k - 1)
                        for b in range(2):
                            mm = nc.tensor.matmul(banks[4 + 2 * (k % 2) + b][:, :], operand["half"],
                                                  pairs[k % 2][:, b * 512:(b + 1) * 512], start=True, stop=True)
                        mm.then_inc(M["hg_att_mm"], 1)
                    pe.wait_ge(M["hg_state"], 2 * pr + 2)
                    for c in range(NC):
                        for hh in range(2):
                            r = slice(hh * HD, (hh + 1) * HD)
                            mm = nc.tensor.matmul(banks[1 + hh][r, c * HC:(c + 1) * HC], state[r, :, c],
                                                  qe[r, c * HC:(c + 1) * HC], start=True, stop=True)
                    mm.then_inc(M["hg_inter_mm"], 1)
                    pe.wait_ge(M["hg_square"], pr + 1)
                    nc.tensor.matmul(banks[0][:, :], operand["halfmean"], o_sq, start=True, stop=True)\
                        .then_inc(M["hg_mean_mm"], 1)

            def halves(name, chunk_name, lhs):
                f = F[name]
                for half_, (at, c) in enumerate(by_name[chunk_name]):
                    arrived(at)
                    w_ = slot_view(at, c)
                    for n in range(NT):
                        k = NT * half_ + n
                        product(banks[k][:, :], [(lhs[:, t, n * P:(n + 1) * P], w_[:, t, :]) for t in range(KD)])\
                            .then_inc(f.mm, 1)
                        if half_ == 1:
                            if n == NT - 1:
                                release(f.mm, 2 * NT)
                            turn_behind(name, n)
                    if half_ == 0:
                        release(f.mm, NT)

            def mix_out():
                halves("mix_out", "w_out", mixT)

            def up():
                f = F["up"]
                for j, (at, c) in enumerate(by_name["w_up"]):
                    arrived(at)
                    w_ = slot_view(at, c)
                    for g in range(4):
                        k = 4 * j + g
                        if k >= 8:
                            pe.wait_ge(f.v, k - 7)
                        product(banks[k % 8][:, :], [(w_[:, t, g * P:(g + 1) * P], xT[:, t, :]) for t in range(KD)])\
                            .then_inc(f.mm, 1)
                    release(f.mm, 4 * j + 4)

            def down():
                f = F["down"]
                for j, (at, c) in enumerate(by_name["w_down"]):
                    arrived(at)
                    w_ = slot_view(at, c)
                    half_, k0 = j // 3, c[1]
                    for n in range(NT):
                        for t in range(c[2]):
                            mm = nc.tensor.matmul(banks[4 * half_ + n][:, :], hidden[:, k0 + t, n * P:(n + 1) * P],
                                                  w_[:, t, :], start=(k0 + t == 0), stop=(k0 + t == FT - 1))
                        mm.then_inc(f.mm, 1)
                        if j == 5:
                            if n == NT - 1:
                                release(f.mm, NT * 6)
                            turn_behind("down", n)
                    if j < 5:
                        release(f.mm, NT * (j + 1))

            def gate():
                f = F["gate"]
                (at_e, c_e), = by_name["w_pe"]
                arrived(at_e)
                pe.wait_ge(pT_loaded, 16)
                w_e = slot_view(at_e, c_e)
                for half_, (at, c) in enumerate(by_name["w_pg"]):
                    arrived(at)
                    w_g = slot_view(at, c)
                    for n in range(NT):
                        k = 2 * (NT * half_ + n)
                        bank_emptied(f, "va" * 8, k)
                        product(banks[k % 8][:, :], [(pT[:, t, n * P:(n + 1) * P],
                                                      w_e[:, t, half_ * 512:(half_ + 1) * 512]) for t in range(2)])\
                            .then_inc(f.mm, 1)
                        bank_emptied(f, "va" * 8, k + 1)
                        product(banks[(k + 1) % 8][:, :], [(xT[:, t, n * P:(n + 1) * P], w_g[:, t, :]) for t in range(KD)])\
                            .then_inc(f.mm, 1)
                        if half_ == 1:
                            if n == NT - 1:
                                release(f.mm, 16)
                                release(f.mm, 16)
                            turn_behind("gate", n)
                    if half_ == 0:
                        release(f.mm, 8)

            def even_in():
                f, k = F["even_in"], 0
                pe.wait_ge(pack_loaded["even"], 16)
                for j, (at, c) in enumerate(by_name["even_w_in_2"]):
                    arrived(at)
                    if j == 1:
                        features(f, EVEN_IN, k, at, c, 0)
                        k += 1
                    for g in range(4):
                        if j == 1:
                            tokens(f, EVEN_IN, k, at, c, g, P, 2 * P)
                        elif j == 4:
                            tokens(f, EVEN_IN, k, at, c, g, 0, 512)
                        else:
                            features(f, EVEN_IN, k, at, c, g * P)
                        k += 1
                    release(f.mm, k)
                bank_emptied(f, EVEN_IN, k)
                product(banks[k % 8][0:8, :], [(fg_w[:, t, :], xT[:, t, :]) for t in range(KD)]).then_inc(f.mm, 1)
                pe.wait_ge(f.s, 3)
                for n in range(NT):
                    mm = nc.tensor.transpose(banks[(k + 1) % 8][:, n * 8:(n + 1) * 8], cum[0:8, n * P:(n + 1) * P],
                                             ident[0:8, 0:8])
                mm.then_inc(f.mm, 1)

            def attend(stage):
                kind = KIND[stage]
                base = 32 * list(KIND).index(stage)

                def score(i):
                    n, h = UNITS[i]
                    u = base + i
                    if u >= 3:
                        pe.wait_ge(biased, u - 2)
                    out_ = banks[u % 3][:, 0:span(kind, n)[1]]
                    if kind == "B":
                        nc.tensor.matmul(out_, head_q(kind, n, h), head_k(kind, n, h), start=True, stop=False)
                        mm = nc.tensor.matmul(out_, pick[:, h, :], negc[:, 0:span(kind, n)[1]],
                                              start=False, stop=True)
                    else:
                        mm = nc.tensor.matmul(out_, head_q(kind, n, h), head_k(kind, n, h), start=True, stop=True)
                    mm.then_inc(scores_done, 1)

                def turn_probs(i):
                    n, h = UNITS[i]
                    u = base + i
                    pe.wait_ge(probs_done, u + 1)
                    if u >= 2:
                        pe.wait_ge(probsT_ready, u - 1)
                    for b in range(span(kind, n)[1] // P):
                        mm = nc.tensor.transpose(banks[3 + u % 2][:, b * P:(b + 1) * P],
                                                 logits[:, u % 3, b * P:(b + 1) * P], ident)
                    mm.then_inc(probsT_done, 1)

                def weigh(i):
                    n, h = UNITS[i]
                    u = base + i
                    s0, w_ = span(kind, n)
                    pe.wait_ge(probsT_ready, u + 1)
                    g = u // 8
                    if h == 0 and g >= 2:
                        pe.wait_ge(out_ready, g - 1)
                    for b in range(w_ // P):
                        mm = nc.tensor.matmul(banks[5 + g % 2][:, h * HD:(h + 1) * HD], probsT[:, u % 2, b * P:(b + 1) * P],
                                              head_v(kind, s0 // P + b, h), start=(b == 0), stop=(b == w_ // P - 1))
                    mm.then_inc(out_done, 1)

                def turn_out(n):
                    g = base // 8 + n
                    pe.wait_ge(out_ready, g + 1)
                    if g >= 1:
                        pe.wait_ge(outT_ready, g)
                    for t in range(4):
                        mm = nc.tensor.transpose(banks[7][:, t * P:(t + 1) * P], heads_out[:, t * P:(t + 1) * P], ident)
                    mm.then_inc(outT_done, 1)

                for i in range(len(UNITS) + 5):
                    if i < len(UNITS):
                        score(i)
                    if 2 <= i < len(UNITS) + 2:
                        turn_probs(i - 2)
                    if 3 <= i < len(UNITS) + 3:
                        weigh(i - 3)
                    if i >= 12 and (i - 12) % 8 == 0:
                        turn_out((i - 12) // 8)

            def even_out():
                halves("even_out", "w_o_even", mixT)

            def odd_out():
                halves("odd_out", "w_o_odd", mixT)

            def route(l):
                f = F[f"route{l}"]
                pe.wait_ge(f.v, 1)
                for n in range(NT):
                    mm = product(banks[1][:, n * E:(n + 1) * E],
                                 [(operand["before"] if m == n else operand["ones"], chosen[:, m, :]) for m in range(n + 1)])
                mm = product(banks[1][:, NT * E:(NT + 1) * E], [(operand["ones"], chosen[:, m, :]) for m in range(NT)])
                mm.then_inc(f.mm, 1)

            def turn_x(b, landed_):
                pe.wait_ge(gathered[b], landed_)
                for g in range(2):
                    for t in range(4):
                        mm = nc.tensor.transpose(banks[g][:, t * P:(t + 1) * P],
                                                 xg[:, b, (4 * g + t) * P:(4 * g + t + 1) * P], ident)
                    mm.then_inc(xgT_done, 1)

            def weight_view(at, k):
                return ring[:, at % RING, :].rearrange("p (k n) -> p k n", k=k)

            def enter(l, e, at, loads, b, next_landed):
                pe.wait_ge(xgT_ready, 2 * e + 2 + 2 * l)
                for j in range(2):
                    pe.wait_ge(w_loaded[(at + j) % RING], loads + 16 * ((at + j) // RING))
                    w_ = weight_view(at + j, KD)
                    product(banks[2 + j][:, :], [(xgT[:, t, :], w_[:, t, :]) for t in range(KD)])\
                        .then_inc(gate_up_done, 1)
                turn_x(1 - b, next_landed)
                for j in range(2):
                    pe.wait_ge(gate_up_done, 2 * e + 1 + j)
                    pe.sem_inc(w_used, 1)

            def leave(e, at, loads):
                pe.wait_ge(hT_ready, e + 1)
                pe.wait_ge(w_loaded[at % RING], loads + 16 * (at // RING))
                w_ = weight_view(at, 4)
                for j in range(2):
                    pe.wait_ge(y_ready, 2 * e + 1 + j)
                    product(banks[5 + j][:, :], [(hidT[:, t, :], w_[:, t, j * 512:(j + 1) * 512]) for t in range(4)])\
                        .then_inc(y_done, 1)

            def turn_h(e):
                pe.wait_ge(h_ready, e + 1)
                for t in range(4):
                    mm = nc.tensor.transpose(banks[4][:, t * P:(t + 1) * P], hid[:, t * P:(t + 1) * P], ident)
                mm.then_inc(hT_done, 1)

            def experts(l):
                c0 = first_expert_chunk[l]
                turn_x(0, 16 * (9 * l + 1))
                enter(l, E * l, c0, 16, 0, 16 * (8 * l + 1))
                turn_h(E * l)
                with pe.Fori(0, E // 2 - 1) as it:
                    for b in range(2):
                        e = it * 2 + (E * l + b + 1)
                        at = c0 + 3 * b + 2
                        enter(l, e, at, it * 16 + 16, 1 - b, it * 16 + (16 * (9 * l + 2) if b == 0 else 16 * (8 * l + 2)))
                        leave(e - 1, at + 2, it * 16 + 16)
                        turn_h(e)
                        release(y_done, 2 * e)
                e = E * (l + 1) - 1
                at = c0 + 3 * (E - 1) - 1
                enter(l, e, at, 16, 1, 16 * (9 * l + 9))
                leave(e - 1, at + 2, 16)
                turn_h(e)
                release(y_done, 2 * e)
                leave(e, at + 3, 16)
                release(y_done, 2 * e + 2)

            def overflow(l):
                n, done = slots_of(pe, l)
                gate_w, up_w = (over_w[:, i, :].rearrange("p (k n) -> p k n", k=KD) for i in range(2))
                down_w = over_w[:, 0, :].rearrange("p (k n) -> p k n", k=4)
                with pe.If(n > 0):
                    with pe.Fori(0, n) as slot:
                        j = slot + done
                        pe.wait_ge(over["in"], j * 48 + 48)
                        for g in range(2):
                            for t in range(4):
                                mm = nc.tensor.transpose(banks[g][:, t * P:(t + 1) * P],
                                                         xg[:, 0, (4 * g + t) * P:(4 * g + t + 1) * P], ident)
                            mm.then_inc(over["xT_mm"], 1)
                        pe.wait_ge(over["xT"], j * 2 + 2)
                        for i, w_ in enumerate((gate_w, up_w)):
                            product(banks[2 + i][:, :], [(xgT[:, t, :], w_[:, t, :]) for t in range(KD)])\
                                .then_inc(over["gate_up_mm"], 1)
                        pe.wait_ge(over["h"], j + 1)
                        for t in range(4):
                            mm = nc.tensor.transpose(banks[4][:, t * P:(t + 1) * P], hid[:, t * P:(t + 1) * P], ident)
                        mm.then_inc(over["hT_mm"], 1)
                        pe.wait_ge(over["hT"], j + 1)
                        pe.wait_ge(over["down_in"], j * 16 + 16)
                        for i in range(2):
                            product(banks[5 + i][:, :], [(hidT[:, t, :], down_w[:, t, i * 512:(i + 1) * 512])
                                                         for t in range(4)]).then_inc(over["y_mm"], 1)

            def combine(l):
                if l == 0:
                    for n in range(NT):
                        turn_tile("combine0", n)

            def odd_in():
                f, k = F["odd_in"], 0
                (a0, c0), (a1_, c1), (a2, c2) = by_name["odd_w_in_2"]
                pe.wait_ge(pack_loaded["odd"], 16)
                arrived(a0)
                features(f, ODD_IN, 0, a0, c0, 384, HD)
                features(f, ODD_IN, 1, a0, c0, P)
                features(f, ODD_IN, 2, a0, c0, 2 * P)
                for n in range(NT):
                    tokens(f, ODD_IN, 3 + n, a0, c0, n, 448, 452)
                pe.wait_ge(f.v, 3)
                pe.wait_ge(keys_cleared, 2)
                k = 7
                for n, h in INDEX:
                    bank_emptied(f, ODD_IN, k)
                    nc.tensor.matmul(banks[k % 8][:, 0:(n + 1) * P], qI[:, h // 2, n * P:(n + 1) * P],
                                     kI[:, h % 2, 0:(n + 1) * P], start=True, stop=True).then_inc(f.mm, 1)
                    k += 1
                features(f, ODD_IN, k, a0, c0, 0, HD)
                k += 1
                for n in range(NT):
                    tokens(f, ODD_IN, k, a0, c0, n, HD, 2 * HD)
                    k += 1
                release(f.mm, k)
                arrived(a1_)
                for n in range(NT):
                    tokens(f, ODD_IN, k, a1_, c1, n, 0, 384)
                    k += 1
                features(f, ODD_IN, k, a1_, c1, 320, MLA)
                k += 1
                release(f.mm, k)
                arrived(a2)
                for g in range(4):
                    features(f, ODD_IN, k, a2, c2, g * P)
                    k += 1
                release(f.mm, k)
                for t in range(3):
                    bank_emptied(f, ODD_IN + "vvv", k + t)
                    for n in range(NT):
                        pe.wait_ge(f.s, n + 1)
                        mm = nc.tensor.transpose(banks[(k + t) % 8][:, n * P:(n + 1) * P],
                                                 cqkv[:, n, t * P:(t + 1) * P], ident)
                    mm.then_inc(f.mm, 1)

            def latent():
                f = F["latent"]
                (aq, cq_), = by_name["odd_w_uq_2"]
                (akv, ckv_), = by_name["odd_w_ukv_2"]
                uq, ukv = slot_view(aq, cq_), slot_view(akv, ckv_)
                turn = operand["turn"][0:MLA, :]
                nc.tensor.matmul(banks[0][0:MLA, :], turn, krT[0:MLA, :], start=True, stop=True).then_inc(f.mm, 1)
                arrived(aq)
                k = 1
                for h in range(8):
                    bank_emptied(f, LATENT, k)
                    product(banks[k % 8][0:MLA, :], [(uq[:, t, h * MLA:(h + 1) * MLA], cqT[:, t, :]) for t in range(2)])\
                        .then_inc(f.mm, 1)
                    bank_emptied(f, LATENT, k + 1)
                    pe.wait_ge(f.a, h + 1)
                    nc.tensor.matmul(banks[(k + 1) % 8][0:MLA, :], turn, raw[0:MLA, h % 2, :], start=True, stop=True)\
                        .then_inc(f.mm, 1)
                    k += 2
                release(f.mm, k)
                arrived(akv)
                for h in range(8):
                    bank_emptied(f, LATENT, k)
                    nc.tensor.matmul(banks[k % 8][0:HD, :], ukv[:, 0, h * P:h * P + HD], ckvT, start=True, stop=True)\
                        .then_inc(f.mm, 1)
                    k += 1
                v_cols = ukv[:, 0, :].rearrange("p (h d) -> p h d", h=8)[:, :, HD:P]
                for n in range(NT):
                    bank_emptied(f, LATENT, k)
                    nc.tensor.matmul(banks[k % 8][:, :], ckvT[:, n * P:(n + 1) * P], v_cols, start=True, stop=True)\
                        .then_inc(f.mm, 1)
                    k += 1
                release(f.mm, k)

            run = {
                "norm1": norm1, "project": project, "mixers": mixers, "hgrn": hgrn, "mix_out": mix_out,
                "up": up, "down": down, "gate": gate, "even_in": even_in,
                "even_a": lambda: attend("even_a"), "even_b": lambda: attend("even_b"), "even_out": even_out,
                "route0": lambda: route(0), "experts0": lambda: experts(0), "combine0": lambda: combine(0),
                "odd_in": odd_in, "odd_c": lambda: attend("odd_c"), "latent": latent,
                "odd_d": lambda: attend("odd_d"), "odd_out": odd_out,
                "overflow0": lambda: overflow(0),
                "overflow1": lambda: overflow(1), "route1": lambda: route(1), "experts1": lambda: experts(1), "combine1": lambda: combine(1),
            }
            for s in stages:
                if s in run:
                    run[s]()
                meet()

        @block.scalar
        def _(act):
            meets = [0]
            steps = [0]

            def meet():
                meets[0] += 1
                act.drain().then_inc(met, 1)
                act.wait_ge(met, 4 * meets[0])
                act.drain()

            def step(ins):
                ins.then_inc(act_step, 1)
                steps[0] += 1
                act.wait_ge(act_step, steps[0])

            A = nc.scalar.activation

            def scaled(out_, in_, s):
                return A(out_, in_, ACT.Identity, scale=s) if s is not None else A(out_, in_, ACT.Copy)

            def unflip(f, mm0, g=None):
                for k in range(0, KD, 2):
                    act.wait_ge(f.mm, mm0 + k + 1)
                    scaled(xT[:, k, :], banks[k][:, :], g[:, k:k + 1] if g is not None else None).then_inc(f.a, 1)

            def root_tile(stage, n):
                act.wait_ge(tile_var, norm_base[stage] + n + 1)
                A(rstd[:, n:n + 1], rstd[:, n:n + 1], ACT.Sqrt).then_inc(tile_sd, 1)

            def take_tile(stage, n):
                act.wait_ge(tile_turned, norm_base[stage] + n + 1)
                for j in range(2):
                    ins = A(xT[:, 4 * j:4 * j + 4, n * P:(n + 1) * P],
                            banks[turn_bank(stage, n) + j][:, :].rearrange("p (t q) -> p t q", t=4), ACT.Copy)
                ins.then_inc(tile_taken, 1)

            def norm_tiles(stage, before=None):
                for n in range(NT + 2):
                    if n < NT:
                        if before:
                            before(n)
                        root_tile(stage, n)
                    if n >= 2 and stage not in FEATURE_GAIN and stage != "combine1":
                        take_tile(stage, n - 2)
                if stage in ("even_out", "odd_out"):
                    act.wait_ge(routed, NT if stage == "even_out" else 2 * NT)
                    A(aff.rearrange("p a b -> p (a b)"), banks[4][:, 0:NT * E], ACT.Sigmoid)

            def norm1():
                f = F["norm1"]
                act.wait_ge(x_loaded, 16)
                for n in range(NT):
                    A(normed[:, n, :], x[:, n, :], ACT.Square, accum_out=sumsq[:, n:n + 1]).then_inc(f.a, 1)
                act.wait_ge(f.s, 1)
                A(rstd, rstd, ACT.Sqrt).then_inc(f.a, 1)
                act.wait_ge(pack_loaded["one"], 16)
                unflip(f, 0, operand["norm1"])

            def combine(l):
                def weigh_first(n):
                    act.wait_ge(rows_gathered[n], 32 * (l + 1))
                    A(y_rows[:, 0, n, :], y_rows[:, 0, n, :], ACT.Copy, scale=weight[:, 0, n:n + 1]).then_inc(first_weighed, 1)

                norm_tiles(f"combine{l}", weigh_first)

            def evacuate(f, plan, jobs, then={}):
                for k, who in enumerate(plan):
                    if who == "a":
                        act.wait_ge(f.mm, k + 1)
                        ins = None
                        for out_, in_, func, s in jobs(k, banks[k % 8]):
                            ins = A(out_, in_, func, scale=s) if s is not None else A(out_, in_, func)
                        ins.then_inc(f.a, 1)
                        if k in then:
                            then[k]()

            def project():
                def jobs(k, bank):
                    if k < 4:
                        return [(zA[:, k, :], bank[:, :], ACT.Gelu_apprx_tanh, None)]
                    if k < 8:
                        return [(zB[:, k - 4, :], bank[:, :], ACT.Gelu_apprx_tanh, None)]
                    if k < 12:
                        return [(zC[:, k - 8, :], bank[:, :], ACT.Silu if k < 10 else ACT.Sigmoid, None)]
                    return [(zC[:, k - 8, :], bank[:, :], ACT.Silu, None)]
                def parameters():
                    step(A(lam_e, operand["lam"], ACT.Abs))
                    A(lam_e, lam_e, ACT.Exp, scale=-1.0).then_inc(M["lam_exp"], 1)
                    act.wait_ge(M["lb_in"], 1)
                    A(lb0, lb0, ACT.Exp).then_inc(M["lb_exp"], 1)
                    act.wait_ge(M["var_ready"], 1)
                    A(rstd, rstd, ACT.Sqrt).then_inc(M["sd_ready"], 1)

                evacuate(F["project"], PROJECT, jobs, {7: parameters})

            def mixers():
                act.wait_ge(M["gates_mm"], 4)
                for t in range(2):
                    A(log_decay[:, t, :], banks[t][:, :], ACT.Sigmoid, bias=operand["ba"][:, t:t + 1]).then_inc(M["r_ready"], 1)
                for t in range(2):
                    A(gate_i[:, t, :], banks[2 + t][:, :], ACT.Sigmoid, bias=operand["bx"][:, t:t + 1]).then_inc(M["i_ready"], 1)
                act.wait_ge(M["decay_ready"], 2)
                for t in range(2):
                    A(decay[:, t, :], log_decay[:, t, :], ACT.Exp)
                    A(tanh_d[:, t, :], log_decay[:, t, :], ACT.Tanh).then_inc(M["decay_exp"], 1)
                for t in range(2):
                    act.wait_ge(M["mult_in"], t + 1)
                    A(tanh_d[:, t, :], tanh_d[:, t, :], ACT.Sqrt, scale=-1.0).then_inc(M["mult_ready"], 1)
                for t in range(2):
                    act.wait_ge(M["yD_mm"], t + 1)
                    scaled(mixT[:, 6 + t, :], banks[2 + t][:, :], operand["dscale"][:, t:t + 1])
                for t in range(2):
                    act.wait_ge(M["yA_mm"], t + 1)
                    scaled(mixT[:, t, :], banks[t][:, :], None)

            def hgrn():
                for pr in range(2):
                    act.wait_ge(M["hg_gate"], pr + 1)
                    A(log_f, zC[:, 2 + pr, :], ACT.Ln).then_inc(M["hg_log"], 1)
                    act.wait_ge(M["hg_decays"], pr + 1)
                    A(exp_b, bb, ACT.Exp).then_inc(M["hg_exp"], 1)
                    A(exp_end, to_end, ACT.Exp).then_inc(M["hg_exp"], 1)
                    A(decay_c[:, 1:NC], bb[:, HC - 1:T - 1:HC], ACT.Exp).then_inc(M["hg_exp"], 1)
                    act.wait_ge(M["hg_kT_mm"], 2 * pr + 2)
                    scaled(keT.rearrange("p a b -> p (a b)"), banks[0][:, :], None).then_inc(M["hg_kT"], 1)
                    scaled(vT.rearrange("p a b -> p (a b)"), banks[1][:, :], None).then_inc(M["hg_kT"], 1)
                    def decay_of(qt):
                        act.wait_ge(M["hg_diff"], NT * pr + qt + 1)
                        A(pairs[qt % 2], pairs[qt % 2], ACT.Exp).then_inc(M["hg_decay"], 1)

                    decay_of(0)
                    decay_of(1)
                    for n in range(NT):
                        act.wait_ge(M["hg_state_mm"], 2 * (NT * pr + n) + 2)
                        for i in (2 * n, 2 * n + 1):
                            m = 8 if i < 7 else 7
                            c0 = 8 * i + 1
                            scaled(state[:, :, c0:c0 + m],
                                   banks[(2 + i) % 4][:, 0:m * HD].rearrange("p (c v) -> p v c", v=HD), None)\
                                .then_inc(M["hg_state_in"], 1)
                        if n in (1, 2):
                            decay_of(n + 1)
                    A(decay_rows.rearrange("p (v c) -> p v c", c=NC), decay_c.unsqueeze(1).to_broadcast([P, HD // 2, NC]),
                      ACT.Copy).then_inc(M["hg_decay_rows"], 1)
                    act.wait_ge(M["hg_mean"], pr + 1)
                    A(exp_b, exp_b, ACT.Sqrt).then_inc(M["hg_sd"], 1)

            def up():
                f = F["up"]
                w3 = operand["fconv_w"].rearrange("p (f t) -> p f t", t=3)
                for k in range(2 * FT + 1):
                    if k < 2 * FT:
                        act.wait_ge(f.mm, k + 1)
                        if 4 <= k < FT + 4:
                            act.wait_ge(f.s, k - 3)
                        if k - 4 >= FT:
                            act.wait_ge(val_scaled, k - 4 - FT + 1)
                        A(conv[:, k % 4, :], banks[k % 8][:, :], ACT.Identity, bias=operand["fconv_b"][:, k:k + 1],
                          scale=w3[:, k, 2:3]).then_inc(f.a, 1)
                    if 1 <= k <= FT:
                        act.wait_ge(f.v, k)
                        A(hidden[:, k - 1, :], conv[:, (k - 1) % 4, :], ACT.Gelu_apprx_tanh).then_inc(f.s, 1)

            def gate():
                f = F["gate"]

                def opened(i):
                    act.wait_ge(f.mm, 2 * i + 2)
                    if i >= 2:
                        act.wait_ge(f.v, i - 1)
                    A(gate_s[:, i % 2, :], banks[(2 * i + 1) % 8][:, :], ACT.Sigmoid).then_inc(f.a, 1)

                for i in range(NT):
                    opened(i)
                norm_tiles("gate", lambda n: opened(NT + n))

            def even_in():
                def jobs(k, bank):
                    if k < 4:
                        return [(qA[(h // 4) * HD:(h // 4 + 1) * HD, h % 4, :], bank[(h % 2) * HD:(h % 2 + 1) * HD, :],
                                 ACT.Copy, HD ** -0.5) for h in (2 * k, 2 * k + 1)]
                    if k < 9:
                        return [(vA[:, k - 5, :], bank[:, 0:P], ACT.Copy, None)]
                    return [(kB[r, 2 * (k - 13) + hh, :], bank[r, :], ACT.Copy, None)
                            for hh, r in enumerate((slice(0, HD), slice(HD, P)))]
                f = F["even_in"]
                evacuate(f, EVEN_IN, jobs)
                act.wait_ge(f.s, 1)
                step(A(soft[0:8, 1, :], soft[0:8, 0, :], ACT.Abs))
                step(A(soft[0:8, 1, :], soft[0:8, 1, :], ACT.Exp, scale=-1.0))
                A(soft[0:8, 1, :], soft[0:8, 1, :], ACT.Ln, bias=1.0).then_inc(f.a, 1)

            def attend(stage):
                kind = KIND[stage]
                base = 32 * list(KIND).index(stage)

                def soft_max(i):
                    n, h = UNITS[i]
                    u = base + i
                    w_ = span(kind, n)[1]
                    g = u // 8
                    if h == 0 and g >= 2:
                        act.wait_ge(out_ready, g - 1)
                    act.wait_ge(shifted, u + 1)
                    if kind == "A":
                        A(sinkexp[:, g % 2, h:h + 1], operand["sinks"][:, h:h + 1], ACT.Exp, bias=negmax[:, u % 8:u % 8 + 1])
                    A(logits[:, u % 3, 0:w_], logits[:, u % 3, 0:w_], ACT.Exp, bias=negmax[:, u % 8:u % 8 + 1],
                      accum_out=rowsum[:, g % 2, h:h + 1]).then_inc(probs_done, 1)

                def take_probs(i):
                    n, h = UNITS[i]
                    u = base + i
                    w_ = span(kind, n)[1]
                    act.wait_ge(probsT_done, u + 1)
                    if u >= 2:
                        act.wait_ge(out_done, u - 1)
                    A(probsT[:, u % 2, 0:w_], banks[3 + u % 2][:, 0:w_], ACT.Copy).then_inc(probsT_ready, 1)

                def take_out(n):
                    g = base // 8 + n
                    act.wait_ge(outT_done, g + 1)
                    t0 = 0 if kind in "AC" else 4
                    A(mixT[:, t0:t0 + 4, n * P:(n + 1) * P], banks[7][:, :].rearrange("p (t q) -> p t q", t=4),
                      ACT.Copy).then_inc(outT_ready, 1)

                for i in range(len(UNITS) + 5):
                    if 2 <= i < len(UNITS) + 2:
                        take_probs(i - 2)
                    if i < len(UNITS):
                        soft_max(i)
                    if i >= 12 and (i - 12) % 8 == 0:
                        take_out((i - 12) // 8)

            def take_x(done):
                for g in range(2):
                    act.wait_ge(xgT_done, done + g + 1)
                    A(xgT[:, 4 * g:4 * g + 4, :].rearrange("p a b -> p (a b)"), banks[g][:, :], ACT.Copy).then_inc(xgT_ready, 1)

            def experts(l):
                if l == 0:
                    act.sem_inc(y_ready, 2)
                    act.sem_inc(y_stored[0], 16)
                    act.sem_inc(y_stored[1], 16)
                take_x(34 * l)
                enter(E * l, 34 * l + 2)
                with act.Fori(0, E // 2 - 1) as it:
                    for b in range(2):
                        e = it * 2 + (E * l + b + 1)
                        enter(e, it * 4 + (34 * l + 2 * b + 4))
                        leave(e - 1, b, it * 16 + (128 * l + 16), it * (2 * P) + b * P)
                e = E * (l + 1) - 1
                enter(e, 34 * l + 2 * E)
                leave(e - 1, 0, 128 * (l + 1), (E - 2) * P)
                leave(e, 1, 128 * (l + 1), (E - 1) * P)
                for b in range(2):
                    act.wait_ge(y_stored[b], 128 * (l + 1) + 16)

            def enter(e, turned_):
                act.wait_ge(gate_up_done, 2 * e + 1)
                A(silu_g, banks[2][:, :], ACT.Silu).then_inc(silu_ready, 1)
                take_x(turned_)

            def leave(e, b, stored_, row):
                act.wait_ge(y_stored[b], stored_)
                for j in range(2):
                    act.wait_ge(y_done, 2 * e + 1 + j)
                    A(y_sb[:, b, j * 512:(j + 1) * 512], banks[5 + j][:, :], ACT.Copy).then_inc(y_ready, 1)
                act.wait_ge(y_ready, 2 * e + 4)
                act.dma_start(y_dram[bass.ds(row, P), :], y_sb[:, b, :]).then_inc(y_stored[b], 16)

            def overflow(l):
                n, done = slots_of(act, l)
                with act.If(n > 0):
                    with act.Fori(0, n) as slot:
                        j = slot + done
                        for g in range(2):
                            act.wait_ge(over["xT_mm"], j * 2 + g + 1)
                            A(xgT[:, 4 * g:4 * g + 4, :].rearrange("p a b -> p (a b)"), banks[g][:, :], ACT.Copy)\
                                .then_inc(over["xT"], 1)
                        act.wait_ge(over["gate_up_mm"], j * 2 + 1)
                        A(silu_g, banks[2][:, :], ACT.Silu).then_inc(over["silu"], 1)
                        for g in range(2):
                            act.wait_ge(over["y_mm"], j * 2 + g + 1)
                            step_in(A(y_sb[:, 0, g * 512:(g + 1) * 512], banks[5 + g][:, :], ACT.Copy), j * 2 + g + 1)
                        act.dma_start(y_dram[bass.ds(slot * P + E * P, P), :], y_sb[:, 0, :]).then_inc(over["stored"], 16)
                    act.wait_ge(over["stored"], (n + done) * 16 + 16)
                    act.sem_inc(over["all_stored"], 1)

            def step_in(ins, value):
                ins.then_inc(over["y"], 1)
                act.wait_ge(over["y"], value)

            def odd_in():
                def jobs(k, bank):
                    if k < 7:
                        return [(wI[:, k - 3, :], bank[:, 0:4], ACT.Copy, 0.5)]
                    if k < 19:
                        i = k - 7
                        n, h = INDEX[i]
                        if i >= 3:
                            act.wait_ge(relu_used, i - 2)
                        return [(relu_d[:, i % 3, 0:(n + 1) * P], bank[:, 0:(n + 1) * P], ACT.Relu, HD ** -0.5)]
                    if k == 19:
                        return [(kC[0:HD, 0, :], bank[0:HD, :], ACT.Copy, None), (kC[HD:P, 1, :], bank[0:HD, :], ACT.Copy, None)]
                    if k < 24:
                        return [(vC[:, k - 20, :], bank[:, 0:HD], ACT.Copy, None)]
                    if k < 28:
                        return [(cqkv[:, k - 24, :], bank[:, 0:384], ACT.Copy, None)]
                    if k == 28:
                        return [(krT[0:MLA, :], bank[0:MLA, :], ACT.Copy, None)]
                    return [(qC[:, k - 29, :], bank[:, :], ACT.Copy, HD ** -0.5)]
                f = F["odd_in"]

                def squared():
                    for n in range(NT):
                        act.wait_ge(f.a, ODD_IN[:25 + n].count("a"))
                        A(squares[:, n, 0:256], cqkv[:, n, 0:256], ACT.Square, accum_out=sumsq[:, n:n + 1])
                        A(squares[:, n, 256:384], cqkv[:, n, 256:384], ACT.Square, accum_out=mean[:, n:n + 1])\
                            .then_inc(odd_sq, 1)

                evacuate(f, ODD_IN, jobs, {28: squared})
                act.wait_ge(odd_var, 1)
                A(rstd, sumsq, ACT.Sqrt)
                A(wide_stat, mean, ACT.Sqrt).then_inc(odd_sq, 1)

            def latent():
                f, k = F["latent"], 0
                for k, who in enumerate(LATENT):
                    if who != "a":
                        continue
                    act.wait_ge(f.mm, k + 1)
                    if k < 17:
                        h = (k - 1) // 2
                        if h >= 2:
                            act.wait_ge(f.s, h - 1)
                        A(raw[0:MLA, h % 2, :], banks[k % 8][0:MLA, :], ACT.Copy, scale=MLA ** -0.5).then_inc(f.a, 1)
                    else:
                        A(kD[0:HD, k - 17, :], banks[k % 8][0:HD, :], ACT.Copy).then_inc(f.a, 1)

            def start():
                act.dma_start(pack_area["base"][:, :], w["pack_base"]).then_inc(pack_loaded["base"], 16)
                act.dma_start(pack_area["one"], w["pack_one"]).then_inc(pack_loaded["one"], 16)

            run = {
                "norm1": norm1, "project": project, "mixers": mixers, "hgrn": hgrn,
                "mix_out": lambda: norm_tiles("mix_out"), "up": up, "down": lambda: norm_tiles("down"), "gate": gate,
                "even_in": even_in, "even_a": lambda: attend("even_a"), "even_b": lambda: attend("even_b"),
                "even_out": lambda: norm_tiles("even_out"), 
                "experts0": lambda: experts(0), "combine0": lambda: combine(0),
                "odd_in": odd_in, "odd_c": lambda: attend("odd_c"), "latent": latent,
                "odd_d": lambda: attend("odd_d"), "odd_out": lambda: norm_tiles("odd_out"),
                "overflow0": lambda: overflow(0),
                "overflow1": lambda: overflow(1), "experts1": lambda: experts(1),
                "combine1": lambda: combine(1),
            }
            start()
            for s in stages:
                if s in run:
                    run[s]()
                meet()

        @block.vector
        def _(dve):
            meets = [0]
            steps = [0]
            V = nc.vector

            def meet():
                meets[0] += 1
                dve.drain().then_inc(met, 1)
                dve.wait_ge(met, 4 * meets[0])
                dve.drain()

            def step(ins):
                ins.then_inc(dve_step, 1)
                steps[0] += 1
                dve.wait_ge(dve_step, steps[0])

            def mul_add(out_, in0, s, in1):
                return V.scalar_tensor_tensor(out_, in0, s, in1, ALU.mult, ALU.add)

            def scaled(out_, in_, s):
                return V.tensor_scalar(out_, in_, s, None, ALU.mult) if s is not None else V.tensor_copy(out_, in_)

            def unflip(f, mm0, g=None):
                for k in range(1, KD, 2):
                    dve.wait_ge(f.mm, mm0 + k + 1)
                    scaled(xT[:, k, :], banks[k][:, :], g[:, k:k + 1] if g is not None else None)

            def norm1():
                f = F["norm1"]
                dve.wait_ge(f.a, NT)
                V.tensor_scalar(rstd, sumsq, 1.0 / D, EPS, ALU.mult, ALU.add).then_inc(f.s, 1)
                dve.wait_ge(f.a, NT + 1)
                step(V.reciprocal(rstd, rstd))
                for n in range(NT):
                    V.tensor_scalar(normed[:, n, :], x[:, n, :], rstd[:, n:n + 1], None, ALU.mult).then_inc(f.v, 1)
                dve.wait_ge(pack_loaded["one"], 16)
                unflip(f, 0, operand["norm1"])

            def norm_tile(stage, n, loads=0):
                base = norm_base[stage] + n
                for h in range(2):
                    step(V.bn_stats(bn[:, h, :], x[:, n, h * 512:(h + 1) * 512]))
                step(V.bn_aggr(mv[:, n, :], bn.rearrange("p h t -> p (h t)")))
                r, mu, var = rstd[:, n:n + 1], mv[:, n, 0:1], mv[:, n, 1:2]
                root_mean = base < norm_base["even_out"]
                if root_mean:
                    step(V.scalar_tensor_tensor(var, mu, mu, var, ALU.mult, ALU.add))
                V.tensor_scalar(r, var, EPS if root_mean else LN_EPS, None, ALU.add).then_inc(tile_var, 1)
                dve.wait_ge(tile_sd, base + 1)
                step(V.reciprocal(r, r))
                if loads:
                    dve.wait_ge(rows_loaded, 16 * loads)
                if stage in FEATURE_GAIN:
                    if n >= 2:
                        dve.wait_ge(tile_turned, base - 1)
                    V.tensor_scalar(tile_normed[:, n % 2, :], x[:, n, :], r, None, ALU.mult).then_inc(tile_ready, 1)
                elif root_mean:
                    V.scalar_tensor_tensor(x[:, n, :], x[:, n, :], r, rowsG, ALU.mult, ALU.mult).then_inc(tile_ready, 1)
                else:
                    step(V.tensor_scalar(x[:, n, :], x[:, n, :], mu, r, ALU.subtract, ALU.mult))
                    gained = V.tensor_tensor(x[:, n, :], x[:, n, :], rowsG, ALU.mult)
                    if stage.startswith("combine"):
                        gained.then_inc(tile_gained, 1)
                    else:
                        step(gained)
                        V.tensor_tensor(x[:, n, :], x[:, n, :], rowsB, ALU.add).then_inc(tile_ready, 1)

            def take_tile(stage, n):
                dve.wait_ge(tile_turned, norm_base[stage] + n + 1)
                for j in range(2):
                    gain = FEATURE_GAIN[stage][:, 4 * j:4 * j + 4].unsqueeze(2).to_broadcast([P, 4, P])
                    ins = V.tensor_tensor(xT[:, 4 * j:4 * j + 4, n * P:(n + 1) * P],
                                          banks[turn_bank(stage, n) + j][:, :].rearrange("p (t q) -> p t q", t=4),
                                          gain, ALU.mult)
                ins.then_inc(tile_taken, 1)

            def residual(name, scale, loads=0):
                f = F[name]
                for k in range(10):
                    if k < 8:
                        dve.wait_ge(f.mm, (20 if k >= 4 else 8) + k % 4 + 1 if name == "down" else k + 1)
                        r = x[:, k % 4, (k // 4) * 512:(k // 4 + 1) * 512]
                        mul_add(r, r, scale, banks[k][:, :]).then_inc(f.v, 1)
                        if k >= 4:
                            dve.wait_ge(f.v, k + 1)
                            norm_tile(name, k - 4, loads)
                    if k >= 6 and name in FEATURE_GAIN:
                        take_tile(name, k - 6)

            def evacuate(f, plan, jobs, then={}):
                for k, who in enumerate(plan):
                    if who == "v":
                        dve.wait_ge(f.mm, k + 1)
                        for out_, in_, s in jobs(k, banks[k % 8]):
                            ins = scaled(out_, in_, s)
                        ins.then_inc(f.v, 1)
                        if k in then:
                            then[k]()

            def project():
                def jobs(k, bank):
                    if k < 6:
                        return [(zB[:, k - 4, :], bank[:, :], None)]
                    if k < 14:
                        return [(zC[:, k - 8, :], bank[:, :], None)]
                    return [(zD[:, k - 16, :], bank[:, :], None)]

                def first_mixers():
                    dve.wait_ge(F["project"].v, 2)
                    cw = operand["bconv_w"].rearrange("p (t k) -> p t k", k=4)
                    for t in range(2):
                        step(V.tensor_scalar(xc[:, t, :], zB[:, t, :], cw[:, t, 3:4], operand["bconv_b"][:, t:t + 1],
                                             ALU.mult, ALU.add))
                        for s in (1, 2):
                            step(mul_add(xc[:, t, s:], zB[:, t, 0:T - s], cw[:, t, 3 - s:4 - s], xc[:, t, s:]))
                        mul_add(xc[:, t, 3:], zB[:, t, 0:T - 3], cw[:, t, 0:1], xc[:, t, 3:]).then_inc(M["conv_done"], 1)
                    step(V.tensor_tensor(lb0, operand["lb"], operand["lb"], ALU.subtract))
                    V.tensor_scalar(lb0, lb0, 0.0, None, ALU.add).then_inc(M["lb_in"], 1)
                    dve.wait_ge(F["project"].a, NT)
                    for n in range(NT):
                        step(V.bn_stats(bn[:, 0, :], zA[:, n, 256:512]))
                        step(V.bn_aggr(mv[:, n, :], bn[:, 0, :]))
                    V.tensor_scalar(rstd, mv[:, :, 1], EPS, None, ALU.add).then_inc(M["var_ready"], 1)

                def parameters():
                    dve.wait_ge(M["lam_exp"], 1)
                    step(V.tensor_scalar(lam_s, lam_e, 2.0, None, ALU.add))
                    step(V.reciprocal(lam_s, lam_s))
                    step(V.tensor_tensor(lam_s, lam_s, lam_e, ALU.mult))
                    step(V.tensor_tensor(lam_q, lam_s, lam_s, ALU.mult))
                    step(V.tensor_scalar(lam_p, lam_q, 1.0 / 17, None, ALU.mult))
                    for m in (15, 13, 11, 9, 7, 5, 3):
                        step(V.scalar_tensor_tensor(lam_p, lam_p, 1.0 / m, lam_q, ALU.add, ALU.mult))
                    step(V.scalar_tensor_tensor(lam_p, lam_p, 1.0, lam_s, ALU.add, ALU.mult))
                    step(V.tensor_scalar(lam_c, operand["lam"], -1.0, 0.0, ALU.mult, ALU.max))
                    step(mul_add(lam_c, lam_p, 2.0, lam_c))
                    step(V.tensor_scalar(lam_c, lam_c, -8.0, None, ALU.mult))
                    dve.wait_ge(M["lb_exp"], 1)
                    step(V.reciprocal(omlb, lb0))
                    step(V.tensor_tensor(lb0, lb0, omlb, ALU.mult))
                    step(V.tensor_tensor(lb0, lb0, lb0, ALU.subtract))
                    step(V.tensor_scalar(omlb, lb0, -1.0, 1.0, ALU.mult, ALU.add))
                    dve.wait_ge(M["sd_ready"], 1)
                    step(V.reciprocal(rstd, rstd))
                    for n in range(NT):
                        v_ = zA[:, n, 256:512]
                        step(V.tensor_scalar(v_, v_, mv[:, n, 0:1], rstd[:, n:n + 1], ALU.subtract, ALU.mult))
                        step(V.tensor_tensor(v_, v_, operand["aln_g"], ALU.mult))
                        V.tensor_tensor(v_, v_, operand["aln_b"], ALU.add).then_inc(M["vn_ready"], 1)

                evacuate(F["project"], PROJECT, jobs, {5: first_mixers, 13: parameters})

            def mixers():
                V.tensor_copy(sums0[:, :, 0:1], zD[:, :, 0:1])
                step(V.tensor_tensor(sums0[:, :, 1:], zD[:, :, 1:], zD[:, :, 0:T - 1], ALU.add))
                V.tensor_copy(sums1[:, :, 0:2], sums0[:, :, 0:2])
                step(V.tensor_tensor(sums1[:, :, 2:], sums0[:, :, 2:], sums0[:, :, 0:T - 2], ALU.add))
                V.tensor_copy(sums0[:, 1, 0:4], sums1[:, 1, 0:4])
                step(V.tensor_tensor(sums0[:, 1, 4:], sums1[:, 1, 4:], sums1[:, 1, 0:T - 4], ALU.add))
                V.tensor_copy(sums1[:, 1, 0:8], sums0[:, 1, 0:8])
                step(V.tensor_tensor(sums1[:, 1, 8:], sums0[:, 1, 8:], sums0[:, 1, 0:T - 8], ALU.add))
                count = operand["count"].rearrange("p (t c) -> p t c", c=16)
                for half_, s in enumerate((sums0, sums1)):
                    r = slice(half_ * HD, (half_ + 1) * HD)
                    for t in range(2):
                        V.scalar_tensor_tensor(pooled[r, t, 16:], s[r, t, 16:], operand["window_share"][r, t:t + 1],
                                               zD[r, t, 16:], ALU.mult, ALU.subtract)
                    step(V.tensor_tensor(s[r, :, 0:16], s[r, :, 0:16], count[r, :, :], ALU.mult))
                    V.tensor_tensor(pooled[r, :, 0:16], s[r, :, 0:16], zD[r, :, 0:16], ALU.subtract)\
                        .then_inc(M["pooled"], 1)
                for t in range(2):
                    dve.wait_ge(M["r_ready"], t + 1)
                    V.tensor_scalar(log_decay[:, t, :], log_decay[:, t, :], lam_c[:, t:t + 1], None, ALU.mult)\
                        .then_inc(M["decay_ready"], 1)
                for t in range(2):
                    dve.wait_ge(M["decay_exp"], t + 1)
                    step(V.tensor_tensor(log_decay[:, t, :], decay[:, t, :], decay[:, t, :], ALU.mult))
                    V.scalar_tensor_tensor(tanh_d[:, t, :], log_decay[:, t, :], 1.0, tanh_d[:, t, :], ALU.add, ALU.mult)\
                        .then_inc(M["mult_in"], 1)
                for t in range(2):
                    dve.wait_ge(M["i_ready"], t + 1)
                    step(V.tensor_tensor(gate_i[:, t, :], gate_i[:, t, :], xc[:, t, :], ALU.mult))
                    dve.wait_ge(M["mult_ready"], t + 1)
                    step(V.tensor_tensor(gate_i[:, t, :], gate_i[:, t, :], tanh_d[:, t, :], ALU.mult))
                    step(V.tensor_tensor_scan(log_decay[:, t, :], decay[:, t, :], gate_i[:, t, :], 0.0, ALU.mult, ALU.add))
                    V.tensor_tensor(mixT[:, 2 + t, :], log_decay[:, t, :], zB[:, 2 + t, :], ALU.mult)
                for n in range(NT):
                    dve.wait_ge(M["spatial_mm"], n + 1)
                    for h in range(4):
                        c = slice(h * HD, (h + 1) * HD)
                        ins = V.scalar_tensor_tensor(zA[:, n, c], banks[4 + n][:, c], operand["bs"][:, h:h + 1],
                                                     zA[:, n, c], ALU.add, ALU.mult)
                    ins.then_inc(M["yA_ready"], 1)

            def hgrn():
                def chunks(a, q0=0, q=NC):
                    return a.rearrange("p (c j) -> p c j", j=HC)[:, q0:q0 + q, :]
                for pr in range(2):
                    f_ = zC[:, 2 + pr, :]
                    step(V.tensor_scalar(f_, f_, omlb[:, pr:pr + 1], lb0[:, pr:pr + 1], ALU.mult, ALU.add))
                    V.memset(decay_c[:, 0:1], 0.0)
                    V.memset(state[:, :, 0:1], 0.0).then_inc(M["hg_gate"], 1)
                    dve.wait_ge(M["hg_log"], pr + 1)
                    V.tensor_scalar(f_, f_, -1.0, 1.0, ALU.mult, ALU.add)
                    step(V.tensor_tensor_scan(bb, operand["inside"], log_f, 0.0, ALU.mult, ALU.add))
                    V.tensor_tensor(chunks(to_end), chunks(bb)[:, :, HC - 1:HC].to_broadcast([P, NC, HC]), chunks(bb),
                                    ALU.subtract).then_inc(M["hg_decays"], 1)
                    dve.wait_ge(M["hg_exp"], 3 * pr + 3)
                    V.tensor_tensor(qe, zC[:, pr, :], exp_b, ALU.mult)
                    V.tensor_tensor(ke, f_, exp_end, ALU.mult).then_inc(M["hg_exps"], 1)
                    q4 = NC // NT
                    shape = [P, q4, HC, HC]
                    hm = operand["hmask"].rearrange("p (t s) -> p t s", s=HC).unsqueeze(1).to_broadcast(shape)

                    def quarter(qt):
                        c0 = q4 * qt
                        return (pairs[qt % 2].rearrange("p (c t s) -> p c t s", t=HC, s=HC),
                                lambda a: chunks(a, c0, q4).unsqueeze(3).to_broadcast(shape),
                                lambda a: chunks(a, c0, q4).unsqueeze(2).to_broadcast(shape))

                    def differ(qt):
                        pd, as_t, as_s = quarter(qt)
                        step(V.tensor_tensor(pd, as_t(bb), as_s(bb), ALU.subtract))
                        V.tensor_tensor(pd, pd, hm, ALU.min).then_inc(M["hg_diff"], 1)

                    def queries_keys(qt):
                        pd, as_t, as_s = quarter(qt)
                        dve.wait_ge(M["hg_decay"], NT * pr + qt + 1)
                        step(V.tensor_tensor(pd, pd, as_t(zC[:, pr, :]), ALU.mult))
                        V.tensor_tensor(pd, pd, as_s(f_), ALU.mult).then_inc(M["hg_att"], 1)

                    def values(qt):
                        pd, as_t, as_s = quarter(qt)
                        k = NT * pr + qt
                        dve.wait_ge(M["hg_att_mm"], k + 1)
                        for b in range(2):
                            part = slice(b * q4 // 2, (b + 1) * q4 // 2)
                            att = banks[4 + 2 * (k % 2) + b][:, :].rearrange("p (c t s) -> p c t s", t=HC, s=HC)
                            ins = V.tensor_tensor(pd[:, part], att, as_s(zC[:, 4 + pr, :])[:, part], ALU.mult)
                        ins.then_inc(M["hg_used"], 1)
                        dve.wait_ge(M["hg_used"], k + 1)
                        step(V.tensor_reduce(mixT[:, 4 + pr, qt * P:(qt + 1) * P],
                                             pairs[qt % 2].rearrange("p (t s) -> p t s", s=HC), AX.X, ALU.add))

                    differ(0)
                    differ(1)
                    queries_keys(0)
                    queries_keys(1)
                    values(0)
                    differ(2)
                    values(1)
                    differ(3)
                    queries_keys(2)
                    queries_keys(3)
                    dve.wait_ge(M["hg_state_in"], 8 * (pr + 1))
                    dve.wait_ge(M["hg_decay_rows"], pr + 1)
                    for i in range(2):
                        part = state[:, i * HD // 2:(i + 1) * HD // 2, :].rearrange("p v c -> p (v c)")
                        V.tensor_tensor_scan(part, decay_rows, part, 0.0, ALU.mult, ALU.add).then_inc(M["hg_state"], 1)
                    values(2)
                    values(3)
                    dve.wait_ge(M["hg_inter_mm"], pr + 1)
                    o = mixT[:, 4 + pr, :]
                    for hh in range(2):
                        r = slice(hh * HD, (hh + 1) * HD)
                        ins = V.tensor_tensor(o[r, :], banks[1 + hh][r, :], o[r, :], ALU.add)
                    step(ins)
                    V.tensor_tensor(o_sq, o, o, ALU.mult).then_inc(M["hg_square"], 1)
                    dve.wait_ge(M["hg_mean_mm"], pr + 1)
                    V.tensor_scalar(exp_b, banks[0][:, :], EPS, None, ALU.add).then_inc(M["hg_mean"], 1)
                    dve.wait_ge(M["hg_sd"], pr + 1)
                    step(V.reciprocal(exp_b, exp_b))
                    step(V.tensor_tensor(o, o, exp_b, ALU.mult))
                    step(V.scalar_tensor_tensor(o, o, operand["cnorm"][:, 0:1], zC[:, 6 + pr, :], ALU.mult, ALU.mult))

            def up():
                f = F["up"]
                w3 = operand["fconv_w"].rearrange("p (f t) -> p f t", t=3)
                for k in range(2 * FT):
                    c = conv[:, k % 4, :]
                    dve.wait_ge(f.a, k + 1)
                    step(mul_add(c[:, 1:], banks[k % 8][:, 0:T - 1], w3[:, k, 1:2], c[:, 1:]))
                    mul_add(c[:, 2:], banks[k % 8][:, 0:T - 2], w3[:, k, 0:1], c[:, 2:]).then_inc(f.v, 1)
                    if k >= FT:
                        dve.wait_ge(f.v, k + 1)
                        dve.wait_ge(f.s, k - FT + 1)
                        V.tensor_tensor(hidden[:, k - FT, :], hidden[:, k - FT, :], c, ALU.mult).then_inc(val_scaled, 1)

            def gate():
                f = F["gate"]
                for i in range(8):
                    dve.wait_ge(f.a, i + 1)
                    V.tensor_tensor(gate_t[:, i % 2, :], banks[(2 * i) % 8][:, :], gate_s[:, i % 2, :], ALU.mult)\
                        .then_inc(f.v, 1)
                    dve.wait_ge(f.v, i + 1)
                    r = x[:, i % 4, (i // 4) * 512:(i // 4 + 1) * 512]
                    step(V.tensor_tensor(r, r, gate_t[:, i % 2, :], ALU.add))
                    if i >= NT:
                        norm_tile("gate", i - NT, 1)

            def even_in():
                f = F["even_in"]

                def jobs(k, bank):
                    if k == 4:
                        return [(kA[r, hh, :], bank[r, :], None) for hh, r in enumerate((slice(0, HD), slice(HD, P)))]
                    if k < 13:
                        return [(qB[:, k - 9, :], bank[:, :], HD ** -0.5)]
                    return [(vB[:, k - 17, :], bank[:, :], None)]
                evacuate(f, EVEN_IN[:21], jobs)
                dve.wait_ge(f.mm, 22)
                V.tensor_scalar(soft[0:8, 0, :], banks[21 % 8][0:8, :], operand["fg_b"][0:8, 0:1], None, ALU.add)\
                    .then_inc(f.s, 1)
                dve.wait_ge(f.a, EVEN_IN.count("a") + 1)
                V.scalar_tensor_tensor(soft[0:8, 0, :], soft[0:8, 0, :], 0.0, soft[0:8, 1, :], ALU.min, ALU.subtract)\
                    .then_inc(f.s, 1)
                dve.wait_ge(f.s, 2)
                V.tensor_tensor_scan(cum[0:8, :], soft[0:8, 0, :], soft[0:8, 0, :], 0.0, ALU.add, ALU.bypass)\
                    .then_inc(f.s, 1)
                dve.wait_ge(f.s, 3)
                dve.wait_ge(keys_cleared, 1)
                V.tensor_scalar(negc[0:8, :], cum[0:8, :], -1.0, None, ALU.mult)
                dve.wait_ge(f.mm, 23)
                V.tensor_copy(cT.rearrange("p a b -> p (a b)"), banks[22 % 8][:, 0:32])

            def attend(stage):
                kind = KIND[stage]
                base = 32 * list(KIND).index(stage)
                slopes = alibi_slopes(8)

                def bias(i):
                    n, h = UNITS[i]
                    u = base + i
                    w_ = span(kind, n)[1]
                    c = slice(u % 8, u % 8 + 1)
                    l_, bank = logits[:, u % 3, 0:w_], banks[u % 3][:, 0:w_]
                    dve.wait_ge(scores_done, u + 1)
                    if u >= 3:
                        dve.wait_ge(probsT_done, u - 2)
                    mask = causal[:, T - w_:T]
                    if kind == "A":
                        ins = V.tensor_tensor(l_, bank, operand["window"][:, (h + 1) * 256 - w_:(h + 1) * 256], ALU.add)
                    elif kind == "B":
                        ins = V.scalar_tensor_tensor(l_, bank, cT[:, n, h:h + 1], mask, ALU.add, ALU.add)
                    elif kind == "C":
                        d0 = n * (n + 1) // 2
                        ins = mul_add(l_, distsel[:, d0:d0 + n + 1, :].rearrange("p a b -> p (a b)"), -float(slopes[h]), bank)
                    else:
                        ins = V.tensor_tensor(l_, bank, mask, ALU.add)
                    ins.then_inc(biased, 1)
                    dve.wait_ge(biased, u + 1)
                    step(V.tensor_reduce(rowmax[:, c], l_, AX.X, ALU.max))
                    low = operand["sinks"][:, h:h + 1] if kind == "A" else TAKEN
                    V.tensor_scalar(negmax[:, c], rowmax[:, c], low, -1.0, ALU.max, ALU.mult).then_inc(shifted, 1)

                def finish(n):
                    g = base // 8 + n
                    dve.wait_ge(out_done, base + 8 * (n + 1))
                    total_ = rowsum[:, g % 2, :]
                    if kind == "A":
                        step(V.tensor_tensor(recip, total_, sinkexp[:, g % 2, :], ALU.add))
                        total_ = recip
                    step(V.reciprocal(recip, total_))
                    if g >= 1:
                        dve.wait_ge(outT_done, g)
                    V.tensor_tensor(heads_out.rearrange("p (h d) -> p h d", h=8),
                                    banks[5 + g % 2][:, :].rearrange("p (h d) -> p h d", h=8),
                                    recip.unsqueeze(2).to_broadcast([P, 8, HD]), ALU.mult).then_inc(out_ready, 1)

                for i in range(len(UNITS) + 4):
                    if i >= 11 and (i - 11) % 8 == 0:
                        finish((i - 11) // 8)
                    if i < len(UNITS):
                        bias(i)

            def route(l):
                f = F[f"route{l}"]
                wide = [P, NT, E]
                g4 = lambda a: a.rearrange("p n (g i) -> p (n g) i", i=4)
                flat = lambda a: a.rearrange("p a b -> p (a b)")
                step(V.tensor_tensor(sel, aff, operand["router_b"].unsqueeze(1).to_broadcast(wide), ALU.add))

                def ranks(a, r, tmp):
                    step(V.memset(r, 0.0))
                    for d in (1, 2, 3):
                        c = tmp[:, :, 0:4 - d]
                        step(V.tensor_tensor(c, a[:, :, 0:4 - d], a[:, :, d:4], ALU.is_ge))
                        step(V.tensor_tensor(r[:, :, d:4], r[:, :, d:4], c, ALU.add))
                        step(V.scalar_tensor_tensor(r[:, :, 0:4 - d], r[:, :, 0:4 - d], 1.0, c, ALU.add, ALU.subtract))

                ranks(g4(sel), g4(rank), g4(cmp))
                step(V.tensor_scalar(flat(tmp16), flat(rank), 2.0, None, ALU.is_lt))
                step(V.tensor_tensor(flat(tmp16), flat(tmp16), flat(sel), ALU.mult))
                step(V.tensor_reduce(flat(gsum), g4(tmp16), AX.X, ALU.add))
                ranks(gsum, trank, gpick)
                step(V.tensor_scalar(flat(gpick), flat(trank), 0.0, None, ALU.is_equal))
                picked = flat(gpick).unsqueeze(2).to_broadcast([P, NT * 4, 4])
                for j, m in enumerate((first, second)):
                    step(V.tensor_scalar(flat(m), flat(rank), float(j), None, ALU.is_equal))
                    step(V.tensor_tensor(g4(m), g4(m), picked, ALU.mult))
                V.tensor_tensor(flat(chosen), flat(first), flat(second), ALU.add).then_inc(f.v, 1)
                dve.wait_ge(f.mm, 1)
                tot = banks[1][:, NT * E:(NT + 1) * E]
                need = operand["over_need"].rearrange("p (k e) -> p k e", e=E)
                step(V.tensor_tensor(flags, tot.unsqueeze(1).to_broadcast([P, 3, E]), need, ALU.is_gt))
                step(V.tensor_tensor_scan(flat(before_), flat(flags), flat(flags), 0.0, ALU.add, ALU.bypass))
                step(V.tensor_tensor(before_, before_, flags, ALU.subtract))
                step(V.scalar_tensor_tensor(flat(slot_row), flat(before_), float(P), operand["over_row"], ALU.mult, ALU.add))
                step(V.tensor_tensor(step_k[:, 0, :], slot_row[:, 0, :], operand["expert_row"], ALU.subtract))
                step(V.tensor_tensor(step_k[:, 1:3, :], slot_row[:, 1:3, :], slot_row[:, 0:2, :], ALU.subtract))
                ranked_n = banks[1][:, 0:NT * E].rearrange("p (n e) -> p n e", e=E)
                step(V.tensor_copy(ranked, ranked_n))
                step(V.tensor_tensor(posn, ranked, operand["expert_row"].unsqueeze(1).to_broadcast(wide), ALU.add))
                for k in (1, 2, 3):
                    step(V.tensor_scalar(flat(tmp16), flat(ranked), float(k * P), None, ALU.is_ge))
                    step(V.tensor_tensor(tmp16, tmp16, step_k[:, k - 1, :].unsqueeze(1).to_broadcast(wide), ALU.mult))
                    step(V.tensor_tensor(flat(posn), flat(posn), flat(tmp16), ALU.add))
                for j, m in enumerate((first, second)):
                    step(V.tensor_tensor(flat(tmp16), flat(m), flat(posn), ALU.mult))
                    step(V.tensor_reduce(r_place[:, j, :], tmp16, AX.X, ALU.add))
                V.tensor_copy(place[:, :, :], r_place).then_inc(f.s, 1)
                for j, m in enumerate((first, second)):
                    step(V.tensor_tensor(flat(tmp16), flat(m), flat(aff), ALU.mult))
                    step(V.tensor_reduce(weight[:, j, :], tmp16, AX.X, ALU.add))
                step(V.tensor_tensor(wsum, weight[:, 0, :], weight[:, 1, :], ALU.add))
                step(V.reciprocal(wsum, wsum))
                for j in range(2):
                    step(V.tensor_tensor(weight[:, j, :], weight[:, j, :], wsum, ALU.mult))
                V.tensor_tensor(over_n[:, l:l + 1], flat(before_)[:, 3 * E - 1:3 * E], flat(flags)[:, 3 * E - 1:3 * E], ALU.add)
                step(V.tensor_tensor(picked_e, flat(before_).unsqueeze(1).to_broadcast([P, 8, 3 * E]),
                                     operand["over_j"].unsqueeze(2).to_broadcast([P, 8, 3 * E]), ALU.is_equal))
                step(V.tensor_tensor(flat(hits), flat(flags), operand["over_e"], ALU.mult))
                step(V.tensor_tensor(picked_e, picked_e, flat(hits).unsqueeze(1).to_broadcast([P, 8, 3 * E]), ALU.mult))
                step(V.tensor_reduce(e_list, picked_e, AX.X, ALU.add))
                step(V.tensor_copy(over_list[:, :], e_list))

            def experts(l):
                with dve.Fori(0, E // 2) as it:
                    for b in range(2):
                        e = it * 2 + (E * l + b)
                        dve.wait_ge(gate_up_done, e * 2 + 2)
                        dve.wait_ge(silu_ready, e + 1)
                        V.tensor_tensor(hid, banks[3][:, :], silu_g, ALU.mult).then_inc(h_ready, 1)
                        dve.wait_ge(hT_done, e + 1)
                        V.tensor_copy(hidT.rearrange("p a b -> p (a b)"), banks[4][:, :]).then_inc(hT_ready, 1)

            def overflow(l):
                n, done = slots_of(dve, l)
                with dve.If(n > 0):
                    with dve.Fori(0, n) as slot:
                        j = slot + done
                        dve.wait_ge(over["gate_up_mm"], j * 2 + 2)
                        dve.wait_ge(over["silu"], j + 1)
                        V.tensor_tensor(hid, banks[3][:, :], silu_g, ALU.mult).then_inc(over["h"], 1)
                        dve.wait_ge(over["hT_mm"], j + 1)
                        V.tensor_copy(hidT.rearrange("p a b -> p (a b)"), banks[4][:, :]).then_inc(over["hT"], 1)

            def combine(l):
                for n in range(NT):
                    dve.wait_ge(rows_gathered[n], 32 * (l + 1))
                    dve.wait_ge(first_weighed, NT * l + n + 1)
                    step(mul_add(y_rows[:, 0, n, :], y_rows[:, 1, n, :], weight[:, 1, n:n + 1], y_rows[:, 0, n, :]))
                    step(mul_add(x[:, n, :], x[:, n, :], ALPHA, y_rows[:, 0, n, :]))
                    norm_tile(f"combine{l}", n, 3 + 4 * l + 2)

            def odd_in():
                f = F["odd_in"]

                def jobs(k, bank):
                    if k == 0:
                        return [(kI[0:HD, 0, :], bank[0:HD, :], None), (kI[HD:P, 1, :], bank[0:HD, :], None)]
                    return [(qI[:, k - 1, :], bank[:, :], None)]
                evacuate(f, ODD_IN, jobs)
                mul_add(distsel[:, 0, :], causal[:, T - P:T], -BIG / 1e30, operand["dist"][:, T - P:T])
                for i, (n, h) in enumerate(INDEX):
                    w_ = (n + 1) * P
                    dve.wait_ge(f.a, NT + i + 1)
                    if h == 0:
                        ins = V.tensor_scalar(score[n], relu_d[:, i % 3, 0:w_], wI[:, n, h:h + 1], None, ALU.mult)
                    else:
                        ins = mul_add(score[n], relu_d[:, i % 3, 0:w_], wI[:, n, h:h + 1], score[n])
                    ins.then_inc(relu_used, 1)
                    dve.wait_ge(relu_used, i + 1)
                for n in range(1, NT):
                    w_ = (n + 1) * P
                    s = score[n]
                    step(V.tensor_tensor(s, s, causal[:, T - w_:T], ALU.add))
                    for _ in range(TOPK // 8):
                        step(V.max(top8, s))
                        step(V.match_replace(s, top8, s, TAKEN))
                    d0 = n * (n + 1) // 2
                    step(V.tensor_scalar(s, s, -2e38, BIG, ALU.is_gt, ALU.mult))
                    V.tensor_tensor(distsel[:, d0:d0 + n + 1, :].rearrange("p a b -> p (a b)"), s,
                                    operand["dist"][:, T - w_:T], ALU.add)
                dve.wait_ge(odd_sq, NT)
                step(V.tensor_scalar(sumsq, sumsq, 1.0 / 256, EPS, ALU.mult, ALU.add))
                V.tensor_scalar(mean, mean, 1.0 / 128, EPS, ALU.mult, ALU.add).then_inc(odd_var, 1)
                dve.wait_ge(odd_sq, NT + 1)
                step(V.reciprocal(rstd, rstd))
                step(V.reciprocal(wide_stat, wide_stat))
                for n in range(NT):
                    V.tensor_scalar(cqkv[:, n, 0:256], cqkv[:, n, 0:256], rstd[:, n:n + 1], None, ALU.mult)
                    V.tensor_scalar(cqkv[:, n, 256:384], cqkv[:, n, 256:384], wide_stat[:, n:n + 1], None, ALU.mult)\
                        .then_inc(f.s, 1)
                for t in range(3):
                    dve.wait_ge(f.mm, 34 + t)
                    bank = banks[(33 + t) % 8][:, :]
                    if t < 2:
                        scaled(cqT[:, t, :], bank, operand["qnorm"][:, t:t + 1]).then_inc(f.v, 1)
                    else:
                        scaled(ckvT, bank, operand["kvnorm"][:, 0:1]).then_inc(f.v, 1)

            def latent():
                f = F["latent"]
                cos, sin = operand["cos"], operand["sin"]
                rope = slice(HD, MLA)
                for k, who in enumerate(LATENT):
                    if who != "v":
                        continue
                    dve.wait_ge(f.mm, k + 1)
                    bank = banks[k % 8]
                    if k == 0:
                        V.tensor_tensor(turned[rope, 0, :], bank[rope, :], sin[rope, :], ALU.mult).then_inc(f.v, 1)
                        step(V.tensor_tensor(krT[rope, :], krT[rope, :], cos[rope, :], ALU.mult))
                        step(V.tensor_tensor(krT[rope, :], krT[rope, :], turned[rope, 0, :], ALU.add))
                        V.tensor_copy(kD[rope, :, :], krT[rope, :].unsqueeze(1).to_broadcast([MLA - HD, 8, T]))
                    elif k < 17:
                        h = (k - 2) // 2
                        V.tensor_tensor(turned[0:MLA, h % 2, :], bank[0:MLA, :], sin[0:MLA, :], ALU.mult).then_inc(f.v, 1)
                        step(V.tensor_tensor(qD[0:MLA, h, :], raw[0:MLA, h % 2, :], cos[0:MLA, :], ALU.mult))
                        V.tensor_tensor(qD[0:MLA, h, :], qD[0:MLA, h, :], turned[0:MLA, h % 2, :], ALU.add).then_inc(f.s, 1)
                    else:
                        V.tensor_copy(vD[:, k - 25, :], bank[:, :]).then_inc(f.v, 1)

            def out_stage(name, loads):
                residual(name, ALPHA, loads)

            run = {
                "norm1": norm1, "project": project, "mixers": mixers, "hgrn": hgrn,
                "mix_out": lambda: residual("mix_out", 1.0), "up": up,
                "down": lambda: residual("down", 1.0), "gate": gate, "even_in": even_in,
                "even_a": lambda: attend("even_a"), "even_b": lambda: attend("even_b"),
                "even_out": lambda: out_stage("even_out", 3), "route0": lambda: route(0),
                "experts0": lambda: experts(0), "combine0": lambda: combine(0),
                "odd_in": odd_in, "odd_c": lambda: attend("odd_c"), "latent": latent,
                "odd_d": lambda: attend("odd_d"), "odd_out": lambda: out_stage("odd_out", 7),
                "overflow0": lambda: overflow(0),
                "overflow1": lambda: overflow(1), "route1": lambda: route(1), "experts1": lambda: experts(1), "combine1": lambda: combine(1),
            }
            for s in stages:
                if s in run:
                    run[s]()
                meet()

        @block.gpsimd
        def _(pool):
            meets = [0]
            G = nc.gpsimd
            steps = [2]

            def meet(i):
                meets[0] += 1
                pool.drain().then_inc(met, 1)
                pool.wait_ge(met, 4 * meets[0])
                pool.drain()
                if i >= 0:
                    f = turns[i % 2]
                    for s in (f.mm, f.a, f.v, f.s):
                        pool.sem_clear(s)

            def step(ins):
                ins.then_inc(pool_step, 1)
                steps[0] += 1
                pool.wait_ge(pool_step, steps[0])

            def load_rows(*names):
                for a, n in zip((rowsG, rowsB), names):
                    pool.dma_start(a, w[n]).then_inc(rows_loaded, 16)

            def project():
                G.memset(y_zero, 0.0).then_inc(pool_step, 1)
                pool.wait_ge(pool_step, 1)
                for j in range(OVER):
                    pool.dma_start(y_dram[(E + j) * P:(E + j + 1) * P, :], y_zero).then_inc(y_cleared, 16)
                G.memset(idx_zero[:, :], 0).then_inc(pool_step, 1)
                pool.dma_start(token_id[:, :], w["token_id"]).then_inc(ids_loaded, 16)
                pool.wait_ge(pool_step, 2)
                pool.dma_start(idx_dram.rearrange("(p c) o -> p (c o)", p=P), idx_zero[:, :]).then_inc(idx_cleared, 16)
                pool.wait_ge(y_cleared, 16 * OVER)

            def mixers():
                ws3 = operand["ws"].rearrange("p (h t) -> p h t", h=4)
                G.tensor_tensor(ws3, ws3, operand["wstril"].unsqueeze(1).to_broadcast([P, 4, P]), ALU.mult)\
                    .then_inc(M["ws_masked"], 1)

            def hgrn():
                of = operand["chunk_of"].unsqueeze(2).to_broadcast([P, P // HC, HD])
                for pr in range(2):
                    pool.wait_ge(M["hg_kT"], 2 * pr + 2)
                    if pr:
                        pool.wait_ge(M["hg_state"], 2 * pr)
                    for n in range(NT):
                        for hh in range(2):
                            if pr or n:
                                pool.wait_ge(M["hg_state_mm"], 2 * (NT * pr + n - 1) + hh + 1)
                            v_ = vT[:, n, hh * HD:(hh + 1) * HD].unsqueeze(1).to_broadcast([P, P // HC, HD])
                            G.tensor_tensor(v_spread[:, hh], v_, of, ALU.mult).then_inc(M["hg_v_spread"], 1)

            def down():
                pool.dma_start(pT.rearrange("p t q -> p (t q)"), w["pT"]).then_inc(pT_loaded, 16)

            def gate():
                pool.dma_start(rowsG, w["final_g"]).then_inc(rows_loaded, 16)
                pool.dma_start(pack_area["even"], w["pack_even"]).then_inc(pack_loaded["even"], 16)

            def clear_halves(tiles):
                step(G.memset(tiles[HD:P, 0::2, :], 0.0))
                step(G.memset(tiles[0:HD, 1::2, :], 0.0))

            def even_in():
                G.memset(negc, 0.0).then_inc(keys_cleared, 1)
                pool.wait_ge(keys_cleared, 1)
                clear_halves(kA)
                clear_halves(kB)

            def odd_in():
                clear_halves(kI)
                pool.sem_inc(keys_cleared, 1)
                clear_halves(kC)

            def out_stage(l, name):
                load_rows(f"ln_g_{l}_0", f"ln_b_{l}_0")
                for n in range(NT):
                    pool.wait_ge(tile_ready, norm_base[name] + n + 1)
                    pool.dma_start(x_dram[n * P:(n + 1) * P, :], x[:, n, :]).then_inc(x_stored, 16)

            def route(l):
                if l == 0:
                    pool.dma_start(pack_area["odd"], w["pack_odd"]).then_inc(pack_loaded["odd"], 16)
                f = F[f"route{l}"]
                pool.wait_ge(f.s, 1)
                pool.wait_ge(ids_loaded, 16)
                pool.wait_ge(idx_cleared, 16)
                for n in range(NT):
                    for j in range(2):
                        pool.indirect_dma_start(idx_dram[:, :], bass.IndirectOffsetOnAxis(ap=place[:, j, n:n + 1], axis=0),
                                                token_id[:, n:n + 1], None).then_inc(listed, 16)
                pool.wait_ge(listed, 128 * (l + 1))
                pool.dma_start(idx_sb[:, :], idx_dram.rearrange("(e q) o -> q (e o)", q=P),
                               allow_slow_non_contiguous=True).then_inc(idx_loaded, 16)
                pool.wait_ge(idx_loaded, 16 * (l + 1))

            def experts(l):
                pool.wait_ge(x_stored, 16 * NT * (l + 1))
                for e in range(E + 1):
                    if e >= 2:
                        pool.wait_ge(xgT_done, 34 * l + 2 * (e - 1))
                    pool.indirect_dma_start(xg[:, e % 2, :], None, x_dram[:, :],
                                            bass.IndirectOffsetOnAxis(ap=idx_sb[:, e:e + 1], axis=0))\
                        .then_inc(gathered[e % 2], 16)

            def overflow(l):
                if l == 0:
                    pool.sem_inc(over["stored"], 16)
                n, done = slots_of(pool, l)
                with pool.If(n > 0):
                    with pool.Fori(0, n) as slot:
                        j = slot + done
                        pool.wait_ge(over["stored"], j * 16 + 16)
                        G.tensor_copy(idx_one[:, :], idx_sb[:, bass.ds(slot + E, 1)]).then_inc(over["idx"], 1)
                        e = pool.value_load(over_list[0:1, bass.ds(slot, 1)], min_val=0, max_val=E - 1)
                        for i, name in enumerate(("moe_w_gate_2", "moe_w_up_2")):
                            src = w[name][l].rearrange("e (k p) n -> e p k n", p=P)[bass.ds(e, 1)]
                            pool.dma_start(over_w[:, i, :].rearrange("p (k n) -> p k n", k=KD), src[0]).then_inc(over["in"], 16)
                        pool.wait_ge(over["idx"], j + 1)
                        pool.sem_inc(over["passed"], 1)
                        pool.indirect_dma_start(xg[:, 0, :], None, x_dram[:, :],
                                                bass.IndirectOffsetOnAxis(ap=idx_one[:, 0:1], axis=0)).then_inc(over["in"], 16)
                        pool.wait_ge(over["gate_up_mm"], j * 2 + 2)
                        pool.sem_inc(over["passed"], 1)
                        src = w["moe_w_down_2"][l].rearrange("e (k p) n -> e p k n", p=P)[bass.ds(e, 1)]
                        pool.dma_start(over_w[:, 0, :].rearrange("p (k n) -> p k n", k=4), src[0]).then_inc(over["down_in"], 16)

            def combine(l):
                load_rows(f"ln_g_{l}_1", f"ln_b_{l}_1")
                for n in range(NT):
                    for j in range(2):
                        pool.indirect_dma_start(y_rows[:, j, n, :], None, y_dram[:, :],
                                                bass.IndirectOffsetOnAxis(ap=place[:, j, n:n + 1], axis=0))\
                            .then_inc(rows_gathered[n], 16)
                for n in range(NT):
                    pool.wait_ge(tile_gained, NT * l + n + 1)
                    if n == 0:
                        pool.wait_ge(rows_loaded, 16 * (3 + 4 * l + 2))
                    G.tensor_tensor(x[:, n, :], x[:, n, :], rowsB, ALU.add).then_inc(tile_ready, 1)

            run = {
                "project": project, "mixers": mixers, "hgrn": hgrn, "down": down, "gate": gate,
                "even_in": even_in, "odd_in": odd_in,
                "even_out": lambda: out_stage(0, "even_out"), "route0": lambda: route(0),
                "experts0": lambda: experts(0), "combine0": lambda: combine(0),
                "odd_out": lambda: out_stage(1, "odd_out"), "overflow0": lambda: overflow(0),
                "overflow1": lambda: overflow(1), "route1": lambda: route(1),
                "experts1": lambda: experts(1), "combine1": lambda: combine(1),
            }
            for i, s in enumerate(stages):
                if s in run:
                    run[s]()
                meet(i)

        @block.sync
        def _(sp):
            sp.dma_start(x[:, :, :], w["x"][0].rearrange("(n p) d -> p n d", p=P)).then_inc(x_loaded, 16)

            def source(c):
                name, k0, nk, c0, nc_ = c
                if name.startswith("w_o_"):
                    m = w["w_o_2"][0 if name.endswith("even") else 1]
                else:
                    m = w[name][0]
                return m[k0 * P:(k0 + nk) * P, c0:c0 + nc_].rearrange("(k p) n -> p k n", p=P)

            def load(at, src, k):
                if at >= RING:
                    sp.wait_ge(w_used, at - RING + 1)
                dst = ring[:, at % RING, 0:src.shape[1] * src.shape[2]].rearrange("p (k n) -> p k n", k=src.shape[1])
                sp.dma_start(dst, src).then_inc(w_loaded[at % RING], 16)

            user = {"w_in": "project", "w_out": "mix_out", "w_up": "up", "w_down": "down", "w_pe": "gate", "w_pg": "gate",
                    "even_w_in_2": "even_in", "w_o_even": "even_out", "odd_w_in_2": "odd_in", "odd_w_uq_2": "latent",
                    "odd_w_ukv_2": "latent", "w_o_odd": "odd_out"}
            static = [(at, c) for at, c in chunks if user[c[0]] in stages]

            def load_experts(l):
                c0 = first_expert_chunk[l]
                views = {n: w[n][l].rearrange("e (k p) n -> e p k n", p=P) for n in EXPERT_W}

                def load_expert(name, e, at, freed):
                    sp.wait_ge(w_used, freed + at - RING + 1)
                    k = 4 if name == "moe_w_down_2" else KD
                    sp.dma_start(ring[:, at % RING, :].rearrange("p (k n) -> p k n", k=k), views[name][bass.ds(e, 1)][0])\
                        .then_inc(w_loaded[at % RING], 16)

                g, u, d = EXPERT_W
                load_expert(g, 0, c0, 0)
                load_expert(u, 0, c0 + 1, 0)
                with sp.Fori(0, E // 2 - 1) as it:
                    for b in range(2):
                        for j, (name, e) in enumerate(((g, b + 1), (u, b + 1), (d, b))):
                            load_expert(name, it * 2 + e, c0 + 3 * b + 2 + j, it * 6)
                for j, (name, e) in enumerate(((g, E - 1), (u, E - 1), (d, E - 2), (d, E - 1))):
                    load_expert(name, e, c0 + 3 * E - 4 + j, 0)

            for at, c in static:
                if at < first_expert_chunk[0]:
                    load(at, source(c), c[2])
            if "experts0" in stages:
                load_experts(0)
                for at, c in static:
                    if at > first_expert_chunk[0]:
                        load(at, source(c), c[2])
            if "experts1" in stages:
                load_experts(1)
            for n in range(NT):
                if "combine1" in stages:
                    sp.wait_ge(tile_ready, norm_base["combine1"] + n + 1)
                else:
                    sp.wait_ge(met, 4 * len(stages))
                sp.dma_start(out[0, n * P:(n + 1) * P, :], x[:, n, :]).then_inc(stored, 16)
            sp.wait_ge(stored, 16 * NT)


EXPERT_W = ["moe_w_gate_2", "moe_w_up_2", "moe_w_down_2"]
BIG_INPUTS = ["x", "w_in", "w_out", "w_up", "w_down", "w_pe", "w_pg", "even_w_in_2", "odd_w_in_2", "odd_w_uq_2",
              "odd_w_ukv_2", "w_o_2", "moe_w_gate_2", "moe_w_up_2", "moe_w_down_2"]


def arrays_of(inputs):
    i = {k: np.asarray(v) for k, v in inputs.items()}
    pk = packs(i)
    arrays = {n: np.ascontiguousarray(i[n]) for n in BIG_INPUTS}
    for n, v in pk.items():
        arrays[f"pack_{n}"] = np.ascontiguousarray(np.concatenate([a for _, a in v], 1))
    arrays["pT"] = np.ascontiguousarray(i["p"][0, 0].reshape(T, 2, P).transpose(2, 1, 0)).reshape(P, -1)
    arrays["token_id"] = np.ascontiguousarray(np.arange(T, dtype=np.uint32).reshape(NT, P).T)
    arrays["final_g"] = np.ascontiguousarray(rows(i["final_g"]))
    for l in range(2):
        for j in range(2):
            arrays[f"ln_g_{l}_{j}"] = np.ascontiguousarray(rows(i["ln_g_2"][l, j]))
            arrays[f"ln_b_{l}_{j}"] = np.ascontiguousarray(rows(i["ln_b_2"][l, j]))
    return arrays, {n: [(m, a.shape[1]) for m, a in v] for n, v in pk.items()}


def program(nc, arrays, shapes, stop=None):
    w = {n: nc.dram_tensor(f"in_{n}", a.shape, mybir.dt.from_np(a.dtype), kind="ExternalInput").ap()
         for n, a in arrays.items()}
    out = nc.dram_tensor("out", (1, T, D), F32, kind="ExternalOutput").ap()
    build(nc, w, shapes, out, stop)
    return nc


def kernel(**inputs):
    from concourse import bacc
    from concourse.bass_utils import run_bass_kernel_spmd

    arrays, shapes = arrays_of(inputs)
    nc = program(bacc.Bacc("TRN2", target_bir_lowering=False, num_devices=1), arrays, shapes)
    r = run_bass_kernel_spmd(nc, [{f"in_{n}": a for n, a in arrays.items()}], core_ids=[0])
    return r.results[0]["out"]
```
